# Optimizing a Trainium2 kernel written in Bass

```python
import math
import jax
import jax.numpy as jnp
from jax import lax
import numpy as np

D_MODEL = 1024
BATCH = 1
SEQ = 256
DEPTH = 2

D_MIX = D_MODEL
FOX_HEADS = 8
FOX_HEAD_DIM = 64
FOX_WIDTH = FOX_HEADS * FOX_HEAD_DIM
Q_BLOCK = 128
S5_WIDTH = D_MIX - FOX_WIDTH
S5_GROUP = 16
S5_GROUPS = S5_WIDTH // S5_GROUP
S5_STATE = 64
EVEN_IN = 3 * FOX_WIDTH + FOX_HEADS + S5_WIDTH
MLSTM_HEADS = 8
MLSTM_HEAD_DIM = D_MIX // MLSTM_HEADS
MLSTM_CHUNK = 64
CONV_WIDTH = 4
ODD_IN = 4 * D_MIX + 2 * MLSTM_HEADS
N_GROUPS = 4
EXPERTS_PER_GROUP = 4
N_EXPERTS = N_GROUPS * EXPERTS_PER_GROUP
EXPERT_TOP_K = 2
D_EXPERT = 256
DN_ALPHA = (2 * DEPTH) ** 0.25
DN_BETA = (8 * DEPTH) ** -0.25
N_EVEN = (DEPTH + 1) // 2
N_ODD = DEPTH // 2
LN_EPS = 1e-5


def layer_norm(x, g, b):
    xf = x.astype(jnp.float32)
    mu = jnp.mean(xf, axis=-1, keepdims=True)
    var = jnp.mean(jnp.square(xf - mu), axis=-1, keepdims=True)
    y = (xf - mu) * lax.rsqrt(var + LN_EPS) * g.astype(jnp.float32) + b.astype(jnp.float32)
    return y.astype(x.dtype)

def forgetting_attention(q, k, v, f_logit):
    B, S, H, Dh = q.shape
    nb = S // Q_BLOCK
    c = jnp.cumsum(jax.nn.log_sigmoid(f_logit.astype(jnp.float32)), axis=1).transpose(0, 2, 1)
    qh = q.transpose(0, 2, 1, 3)
    kh = k.transpose(0, 2, 1, 3)
    vh = v.transpose(0, 2, 1, 3)
    q_blocks = qh.reshape(B, H, nb, Q_BLOCK, Dh).transpose(2, 0, 1, 3, 4)
    c_blocks = c.reshape(B, H, nb, Q_BLOCK).transpose(2, 0, 1, 3)
    pos_k = jnp.arange(S)
    scale = Dh ** -0.5

    def one_block(args):
        qb, cb, i = args
        s = jnp.einsum('bhqd,bhkd->bhqk', qb, kh).astype(jnp.float32) * scale
        s = s + cb[..., :, None] - c[..., None, :]
        pos_q = i * Q_BLOCK + jnp.arange(Q_BLOCK)
        mask = pos_k[None, :] <= pos_q[:, None]
        s = jnp.where(mask, s, -jnp.inf)
        p = jax.nn.softmax(s, axis=-1).astype(vh.dtype)
        return jnp.einsum('bhqk,bhkd->bhqd', p, vh)

    out = lax.map(one_block, (q_blocks, c_blocks, jnp.arange(nb)))
    return out.transpose(1, 0, 3, 2, 4).reshape(B, S, H, Dh)

def s5_scan(u, a_re, a_im, log_dt, b_re, b_im, c_re, c_im, d_skip):
    dt = jnp.exp(log_dt)[:, None]
    mag = jnp.exp(a_re * dt)
    lb_re = mag * jnp.cos(a_im * dt)
    lb_im = mag * jnp.sin(a_im * dt)
    num_re = lb_re - 1.0
    num_im = lb_im
    den = a_re * a_re + a_im * a_im
    z_re = (num_re * a_re + num_im * a_im) / den
    z_im = (num_im * a_re - num_re * a_im) / den
    bb_re = z_re[..., None] * b_re - z_im[..., None] * b_im
    bb_im = z_re[..., None] * b_im + z_im[..., None] * b_re
    bu_re = jnp.einsum('bsgc,gpc->bsgp', u, bb_re)
    bu_im = jnp.einsum('bsgc,gpc->bsgp', u, bb_im)
    a_re_t = jnp.broadcast_to(lb_re, bu_re.shape)
    a_im_t = jnp.broadcast_to(lb_im, bu_im.shape)

    def combine(e1, e2):
        a1r, a1i, b1r, b1i = e1
        a2r, a2i, b2r, b2i = e2
        return (a2r * a1r - a2i * a1i,
                a2r * a1i + a2i * a1r,
                a2r * b1r - a2i * b1i + b2r,
                a2r * b1i + a2i * b1r + b2i)

    _, _, h_re, h_im = lax.associative_scan(combine, (a_re_t, a_im_t, bu_re, bu_im), axis=1)
    y = jnp.einsum('bsgp,gcp->bsgc', h_re, c_re) - jnp.einsum('bsgp,gcp->bsgc', h_im, c_im)
    return y + d_skip * u

def causal_dwconv(x, w, b):
    C = x.shape[-1]
    y = lax.conv_general_dilated(x, w[:, None, :], window_strides=(1,), padding=[(CONV_WIDTH - 1, 0)],
                                 dimension_numbers=('NWC', 'WIO', 'NWC'), feature_group_count=C)
    return y + b

def mlstm_chunkwise(q, k, v, i_pre, f_pre):
    B, S, H, Dh = q.shape
    L = MLSTM_CHUNK
    NC = S // L
    f32 = jnp.float32

    def to_chunks(t):
        return t.reshape(B, NC, L, H, Dh).transpose(0, 3, 1, 2, 4)

    qc = to_chunks(q)
    kc = to_chunks(k * (Dh ** -0.5))
    vc = to_chunks(v)
    log_i = i_pre.astype(f32).reshape(B, NC, L, H).transpose(0, 3, 1, 2)
    log_f = jax.nn.log_sigmoid(f_pre.astype(f32)).reshape(B, NC, L, H).transpose(0, 3, 1, 2)
    bcum = jnp.cumsum(log_f, axis=-1)
    b_last = bcum[..., -1]
    g = b_last[..., None] - bcum + log_i
    m_loc = jnp.max(g, axis=-1)

    def step(carry, inp):
        Cm, nv, m = carry
        k_n, v_n, g_n, bl_n, ml_n = inp
        m_new = jnp.maximum(bl_n + m, ml_n)
        decay = jnp.exp(bl_n + m - m_new)
        w = jnp.exp(g_n - m_new[..., None])
        C_new = decay[..., None, None] * Cm + jnp.einsum('bhld,bhle->bhde', v_n * w[..., None], k_n)
        n_new = decay[..., None] * nv + jnp.einsum('bhl,bhle->bhe', w, k_n)
        return (C_new, n_new, m_new), (Cm, nv, m)

    init = (jnp.zeros((B, H, Dh, Dh), f32), jnp.zeros((B, H, Dh), f32), jnp.zeros((B, H), f32))
    xs = (kc.transpose(2, 0, 1, 3, 4), vc.transpose(2, 0, 1, 3, 4), g.transpose(2, 0, 1, 3),
          b_last.transpose(2, 0, 1), m_loc.transpose(2, 0, 1))
    _, (C_prev, n_prev, m_prev) = lax.scan(step, init, xs)
    C_prev = C_prev.transpose(1, 2, 0, 3, 4)
    n_prev = n_prev.transpose(1, 2, 0, 3)
    m_prev = m_prev.transpose(1, 2, 0)

    causal = jnp.tril(jnp.ones((L, L), dtype=bool))
    log_D = bcum[..., :, None] - bcum[..., None, :] + log_i[..., None, :]
    log_D = jnp.where(causal, log_D, -jnp.inf)
    m_inter = bcum + m_prev[..., None]
    m_t = jnp.maximum(m_inter, jnp.max(log_D, axis=-1))
    Dmat = jnp.exp(log_D - m_t[..., None])
    s = jnp.einsum('bhnld,bhnjd->bhnlj', qc, kc) * Dmat
    inter_scale = jnp.exp(m_inter - m_t)
    num = jnp.einsum('bhnlj,bhnjd->bhnld', s, vc) + inter_scale[..., None] * jnp.einsum('bhnvk,bhnlk->bhnlv', C_prev, qc)
    den = jnp.sum(s, axis=-1) + inter_scale * jnp.einsum('bhnk,bhnlk->bhnl', n_prev, qc)
    h = num / jnp.maximum(jnp.abs(den), jnp.exp(-m_t))[..., None]
    return h.transpose(0, 2, 3, 1, 4).reshape(B, S, H, Dh).astype(v.dtype)

def fox_s5_mixer(x, w_in, f_bias, a_re, a_im, log_dt, b_re, b_im, c_re, c_im, d_skip, w_glu, b_glu, w_out):
    B, S, _ = x.shape
    z = x @ w_in
    q, k, v, f_logit, u = jnp.split(z, [FOX_WIDTH, 2 * FOX_WIDTH, 3 * FOX_WIDTH, 3 * FOX_WIDTH + FOX_HEADS], axis=-1)
    shp = (B, S, FOX_HEADS, FOX_HEAD_DIM)
    att = forgetting_attention(q.reshape(shp), k.reshape(shp), v.reshape(shp), f_logit + f_bias)
    att = att.reshape(B, S, FOX_WIDTH)
    y = s5_scan(u.reshape(B, S, S5_GROUPS, S5_GROUP), a_re, a_im, log_dt, b_re, b_im, c_re, c_im, d_skip)
    y = jax.nn.gelu(y.reshape(B, S, S5_WIDTH))
    y = y * jax.nn.sigmoid(y @ w_glu + b_glu)
    return jnp.concatenate([att, y], axis=-1) @ w_out

def mlstm_mixer(x, w_in, conv_w, conv_b, i_bias, f_bias, w_out):
    B, S, _ = x.shape
    z = x @ w_in
    qk, v, o, i_pre, f_pre = jnp.split(z, [2 * D_MIX, 3 * D_MIX, 4 * D_MIX, 4 * D_MIX + MLSTM_HEADS], axis=-1)
    qk = jax.nn.silu(causal_dwconv(qk, conv_w, conv_b))
    q, k = jnp.split(qk, 2, axis=-1)
    shp = (B, S, MLSTM_HEADS, MLSTM_HEAD_DIM)
    h = mlstm_chunkwise(q.reshape(shp), k.reshape(shp), v.reshape(shp), i_pre + i_bias, f_pre + f_bias)
    h = h.reshape(B, S, D_MIX) * jax.nn.sigmoid(o)
    return h @ w_out

def hier_moe(x, w_group, b_group, w_expert, b_expert, w_gate, w_up, w_down):
    B, S, D = x.shape
    t = x.reshape(B * S, D)
    g_prob = jax.nn.softmax((t @ w_group + b_group).astype(jnp.float32), axis=-1)
    g_val, g_idx = lax.top_k(g_prob, 1)
    e_all = jnp.einsum('td,gde->tge', t, w_expert) + b_expert
    e_logits = jnp.take_along_axis(e_all, g_idx[:, :, None], axis=1)[:, 0]
    e_prob = jax.nn.softmax(e_logits.astype(jnp.float32), axis=-1)
    e_val, e_idx = lax.top_k(e_prob, EXPERT_TOP_K)
    e_val = e_val / jnp.sum(e_val, axis=-1, keepdims=True)
    weights = g_val * e_val
    expert_id = g_idx * EXPERTS_PER_GROUP + e_idx
    combine = jnp.einsum('tk,tke->te', weights, jax.nn.one_hot(expert_id, N_EXPERTS, dtype=jnp.float32))
    hid = jax.nn.silu(jnp.einsum('td,edf->tef', t, w_gate)) * jnp.einsum('td,edf->tef', t, w_up)
    hid = hid * combine.astype(hid.dtype)[:, :, None]
    out = jnp.einsum('tef,efd->td', hid, w_down)
    return out.reshape(B, S, D)

def first_inputs(seed: int = 0) -> dict:
    key = jax.random.key(seed)
    ks = iter(jax.random.split(key, 48))
    f32 = jnp.float32

    def nrm(shape, scale):
        return jax.random.normal(next(ks), shape, f32) * scale

    x = nrm((BATCH, SEQ, D_MODEL), 1.0)
    ln_g = 1.0 + nrm((DEPTH, 2, D_MODEL), 0.01)
    ln_b = nrm((DEPTH, 2, D_MODEL), 0.01)
    even_w_in = nrm((N_EVEN, D_MODEL, EVEN_IN), D_MODEL ** -0.5)
    fox_f_bias = jnp.linspace(2.0, 5.0, FOX_HEADS, dtype=f32)[None, :] + nrm((N_EVEN, FOX_HEADS), 0.1)
    s5_a_re = -0.5 + nrm((N_EVEN, S5_GROUPS, S5_STATE), 0.01)
    s5_a_im = jnp.pi * jnp.arange(S5_STATE, dtype=f32)[None, None, :] + nrm((N_EVEN, S5_GROUPS, S5_STATE), 0.01)
    s5_log_dt = jax.random.uniform(next(ks), (N_EVEN, S5_GROUPS), f32, minval=math.log(1e-3), maxval=math.log(1e-1))
    s5_b_re = nrm((N_EVEN, S5_GROUPS, S5_STATE, S5_GROUP), (2 * S5_GROUP) ** -0.5)
    s5_b_im = nrm((N_EVEN, S5_GROUPS, S5_STATE, S5_GROUP), (2 * S5_GROUP) ** -0.5)
    s5_c_re = nrm((N_EVEN, S5_GROUPS, S5_GROUP, S5_STATE), S5_STATE ** -0.5)
    s5_c_im = nrm((N_EVEN, S5_GROUPS, S5_GROUP, S5_STATE), S5_STATE ** -0.5)
    s5_d = nrm((N_EVEN, S5_GROUPS, S5_GROUP), 1.0)
    s5_w_glu = nrm((N_EVEN, S5_WIDTH, S5_WIDTH), S5_WIDTH ** -0.5)
    s5_b_glu = nrm((N_EVEN, S5_WIDTH), 0.01)
    even_w_out = nrm((N_EVEN, D_MIX, D_MODEL), D_MIX ** -0.5 * DN_BETA)
    odd_w_in = nrm((N_ODD, D_MODEL, ODD_IN), D_MODEL ** -0.5)
    mlstm_conv_w = nrm((N_ODD, CONV_WIDTH, 2 * D_MIX), CONV_WIDTH ** -0.5)
    mlstm_conv_b = nrm((N_ODD, 2 * D_MIX), 0.01)
    mlstm_i_bias = nrm((N_ODD, MLSTM_HEADS), 0.1)
    mlstm_f_bias = jnp.linspace(3.0, 6.0, MLSTM_HEADS, dtype=f32)[None, :] + nrm((N_ODD, MLSTM_HEADS), 0.01)
    odd_w_out = nrm((N_ODD, D_MIX, D_MODEL), D_MIX ** -0.5 * DN_BETA)
    moe_w_group = nrm((DEPTH, D_MODEL, N_GROUPS), D_MODEL ** -0.5)
    moe_b_group = nrm((DEPTH, N_GROUPS), 0.01)
    moe_w_expert = nrm((DEPTH, N_GROUPS, D_MODEL, EXPERTS_PER_GROUP), D_MODEL ** -0.5)
    moe_b_expert = nrm((DEPTH, N_GROUPS, EXPERTS_PER_GROUP), 0.01)
    moe_w_gate = nrm((DEPTH, N_EXPERTS, D_MODEL, D_EXPERT), D_MODEL ** -0.5)
    moe_w_up = nrm((DEPTH, N_EXPERTS, D_MODEL, D_EXPERT), D_MODEL ** -0.5)
    moe_w_down = nrm((DEPTH, N_EXPERTS, D_EXPERT, D_MODEL), D_EXPERT ** -0.5 * DN_BETA)
    return {'x': x, 'ln_g': ln_g, 'ln_b': ln_b,
            'even_w_in': even_w_in, 'fox_f_bias': fox_f_bias,
            's5_a_re': s5_a_re, 's5_a_im': s5_a_im, 's5_log_dt': s5_log_dt,
            's5_b_re': s5_b_re, 's5_b_im': s5_b_im, 's5_c_re': s5_c_re, 's5_c_im': s5_c_im,
            's5_d': s5_d, 's5_w_glu': s5_w_glu, 's5_b_glu': s5_b_glu, 'even_w_out': even_w_out,
            'odd_w_in': odd_w_in, 'mlstm_conv_w': mlstm_conv_w, 'mlstm_conv_b': mlstm_conv_b,
            'mlstm_i_bias': mlstm_i_bias, 'mlstm_f_bias': mlstm_f_bias, 'odd_w_out': odd_w_out,
            'moe_w_group': moe_w_group, 'moe_b_group': moe_b_group,
            'moe_w_expert': moe_w_expert, 'moe_b_expert': moe_b_expert,
            'moe_w_gate': moe_w_gate, 'moe_w_up': moe_w_up, 'moe_w_down': moe_w_down}

def first_block(x, ln_g, ln_b, even_w_in, fox_f_bias, s5_a_re, s5_a_im, s5_log_dt, s5_b_re, s5_b_im,
              s5_c_re, s5_c_im, s5_d, s5_w_glu, s5_b_glu, even_w_out, odd_w_in, mlstm_conv_w,
              mlstm_conv_b, mlstm_i_bias, mlstm_f_bias, odd_w_out, moe_w_group, moe_b_group,
              moe_w_expert, moe_b_expert, moe_w_gate, moe_w_up, moe_w_down):
    h = x
    for layer in range(DEPTH):
        j = layer // 2
        if layer % 2 == 0:
            mix = fox_s5_mixer(h, even_w_in[j], fox_f_bias[j], s5_a_re[j], s5_a_im[j], s5_log_dt[j],
                               s5_b_re[j], s5_b_im[j], s5_c_re[j], s5_c_im[j], s5_d[j],
                               s5_w_glu[j], s5_b_glu[j], even_w_out[j])
        else:
            mix = mlstm_mixer(h, odd_w_in[j], mlstm_conv_w[j], mlstm_conv_b[j], mlstm_i_bias[j],
                              mlstm_f_bias[j], odd_w_out[j])
        h = layer_norm(DN_ALPHA * h + mix, ln_g[layer, 0], ln_b[layer, 0])
        ffn = hier_moe(h, moe_w_group[layer], moe_b_group[layer], moe_w_expert[layer], moe_b_expert[layer],
                       moe_w_gate[layer], moe_w_up[layer], moe_w_down[layer])
        h = layer_norm(DN_ALPHA * h + ffn, ln_g[layer, 1], ln_b[layer, 1])
    return h


DEPTH_2 = 1

A_HEADS = 8
A_HEAD_DIM = 128
IDX_HEADS = 8
IDX_DIM = 64
TOPK_MAX = 256
REL_BUCKETS = 32
REL_MAX_DIST = 128
B_HEADS = 8
B_HEAD_DIM = D_MODEL // B_HEADS
B_CHUNK = 64
C_HEADS = 4
C_QK_DIM = 256
C_V_DIM = 512
C_CHUNK = 128
EXPERTS_PER_GROUP_2 = 8
N_EXPERTS_2 = N_GROUPS * EXPERTS_PER_GROUP_2
EXPERT_TOPK = 2
D_EXPERT_2 = 512
EPS = 1e-6

A_WIDTH = A_HEADS * A_HEAD_DIM
B_WIDTH = B_HEADS * B_HEAD_DIM
C_QK_WIDTH = C_HEADS * C_QK_DIM
C_V_WIDTH = C_HEADS * C_V_DIM
IN_SPLITS = (A_WIDTH, A_WIDTH, A_WIDTH, IDX_HEADS * IDX_DIM, IDX_DIM, IDX_HEADS,
             B_WIDTH, B_WIDTH, B_WIDTH, B_WIDTH,
             C_QK_WIDTH, C_QK_WIDTH, C_V_WIDTH, C_V_WIDTH,
             D_MODEL, D_MODEL, D_MODEL)
N_IN = sum(IN_SPLITS)


def rmsnorm(x, g=None):
    xf = x.astype(jnp.float32)
    y = xf * lax.rsqrt(jnp.mean(xf * xf, axis=-1, keepdims=True) + EPS)
    if g is not None:
        y = y * g.astype(jnp.float32)
    return y.astype(x.dtype)

def t5_bucket(rel):
    max_exact = REL_BUCKETS // 2
    relf = jnp.maximum(rel, 1).astype(jnp.float32)
    large = max_exact + (jnp.log(relf / max_exact) / math.log(REL_MAX_DIST / max_exact)
                         * (REL_BUCKETS - max_exact)).astype(jnp.int32)
    large = jnp.minimum(large, REL_BUCKETS - 1)
    return jnp.where(rel < max_exact, rel, large)

def split_cols(proj):
    offs = np.cumsum(np.array(IN_SPLITS))[:-1].tolist()
    return jnp.split(proj, offs, axis=-1)

def dsa_attention(q, k, v, q_idx, k_idx, w_idx, rel_bias):
    bsz, seq = q.shape[0], q.shape[1]
    top_k = min(TOPK_MAX, seq // 4)
    n_blk = seq // Q_BLOCK
    s_pos = jnp.arange(seq, dtype=jnp.int32)
    k_idx32 = k_idx.astype(jnp.float32)
    idx_scale = (IDX_HEADS * IDX_DIM) ** -0.5

    def to_blocks(a):
        return jnp.moveaxis(a.reshape((bsz, n_blk, Q_BLOCK) + a.shape[2:]), 1, 0)

    def one_block(args):
        qb, qib, wb, t0 = args
        t_pos = t0 + jnp.arange(Q_BLOCK, dtype=jnp.int32)
        rel = jax.nn.relu(jnp.einsum('bqhd,bsd->bqhs', qib.astype(jnp.float32), k_idx32))
        score = jnp.einsum('bqhs,bqh->bqs', rel, wb.astype(jnp.float32) * idx_scale)
        causal = s_pos[None, :] <= t_pos[:, None]
        score = jnp.where(causal[None], score, -jnp.inf)
        _, sel = lax.top_k(score, top_k)
        valid = sel <= t_pos[None, :, None]
        k_sel = jax.vmap(lambda kb, ib: kb[ib])(k, sel)
        v_sel = jax.vmap(lambda vb, ib: vb[ib])(v, sel)
        logits = jnp.einsum('bqhd,bqkhd->bqhk', qb, k_sel).astype(jnp.float32) * (A_HEAD_DIM ** -0.5)
        bucket = t5_bucket(jnp.maximum(t_pos[None, :, None] - sel, 0))
        logits = logits + jnp.transpose(rel_bias[bucket], (0, 1, 3, 2)).astype(jnp.float32)
        logits = jnp.where(valid[:, :, None, :], logits, -jnp.inf)
        p = jax.nn.softmax(logits, axis=-1).astype(v.dtype)
        return jnp.einsum('bqhk,bqkhd->bqhd', p, v_sel)

    t0s = jnp.arange(n_blk, dtype=jnp.int32) * Q_BLOCK
    out = lax.map(one_block, (to_blocks(q), to_blocks(q_idx), to_blocks(w_idx), t0s))
    return jnp.moveaxis(out, 0, 1).reshape(bsz, seq, A_WIDTH)

def hgrn2(q, f_pre, i, g_out, lb, norm_g):
    bsz, seq = q.shape[0], q.shape[1]
    nc = seq // B_CHUNK
    lb = lb.reshape(B_HEADS, B_HEAD_DIM).astype(jnp.float32)
    f = lb + (1.0 - lb) * jax.nn.sigmoid(f_pre.astype(jnp.float32))
    log_f = jnp.log(f)
    kk = 1.0 - f

    def chunks(a):
        return jnp.transpose(a.reshape(bsz, nc, B_CHUNK, B_HEADS, -1), (1, 0, 3, 2, 4))

    causal = jnp.tril(jnp.ones((B_CHUNK, B_CHUNK), dtype=bool))

    def step(state, inp):
        qt, kt, vt, gt = inp
        b = jnp.cumsum(gt, axis=2)
        diff = b[:, :, :, None, :] - b[:, :, None, :, :]
        decay = jnp.exp(jnp.where(causal[None, None, :, :, None], diff, -jnp.inf))
        attn = jnp.einsum('bhtd,bhsd,bhtsd->bhts', qt, kt, decay)
        o = (jnp.einsum('bhts,bhsv->bhtv', attn, vt)
             + jnp.einsum('bhtd,bhdv->bhtv', qt * jnp.exp(b), state))
        b_last = b[:, :, -1:, :]
        state = (jnp.exp(b_last[:, :, 0, :, None]) * state
                 + jnp.einsum('bhsd,bhsv->bhdv', kt * jnp.exp(b_last - b), vt))
        return state, o

    s0 = jnp.zeros((bsz, B_HEADS, B_HEAD_DIM, B_HEAD_DIM), jnp.float32)
    _, o = lax.scan(step, s0, (chunks(q.astype(jnp.float32)), chunks(kk),
                               chunks(i.astype(jnp.float32)), chunks(log_f)))
    o = jnp.transpose(o, (1, 0, 3, 2, 4)).reshape(bsz, seq, B_HEADS, B_HEAD_DIM)
    o = rmsnorm(o, norm_g) * jax.nn.silu(g_out.astype(jnp.float32))
    return o.reshape(bsz, seq, B_WIDTH).astype(q.dtype)

def retention(q, k, v, g):
    bsz, seq = q.shape[0], q.shape[1]
    nc = seq // C_CHUNK
    pos = jnp.arange(seq, dtype=jnp.float32)
    theta = jnp.repeat(1.0 / (10000.0 ** jnp.linspace(0.0, 1.0, C_QK_DIM // 2)), 2)
    ang = pos[:, None] * theta[None, :]
    sin = jnp.sin(ang)[None, :, None, :]
    cos = jnp.cos(ang)[None, :, None, :]

    def rot(a):
        a2 = jnp.stack([-a[..., 1::2], a[..., 0::2]], axis=-1).reshape(a.shape)
        return a * cos + a2 * sin

    qr = rot(q.astype(jnp.float32))
    kr = rot(k.astype(jnp.float32)) * (C_QK_DIM ** -0.5)
    log_gamma = jnp.log(1.0 - 2.0 ** (-5.0 - jnp.arange(C_HEADS, dtype=jnp.float32)))
    idx = jnp.arange(C_CHUNK, dtype=jnp.float32)
    causal = idx[:, None] >= idx[None, :]
    intra_decay = jnp.exp(jnp.where(causal[None], (idx[:, None] - idx[None, :])[None] * log_gamma[:, None, None], -jnp.inf))
    q_decay = jnp.exp((idx + 1.0)[None, :] * log_gamma[:, None])[..., None]
    k_decay = jnp.exp((C_CHUNK - 1.0 - idx)[None, :] * log_gamma[:, None])[..., None]
    chunk_decay = jnp.exp(C_CHUNK * log_gamma)[:, None, None]

    def chunks(a):
        return jnp.transpose(a.reshape(bsz, nc, C_CHUNK, C_HEADS, -1), (1, 0, 3, 2, 4))

    def step(state, inp):
        qt, kt, vt = inp
        attn = jnp.einsum('bhtd,bhsd->bhts', qt, kt) * intra_decay
        o = (jnp.einsum('bhts,bhsv->bhtv', attn, vt)
             + jnp.einsum('bhtd,bhdv->bhtv', qt * q_decay, state))
        state = chunk_decay * state + jnp.einsum('bhsd,bhsv->bhdv', kt * k_decay, vt)
        return state, o

    s0 = jnp.zeros((bsz, C_HEADS, C_QK_DIM, C_V_DIM), jnp.float32)
    _, o = lax.scan(step, s0, (chunks(qr), chunks(kr), chunks(v.astype(jnp.float32))))
    o = jnp.transpose(o, (1, 0, 3, 2, 4)).reshape(bsz, seq, C_HEADS, C_V_DIM)
    o = rmsnorm(o).reshape(bsz, seq, C_V_WIDTH)
    return (jax.nn.silu(g.astype(jnp.float32)) * o).astype(q.dtype)

def hier_moe_2(h, rg_w, rg_b, re_w, re_b, w_gate, w_up, w_down):
    bsz, seq, dm = h.shape
    x = h.reshape(-1, dm)
    group_logits = (x @ rg_w + rg_b).astype(jnp.float32)
    group_p = jax.nn.softmax(group_logits, axis=-1)
    g_sel = jnp.argmax(group_logits, axis=-1)
    g_prob = jnp.take_along_axis(group_p, g_sel[:, None], axis=-1)
    exp_logits = (x @ re_w + re_b).astype(jnp.float32).reshape(-1, N_GROUPS, EXPERTS_PER_GROUP_2)
    in_group = jnp.take_along_axis(exp_logits, g_sel[:, None, None], axis=1)[:, 0]
    top_v, top_i = lax.top_k(in_group, EXPERT_TOPK)
    top_w = jax.nn.softmax(top_v, axis=-1) * g_prob
    w_group = jnp.sum(jax.nn.one_hot(top_i, EXPERTS_PER_GROUP_2, dtype=jnp.float32) * top_w[..., None], axis=1)
    gates = (jax.nn.one_hot(g_sel, N_GROUPS, dtype=jnp.float32)[:, :, None] * w_group[:, None, :]).astype(x.dtype)
    wg = w_gate.reshape(N_GROUPS, EXPERTS_PER_GROUP_2, dm, D_EXPERT_2)
    wu = w_up.reshape(N_GROUPS, EXPERTS_PER_GROUP_2, dm, D_EXPERT_2)
    wd = w_down.reshape(N_GROUPS, EXPERTS_PER_GROUP_2, D_EXPERT_2, dm)
    y = jnp.zeros_like(x)
    for gi in range(N_GROUPS):
        hg = jax.nn.silu(jnp.einsum('nd,edf->nef', x, wg[gi])) * jnp.einsum('nd,edf->nef', x, wu[gi])
        y = y + jnp.einsum('nef,efd->nd', hg * gates[:, gi, :, None], wd[gi])
    return y.reshape(bsz, seq, dm)

def hybrid_layer(x, c, lb, rel_bias, norm1_g, norm2_g, ada_w, ada_b, w_in, hgrn_norm_g,
                 w_branch_a, w_branch_b, w_branch_c, w_out, rg_w, rg_b, re_w, re_b,
                 e_gate, e_up, e_down):
    bsz, seq, _ = x.shape
    mod = (jax.nn.silu(c) @ ada_w + ada_b)[:, None, :]
    sh1, sc1, gt1, sh2, sc2, gt2 = jnp.split(mod, 6, axis=-1)
    h = rmsnorm(x, norm1_g) * (1.0 + sc1) + sh1
    (aq, ak, av, iq, ik, iw, bq, bf, bi, bg, cq, ck, cv, cg, ga, gb, gc) = split_cols(h @ w_in)
    o_a = dsa_attention(aq.reshape(bsz, seq, A_HEADS, A_HEAD_DIM),
                        ak.reshape(bsz, seq, A_HEADS, A_HEAD_DIM),
                        av.reshape(bsz, seq, A_HEADS, A_HEAD_DIM),
                        iq.reshape(bsz, seq, IDX_HEADS, IDX_DIM), ik, iw, rel_bias)
    hs = (bsz, seq, B_HEADS, B_HEAD_DIM)
    o_b = hgrn2(bq.reshape(hs), bf.reshape(hs), bi.reshape(hs), bg.reshape(hs), lb, hgrn_norm_g)
    o_c = retention(cq.reshape(bsz, seq, C_HEADS, C_QK_DIM), ck.reshape(bsz, seq, C_HEADS, C_QK_DIM),
                    cv.reshape(bsz, seq, C_HEADS, C_V_DIM), cg)
    merged = (jax.nn.sigmoid(ga) * (o_a @ w_branch_a)
              + jax.nn.sigmoid(gb) * (o_b @ w_branch_b)
              + jax.nn.sigmoid(gc) * (o_c @ w_branch_c))
    x = x + gt1 * (merged @ w_out)
    h2 = rmsnorm(x, norm2_g) * (1.0 + sc2) + sh2
    x = x + gt2 * hier_moe_2(h2, rg_w, rg_b, re_w, re_b, e_gate, e_up, e_down)
    return x

def second_inputs(seed: int = 0) -> dict:
    key = jax.random.key(seed)
    ks = jax.random.split(key, 22)
    D = D_MODEL

    def nrm(k, shape, scale):
        return jax.random.normal(k, shape, jnp.float32) * scale

    return {
        'x': nrm(ks[0], (BATCH, SEQ, D), 1.0),
        'c': nrm(ks[1], (BATCH, D), 1.0),
        'rel_bias': nrm(ks[2], (REL_BUCKETS, A_HEADS), 0.5),
        'hgrn_lb_raw': nrm(ks[3], (DEPTH_2, B_WIDTH), 0.5),
        'norm1_g': 1.0 + nrm(ks[4], (DEPTH_2, D), 0.05),
        'norm2_g': 1.0 + nrm(ks[5], (DEPTH_2, D), 0.05),
        'ada_w': nrm(ks[6], (DEPTH_2, D, 6 * D), 0.5 * D ** -0.5),
        'ada_b': nrm(ks[7], (DEPTH_2, 6 * D), 0.02),
        'w_in': nrm(ks[8], (DEPTH_2, D, N_IN), D ** -0.5),
        'hgrn_norm_g': 1.0 + nrm(ks[9], (DEPTH_2, B_HEAD_DIM), 0.05),
        'w_branch_a': nrm(ks[10], (DEPTH_2, A_WIDTH, D), A_WIDTH ** -0.5),
        'w_branch_b': nrm(ks[11], (DEPTH_2, B_WIDTH, D), B_WIDTH ** -0.5),
        'w_branch_c': nrm(ks[12], (DEPTH_2, C_V_WIDTH, D), C_V_WIDTH ** -0.5),
        'w_out': nrm(ks[13], (DEPTH_2, D, D), D ** -0.5),
        'router_group_w': nrm(ks[14], (DEPTH_2, D, N_GROUPS), D ** -0.5),
        'router_group_b': nrm(ks[15], (DEPTH_2, N_GROUPS), 0.01),
        'router_expert_w': nrm(ks[16], (DEPTH_2, D, N_EXPERTS_2), D ** -0.5),
        'router_expert_b': nrm(ks[17], (DEPTH_2, N_EXPERTS_2), 0.01),
        'expert_w_gate': nrm(ks[18], (DEPTH_2, N_EXPERTS_2, D, D_EXPERT_2), D ** -0.5),
        'expert_w_up': nrm(ks[19], (DEPTH_2, N_EXPERTS_2, D, D_EXPERT_2), D ** -0.5),
        'expert_w_down': nrm(ks[20], (DEPTH_2, N_EXPERTS_2, D_EXPERT_2, D), D_EXPERT_2 ** -0.5),
        'final_norm_g': 1.0 + nrm(ks[21], (D,), 0.05),
    }

def second_block(x, c, rel_bias, hgrn_lb_raw, norm1_g, norm2_g, ada_w, ada_b, w_in, hgrn_norm_g,
              w_branch_a, w_branch_b, w_branch_c, w_out, router_group_w, router_group_b,
              router_expert_w, router_expert_b, expert_w_gate, expert_w_up, expert_w_down,
              final_norm_g):
    lb_soft = jax.nn.softmax(hgrn_lb_raw.astype(jnp.float32), axis=0)
    lb_all = jnp.cumsum(lb_soft, axis=0) - lb_soft[0:1]
    for l in range(DEPTH_2):
        x = hybrid_layer(x, c, lb_all[l], rel_bias, norm1_g[l], norm2_g[l], ada_w[l], ada_b[l],
                         w_in[l], hgrn_norm_g[l], w_branch_a[l], w_branch_b[l], w_branch_c[l],
                         w_out[l], router_group_w[l], router_group_b[l], router_expert_w[l],
                         router_expert_b[l], expert_w_gate[l], expert_w_up[l], expert_w_down[l])
    return rmsnorm(x, final_norm_g)


def setup_inputs(seed=0):
    out = dict(first_inputs(seed))
    for name, value in second_inputs(seed + 1).items():
        if name != "x":
            out[name + "_2"] = value
    return out


def reference(
    x, ln_g, ln_b, even_w_in, fox_f_bias, s5_a_re, s5_a_im, s5_log_dt, s5_b_re, s5_b_im,
    s5_c_re, s5_c_im, s5_d, s5_w_glu, s5_b_glu, even_w_out, odd_w_in, mlstm_conv_w,
    mlstm_conv_b, mlstm_i_bias, mlstm_f_bias, odd_w_out, moe_w_group, moe_b_group, moe_w_expert,
    moe_b_expert, moe_w_gate, moe_w_up, moe_w_down, c_2, rel_bias_2, hgrn_lb_raw_2, norm1_g_2,
    norm2_g_2, ada_w_2, ada_b_2, w_in_2, hgrn_norm_g_2, w_branch_a_2, w_branch_b_2,
    w_branch_c_2, w_out_2, router_group_w_2, router_group_b_2, router_expert_w_2,
    router_expert_b_2, expert_w_gate_2, expert_w_up_2, expert_w_down_2, final_norm_g_2,
):
    x = first_block(
        x, ln_g, ln_b, even_w_in, fox_f_bias, s5_a_re, s5_a_im, s5_log_dt, s5_b_re, s5_b_im,
        s5_c_re, s5_c_im, s5_d, s5_w_glu, s5_b_glu, even_w_out, odd_w_in, mlstm_conv_w,
        mlstm_conv_b, mlstm_i_bias, mlstm_f_bias, odd_w_out, moe_w_group, moe_b_group,
        moe_w_expert, moe_b_expert, moe_w_gate, moe_w_up, moe_w_down,
    )
    return second_block(
        x, c_2, rel_bias_2, hgrn_lb_raw_2, norm1_g_2, norm2_g_2, ada_w_2, ada_b_2, w_in_2,
        hgrn_norm_g_2, w_branch_a_2, w_branch_b_2, w_branch_c_2, w_out_2, router_group_w_2,
        router_group_b_2, router_expert_w_2, router_expert_b_2, expert_w_gate_2, expert_w_up_2,
        expert_w_down_2, final_norm_g_2,
    )


_drawn_inputs = setup_inputs


def setup_inputs(seed=0):
    import zlib

    import numpy as np

    out = dict(_drawn_inputs(seed))
    spreads = {}
    factors = {'s5_a_re': 64.0,
     's5_a_im': 42.584,
     's5_log_dt': 39.256,
     's5_b_re': 37.808,
     's5_b_im': 46.528,
     's5_c_re': 48.616,
     's5_c_im': 36.528,
     's5_b_glu': 8.0,
     'mlstm_conv_b': 8.0,
     'mlstm_i_bias': 8.0,
     'moe_b_group': 5.889,
     'moe_b_expert': 7.767,
     'rel_bias_2': 2.746,
     'norm2_g_2': 3.362,
     'hgrn_norm_g_2': 8.0,
     'router_group_b_2': 8.0,
     'router_expert_b_2': 8.0}
    for name, (base, spread) in spreads.items():
        noise = np.random.default_rng([zlib.crc32(name.encode()), seed]).standard_normal(out[name].shape)
        drawn = base * np.exp(spread * noise) if base else spread * noise
        out[name] = jnp.asarray(drawn.astype(out[name].dtype))
    for name, factor in factors.items():
        out[name] = (out[name] * factor).astype(out[name].dtype)
    return out
```

```python
import math
from contextlib import ExitStack

import numpy as np

import concourse.bass as bass
from concourse import mybir
from concourse.alu_op_type import AluOpType as ALU

ACT = mybir.ActivationFunctionType
F32 = mybir.dt.float32
I32 = mybir.dt.int32
AX = mybir.AxisListType.X

P = 128
SEQ = 256
D = 1024
KT = D // P
NT = SEQ // P
HEADS = 8
UNIT = 2048
SLOTS = 12
BANKS = 8
SCRATCH = 19900
ALPHA = 4 ** 0.25
LN_EPS = 1e-5
RMS_EPS = 1e-6
MASKED = -1e30
TAKEN = -3e38
ROUND = 12582912.0
TWO_PI_HI, TWO_PI_MID, TWO_PI_LO = 6.28125, 0.0019350051879882812, 3.0198e-07
MOE1_E, MOE1_F = 16, 256
MOE2_E, MOE2_F = 32, 512
TOPK = 64
TRI = 3 * P
LEVELS = (64, 32, 16, 8, 4, 2, 1)

SMALL = {}
for _name, _n in (("fox_f", 8), ("route0", 20), ("mlstm_i", 8), ("mlstm_f", 8), ("route1", 20), ("idx_w", 8), ("route2", 36)):
    SMALL[_name] = (sum(n for _, n in SMALL.values()), _n)
N_SMALL = sum(n for _, n in SMALL.values())
COLS = {}
for _name, _n in (("b_glu", 4), ("s5_d", 4), ("a_re", 16), ("a_im", 16), ("log_dt", 16), ("fox_f_bias", 1),
                  ("mlstm_i_bias", 1), ("mlstm_f_bias", 1), ("conv_b", 16), ("conv_w", 64), ("ada_b", 32),
                  ("norm1_g", 8), ("norm2_g", 8), ("c", 8), ("lb_raw", 8)):
    COLS[_name] = (sum(n for _, n in COLS.values()), _n)
N_COLS = sum(n for _, n in COLS.values())
ROUTES = ((4, 4), (4, 4), (4, 8))
ROUTE_BIAS = (0, 20, 40)
ROWS = ("ln_g0", "ln_b0", "ln_g1", "ln_b1", "ln_g2", "ln_b2", "ln_g3", "ln_b3", "final_g", "ada_gt1", "ada_gt2", "hgrn_g")


class Steps:

    def __init__(self, eng, sem):
        self.eng, self.sem, self.n = eng, sem, 0

    def __call__(self, ins):
        ins.then_inc(self.sem, 1)
        self.n += 1
        self.eng.wait_ge(self.sem, self.n)


class PsumTiles:

    def __init__(self, ctx, nc):
        self.bank = [ctx.enter_context(nc.psum_tensor(f"bank{b}", [P, 512], F32)) for b in range(BANKS)]
        self.ready = [ctx.enter_context(nc.semaphore(f"bank{b}_ready")) for b in range(BANKS)]
        self.freed = [ctx.enter_context(nc.semaphore(f"bank{b}_freed")) for b in range(BANKS)]
        self.uses = [0] * BANKS
        self.jobs = {}
        self.turn = 0

    def open(self, pe, key, banks=range(BANKS)):
        b = banks[self.turn % len(banks)]
        self.turn += 1
        if self.uses[b]:
            pe.wait_ge(self.freed[b], self.uses[b])
        self.jobs[key] = (b, self.uses[b])
        self.uses[b] += 1
        return self.bank[b]

    def close(self, key, ins):
        ins.then_inc(self.ready[self.jobs[key][0]], 1)

    def take(self, eng, key):
        b, k = self.jobs[key]
        eng.wait_ge(self.ready[b], k + 1)
        return self.bank[b]

    def free(self, eng, key):
        eng.sem_inc(self.freed[self.jobs[key][0]], 1)


class Arena:

    def __init__(self, mem, at=0):
        self.mem, self.at = mem, at

    def take(self, n, *shape, rows=P):
        v = self.mem[0:rows, self.at:self.at + n]
        self.at += n
        assert self.at <= self.mem.shape[1], self.at
        if len(shape) == 2:
            v = v.rearrange("p (a b) -> p a b", a=shape[0], b=shape[1])
        elif len(shape) == 3:
            v = v.rearrange("p (a b c) -> p a b c", a=shape[0], b=shape[1], c=shape[2])
        return v


class Net:
    def __init__(self, nc, ctx, io, phases):
        self.nc, self.io, self.phases = nc, io, phases
        self.ctx = ctx
        self.sems = {}
        self.T = PsumTiles(ctx, nc)
        sb = lambda name, n, rows=P, dt=F32: ctx.enter_context(nc.sbuf_tensor(name + "_sb", [rows, n], dt))
        self.ring = sb("ring", SLOTS * UNIT)
        self.x = sb("x", NT * D)[:, :].rearrange("p (i d) -> p i d", i=NT)
        self.xT = sb("xT", KT * SEQ)[:, :].rearrange("p (k t) -> p k t", k=KT)
        self.small = sb("small", KT * N_SMALL)[:, :].rearrange("p (k n) -> p k n", k=KT)
        self.cols = sb("cols", N_COLS)
        self.ident = sb("ident", P)
        self.causal = sb("causal", TRI)
        self.bias_row = sb("bias_row", 84)
        self.rows = sb("rows", 2 * D)[:, :].rearrange("p (r d) -> p r d", r=2)
        self.stat = sb("stat", 64)
        self.ones = sb("ones", 256)
        self.mod = sb("mod", 40)
        self.zeros = sb("zeros", 512)
        self.scratch = sb("scratch", SCRATCH)
        self.unit = 0
        self.released = {}
        self.loops = []
        self.n_ended = {}
        self.n_rows = 0

    def sem(self, name):
        if name not in self.sems:
            self.sems[name] = self.ctx.enter_context(self.nc.semaphore(name))
        return self.sems[name]

    def col(self, name, j=0, n=1, rows=P):
        at, width = COLS[name]
        return self.cols[0:rows, at + j:at + j + n]

    def join(self, eng, name):
        sems = [self.sem(f"{e}_ended") for e in ("tensor", "vector", "scalar", "gpsimd")]
        self.n_ended[name] = self.n_ended.get(name, 0) + 1
        eng.drain().then_inc(self.sem(f"{name}_ended"), 1)
        for s in sems:
            eng.wait_ge(s, self.n_ended[name])

    def slot(self, u):
        s = u % SLOTS
        return self.ring[:, s * UNIT:(s + 1) * UNIT]

    def use_unit(self, pe):
        u = self.unit
        self.unit += 1
        pe.wait_ge(self.sem(f"slot{u % SLOTS}_loaded"), 16 * (u // SLOTS + 1))
        return u, self.slot(u)

    def release(self, units, key):
        b, k = self.T.jobs[key]
        for u in units:
            self.released[u] = (self.T.ready[b], k + 1)

    def product(self, pe, key, actT, kt=KT, banks=range(BANKS)):
        us = [self.use_unit(pe) for _ in range(kt // 4)]
        for i in range(NT):
            t = self.T.open(pe, (key, i), banks)
            for k in range(kt):
                w = us[k // 4][1].rearrange("p (k n) -> p k n", k=4)
                mm = pe.matmul(t[:, :], actT[:, k, i * P:(i + 1) * P], w[:, k % 4, :], start=k == 0, stop=k == kt - 1)
            self.T.close((key, i), mm)
        self.release([u for u, _ in us], (key, NT - 1))

    def product_T(self, pe, key, actT, kt=KT, banks=range(BANKS)):
        us = [self.use_unit(pe) for _ in range(kt // 4)]
        for c in range(2):
            t = self.T.open(pe, (key, c), banks)
            for m in range(2):
                for k in range(kt):
                    w = us[k // 4][1].rearrange("p (k n) -> p k n", k=4)
                    n0 = (2 * c + m) * P
                    mm = pe.matmul(t[:, m * SEQ:(m + 1) * SEQ], w[:, k % 4, n0:n0 + P], actT[:, k, :],
                                   start=k == 0, stop=k == kt - 1)
            self.T.close((key, c), mm)
        self.release([u for u, _ in us], (key, 1))

    def small_T(self, pe, key, name, actT, banks=range(BANKS)):
        at, n = SMALL[name]
        t = self.T.open(pe, key, banks)
        for k in range(KT):
            mm = pe.matmul(t[0:n, 0:SEQ], self.small[:, k, at:at + n], actT[:, k, :], start=k == 0, stop=k == KT - 1)
        self.T.close(key, mm)

    def small_rows(self, pe, key, name, actT, banks=range(BANKS)):
        at, n = SMALL[name]
        t = self.T.open(pe, key, banks)
        for i in range(NT):
            for k in range(KT):
                mm = pe.matmul(t[:, i * n:(i + 1) * n], actT[:, k, i * P:(i + 1) * P], self.small[:, k, at:at + n],
                               start=k == 0, stop=k == KT - 1)
        self.T.close(key, mm)

    def tri_scores(self, pe, t, qT, kT, extra=None):
        for i in range(NT):
            out = t[:, i * P:i * P + (i + 1) * P]
            mm = pe.matmul(out, qT[:, i * P:(i + 1) * P], kT[:, 0:(i + 1) * P], start=True, stop=extra is None)
            if extra:
                mm = extra(i, out, (i + 1) * P)
        return mm

    def tri_transpose(self, pe, t, src):
        for b in range(3):
            mm = pe.transpose(t[:, b * P:(b + 1) * P], src[:, b * P:(b + 1) * P], self.ident[:, :])
        return mm

    def tri_values(self, pe, out, v0, v1, pT):
        pe.matmul(out, v0, pT[:, 0:2 * P], start=True, stop=False, skip_group_check=True)
        return pe.matmul(out[:, P:2 * P], v1, pT[:, 2 * P:3 * P], start=False, stop=True, skip_group_check=True)


class Phase:

    shared = {}

    def s(self, what):
        for family, counts in self.shared.items():
            if what in counts:
                return self.net.sem(f"{family}_{what}")
        return self.net.sem(f"{self.tag}_{what}")

    def base(self, what):
        n = 0
        for ph in self.net.phase_objects:
            if ph is self:
                return n
            for family, counts in self.shared.items():
                if what in counts and family in ph.shared:
                    n += ph.shared[family][what]

    def rows(self):
        return ()

    def rows_here(self, eng):
        eng.wait_ge(self.net.sem("row_loaded"), self.net.rows_at[self.tag])

    def gpsimd(self, pool):
        pass


class Start(Phase):
    tag = "start"

    def __init__(self, net):
        self.net = net

    def tensor(self, pe):
        pe.wait_ge(self.net.sem("constants_loaded"), 16 * 7)

    def vector(self, dve):
        net = self.net
        net.dv(dve.memset(net.ones[:, :], 1.0))
        net.dv(dve.memset(net.zeros[:, :], 0.0))
        dve.wait_ge(net.sem("constants_loaded"), 16 * 7)

    def scalar(self, act):
        net, io = self.net, self.net.io
        for dst, src in ((net.x, io["x"].rearrange("(i p) d -> p i d", p=P)),
                         (net.xT, io["xT"].rearrange("(k p) t -> p k t", p=P)),
                         (net.small, io["small"].rearrange("(k p) n -> p k n", p=P)),
                         (net.cols[:, :], io["cols"]), (net.ident[:, :], io["ident"]),
                         (net.causal[:, :], io["causal"]),
                         (net.bias_row[:, :], io["bias_row"].partition_broadcast(P))):
            act.dma_start(dst, src).then_inc(net.sem("constants_loaded"), 16)
        act.wait_ge(net.sem("constants_loaded"), 16 * 7)

    def gpsimd(self, pool):
        pool.wait_ge(self.net.sem("constants_loaded"), 16 * 7)


class LayerNorm(Phase):
    shared = {"ln": {"var": NT, "rstd": NT, "normed": NT}}

    def __init__(self, net, n):
        self.net, self.n, self.tag = net, n, f"ln{n}"

    def tensor(self, pe):
        net = self.net
        for i in range(NT):
            pe.wait_ge(self.s("normed"), self.base("normed") + i + 1)
            for c in range(2):
                t = net.T.open(pe, (self.tag, i, c))
                for k in range(4):
                    n0 = (4 * c + k) * P
                    mm = pe.transpose(t[:, k * P:(k + 1) * P], net.x[:, i, n0:n0 + P], net.ident[:, :])
                net.T.close((self.tag, i, c), mm)

    def vector(self, dve):
        net, s, st = self.net, self.net.dv, self.net.stat
        for i in range(NT):
            raw = st[:, 16 * i:16 * i + 12]
            for c in range(2):
                s(dve.bn_stats(raw[:, 6 * c:6 * c + 6], net.x[:, i, 512 * c:512 * c + 512]))
            s(dve.bn_aggr(st[:, 32 + 4 * i:34 + 4 * i], raw))
            s(dve.tensor_scalar(st[:, 34 + 4 * i:35 + 4 * i], st[:, 33 + 4 * i:34 + 4 * i], LN_EPS, None, ALU.add))
            dve.sem_inc(self.s("var"), 1)
        self.rows_here(dve)
        for i in range(NT):
            dve.wait_ge(self.s("rstd"), self.base("rstd") + i + 1)
            s(dve.tensor_scalar(net.x[:, i, :], net.x[:, i, :], st[:, 32 + 4 * i:33 + 4 * i],
                                st[:, 35 + 4 * i:36 + 4 * i], ALU.subtract, ALU.mult))
            s(dve.tensor_tensor(net.x[:, i, :], net.x[:, i, :], net.rows[:, 0, :], ALU.mult))
            s(dve.tensor_tensor(net.x[:, i, :], net.x[:, i, :], net.rows[:, 1, :], ALU.add))
            dve.sem_inc(self.s("normed"), 1)

    def gpsimd(self, pool):
        net, st = self.net, self.net.stat
        net.po(pool.memset(st[:, 60:61], -0.5))
        for i in range(NT):
            pool.wait_ge(self.s("var"), self.base("var") + i + 1)
            net.po(pool.tensor_tensor(st[:, 35 + 4 * i:36 + 4 * i], st[:, 34 + 4 * i:35 + 4 * i], st[:, 60:61], ALU.pow))
            pool.sem_inc(self.s("rstd"), 1)

    def scalar(self, act):
        net = self.net
        for i in range(NT):
            for c in range(2):
                t = net.T.take(act, (self.tag, i, c))
                net.ac(act.activation(net.xT[:, 4 * c:4 * c + 4, i * P:(i + 1) * P],
                                      t[:, :].rearrange("p (k t) -> p k t", k=4), ACT.Copy))
                net.T.free(act, (self.tag, i, c))

    def rows(self):
        return f"ln_g{self.n}", f"ln_b{self.n}"


class Residual(Phase):

    def tensor_out(self, pe, catT):
        for c in range(2):
            self.net.product(pe, (self.tag, "mix", c), catT)

    def vector_out(self, dve):
        net = self.net
        for c in range(2):
            for i in range(NT):
                t = net.T.take(dve, ((self.tag, "mix", c), i))
                xs = net.x[:, i, c * 512:(c + 1) * 512]
                net.dv(dve.scalar_tensor_tensor(xs, xs, ALPHA, t[:, :], ALU.mult, ALU.add))
                net.T.free(dve, ((self.tag, "mix", c), i))


class Heads:
    mlstm = False

    def alloc_heads(self, a):
        self.sm, self.p, self.pT = ([a.take(TRI) for _ in range(2)] for _ in range(3))
        self.hs = a.take(32).rearrange("p (b n) -> p b n", b=2)

    def tensor_heads(self, pe):
        net, T = self.net, self.net.T
        for h in range(HEADS + 1):
            if h < HEADS:
                if self.mlstm:
                    t = T.open(pe, (self.tag, "L", h))
                    for i in range(NT):
                        out, n = t[:, i * P:i * P + (i + 1) * P], (i + 1) * P
                        mm = self.head_bias(pe, h, i, out, n, True, True)
                    T.close((self.tag, "L", h), mm)
                t = T.open(pe, (self.tag, "S", h))
                for i in range(NT):
                    out, n = t[:, i * P:i * P + (i + 1) * P], (i + 1) * P
                    mm = pe.matmul(out, self.q(h)[:, i * P:(i + 1) * P], self.k(h)[:, 0:n], start=True,
                                   stop=self.mlstm)
                    if not self.mlstm:
                        mm = self.head_bias(pe, h, i, out, n, False, True)
                T.close((self.tag, "S", h), mm)
            if h >= 1:
                g = h - 1
                pe.wait_ge(self.s("p_ready"), self.base("p_ready") + g + 1)
                t = T.open(pe, (self.tag, "PT", g))
                for b in range(3):
                    mm = pe.transpose(t[:, b * P:(b + 1) * P], self.p[g % 2][:, b * P:(b + 1) * P], net.ident[:, :])
                T.close((self.tag, "PT", g), mm)
                t = T.open(pe, (self.tag, "O", g))
                pe.wait_ge(self.s("pT_ready"), self.base("pT_ready") + g + 1)
                lo, hi = self.out_rows(g)
                pe.matmul(t[lo:hi, 0:SEQ], self.v(g, 0), self.pT[g % 2][:, 0:2 * P], start=True, stop=False,
                          skip_group_check=True)
                mm = pe.matmul(t[lo:hi, P:SEQ], self.v(g, 1), self.pT[g % 2][:, 2 * P:3 * P], start=False, stop=True,
                               skip_group_check=True)
                T.close((self.tag, "O", g), mm)

    def vector_heads(self, dve):
        net, T, s = self.net, self.net.T, self.net.dv
        for h in range(HEADS + 1):
            if h < HEADS:
                sm, hs = self.sm[h % 2], self.hs[:, h % 2, :]
                key = (self.tag, "L" if self.mlstm else "S", h)
                t = T.take(dve, key)
                s(dve.tensor_tensor(sm, t[:, 0:TRI], self.mask, ALU.add))
                T.free(dve, key)
                for i in range(NT):
                    s(dve.tensor_reduce(hs[:, i:i + 1], sm[:, i * P:i * P + (i + 1) * P], AX, ALU.max))
                if self.mlstm:
                    s(dve.tensor_tensor(hs[:, 0:2], hs[:, 0:2], self.F_rows[:, :, h], ALU.max))
                s(dve.tensor_scalar(hs[:, 2:4], hs[:, 0:2], -1.0, None, ALU.mult))
                dve.sem_inc(self.s("max_ready"), 1)
            if h >= 1:
                g = h - 1
                p, hs = self.p[g % 2], self.hs[:, g % 2, :]
                dve.wait_ge(self.s("exp_ready"), self.base("exp_ready") + g + 1)
                if self.mlstm:
                    t = T.take(dve, (self.tag, "S", g))
                    for i in range(NT):
                        a, n = i * P, (i + 1) * P
                        s(dve.tensor_tensor_reduce(p[:, a:a + n], p[:, a:a + n], t[:, a:a + n], 1.0, 0.0, ALU.mult,
                                                   ALU.add, hs[:, 4 + i:5 + i]))
                    T.free(dve, (self.tag, "S", g))
                    s(dve.scalar_tensor_tensor(hs[:, 6:8], hs[:, 4:6], -1.0, hs[:, 4:6], ALU.mult, ALU.max))
                    s(dve.tensor_tensor(hs[:, 6:8], hs[:, 6:8], hs[:, 8:10], ALU.max))
                    s(dve.reciprocal(hs[:, 10:12], hs[:, 6:8]))
                else:
                    s(dve.reciprocal(hs[:, 10:12], hs[:, 4:6]))
                for i in range(NT):
                    a, n = i * P, (i + 1) * P
                    s(dve.tensor_scalar(p[:, a:a + n], p[:, a:a + n], hs[:, 10 + i:11 + i], None, ALU.mult))
                dve.sem_inc(self.s("p_ready"), 1)

    def scalar_heads(self, act):
        net, T, s = self.net, self.net.T, self.net.ac
        for h in range(HEADS + 1):
            if h < HEADS:
                act.wait_ge(self.s("max_ready"), self.base("max_ready") + h + 1)
                hs = self.hs[:, h % 2, :]
                for i in range(NT):
                    a, n = i * P, (i + 1) * P
                    kw = {} if self.mlstm else {"accum_out": hs[:, 4 + i:5 + i]}
                    s(act.activation(self.p[h % 2][:, a:a + n], self.sm[h % 2][:, a:a + n], ACT.Exp,
                                     bias=hs[:, 2 + i:3 + i], **kw))
                if self.mlstm:
                    s(act.activation(hs[:, 8:10], hs[:, 2:4], ACT.Exp))
                act.sem_inc(self.s("exp_ready"), 1)
            if h >= 1:
                g = h - 1
                t = T.take(act, (self.tag, "PT", g))
                s(act.activation(self.pT[g % 2], t[:, 0:TRI], ACT.Copy))
                T.free(act, (self.tag, "PT", g))
                act.sem_inc(self.s("pT_ready"), 1)
                t = T.take(act, (self.tag, "O", g))
                lo, hi = self.out_rows(g)
                self.keep_out(act, g, t[lo:hi, 0:SEQ])
                T.free(act, (self.tag, "O", g))
                act.sem_inc(self.s("out_kept"), 1)


HEAD_COUNTS = {w: HEADS for w in ("max_ready", "exp_ready", "p_ready", "pT_ready", "out_kept")}
GATE_COUNTS = {w: 2 * NT for w in ("gate_ready", "gate_used")}


class Fox(Residual, Heads):
    tag = "fox"
    shared = {"head": HEAD_COUNTS}

    def __init__(self, net):
        self.net = net
        a = Arena(net.scratch)
        self.catT = a.take(8 * SEQ, 8, SEQ)
        self.uT = a.take(4 * SEQ, 4, SEQ)
        self.qT = a.take(4 * SEQ, 4, SEQ)
        self.kT = a.take(4 * SEQ, 4, SEQ)
        self.vv = a.take(NT * 512, NT, 512)
        self.B = [a.take(512, 4, P) for _ in range(2)]
        self.Cz = [a.take(512, 16, 32) for _ in range(2)]
        self.g = [a.take(512) for _ in range(2)]
        self.t = a.take(512)
        self.h = [a.take(512) for _ in range(2)]
        self.C = [h.rearrange("p (a b) -> p a b", a=16) for h in self.h]
        self.w = a.take(20 * 16, 20, 16)
        b = Arena(net.scratch, a.at)
        self.ph = [a.take(16 * SEQ, 16, SEQ) for _ in range(2)]
        self.alloc_heads(b)
        self.sel = b.take(8 * P, 8, P, rows=8)
        self.ft = [b.take(SEQ, rows=8) for _ in range(6)]
        self.yT = self.catT[:, 4:8, :]
        self.mask = net.causal[:, :]
        self.sig = [self.B[0].rearrange("p a b -> p (a b)"), self.B[1].rearrange("p a b -> p (a b)")]

    def q(self, h):
        r = 64 * (h % 2)
        return self.qT[r:r + 64, h // 2, :]

    def k(self, h):
        r = 64 * (h % 2)
        return self.kT[r:r + 64, h // 2, :]

    def v(self, h, i):
        return self.vv[:, i, h * 64:(h + 1) * 64]

    def out_rows(self, h):
        return 64 * (h % 2), 64 * (h % 2) + 64

    def keep_out(self, act, h, out):
        lo, hi = self.out_rows(h)
        self.net.ac(act.activation(self.catT[lo:hi, h // 2, :], out, ACT.Copy))

    def head_bias(self, pe, h, i, out, n, first, last):
        c, negc = self.ft[4], self.ft[5]
        pe.matmul(out, self.sel[0:8, h, :], negc[0:8, 0:n], start=first, stop=False)
        return pe.matmul(out, c[0:8, i * P:(i + 1) * P], self.sel[0:8, h, 0:1].to_broadcast([8, n]), start=False,
                         stop=last)

    def tensor(self, pe):
        net, T = self.net, self.net.T
        low, high = range(4), range(4, 8)
        net.product_T(pe, "fox_u", net.xT, banks=high)
        pe.wait_ge(self.s("params_loaded"), 16 * 4)

        def bu(j):
            k, m = divmod(j, 4)
            t = T.open(pe, ("bu", j), low)
            for part in range(2):
                mm = pe.matmul(t[:, part * SEQ:(part + 1) * SEQ], self.B[part][32 * m:32 * m + 32, k, :],
                               self.uT[32 * m:32 * m + 32, k, :], start=True, stop=True)
            T.close(("bu", j), mm)

        def y(k):
            t = T.open(pe, ("y", k), high)
            for m in range(4):
                j = 4 * k + m
                pe.wait_ge(self.s("h_ready"), j + 1)
                for part in range(2):
                    mm = pe.matmul(t[32 * m:32 * m + 32, 0:SEQ], self.Cz[part][:, j, :],
                                   self.h[j % 2][:, part * SEQ:(part + 1) * SEQ], start=part == 0, stop=part == 1)
                if m < 3:
                    mm.then_inc(self.s("h_used"), 1)
                else:
                    T.close(("y", k), mm)
                if j + 4 < 16:
                    bu(j + 4)

        pe.wait_ge(self.s("u_kept"), 2)
        for j in range(4):
            bu(j)
        net.product_T(pe, "fox_q", net.xT, banks=high)
        y(0)
        net.product_T(pe, "fox_k", net.xT, banks=high)
        y(1)
        net.product(pe, "fox_v", net.xT, banks=high)
        y(2)
        net.small_T(pe, "fox_f", "fox_f", net.xT, banks=high)
        y(3)
        pe.wait_ge(self.s("qkv_kept"), 6)
        pe.wait_ge(self.s("sel_loaded"), 16)
        pe.wait_ge(self.s("c_ready"), 1)
        self.tensor_heads(pe)
        pe.wait_ge(self.s("gelu_kept"), 4)
        net.product_T(pe, "fox_glu", self.gT(), kt=4)
        pe.wait_ge(self.s("out_kept"), self.base("out_kept") + HEADS)
        pe.wait_ge(self.s("glu_done"), 2)
        self.tensor_out(pe, self.catT)

    def gT(self):
        return self.yT

    def scalar(self, act):
        net, T, s, io = self.net, self.net.T, self.net.ac, self.net.io
        for n, dst in enumerate(self.B):
            act.dma_start(dst, io["s5_b"][n].rearrange("p (k n) -> p k n", k=4)).then_inc(self.s("params_loaded"), 16)
        for n, dst in enumerate(self.C):
            act.dma_start(dst, io["s5_c"][n].rearrange("p (k n) -> p k n", k=16)).then_inc(self.s("params_loaded"), 16)
        for c in range(2):
            t = T.take(act, ("fox_u", c))
            s(act.activation(self.uT[:, 2 * c:2 * c + 2, :], t[:, :].rearrange("p (m t) -> p m t", m=2), ACT.Copy))
            T.free(act, ("fox_u", c))
            act.sem_inc(self.s("u_kept"), 1)
        for key, dst, scale in (("fox_q", self.qT, 0.125), ("fox_k", self.kT, 1.0)):
            for c in range(2):
                t = T.take(act, (key, c))
                s(act.activation(dst[:, 2 * c:2 * c + 2, :], t[:, :].rearrange("p (m t) -> p m t", m=2), ACT.Copy,
                                 scale=scale))
                T.free(act, (key, c))
                act.sem_inc(self.s("qkv_kept"), 1)
        for i in range(NT):
            t = T.take(act, ("fox_v", i))
            s(act.activation(self.vv[:, i, :], t[:, :], ACT.Copy))
            T.free(act, ("fox_v", i))
            act.sem_inc(self.s("qkv_kept"), 1)
        for k in range(4):
            act.wait_ge(self.s("y_kept"), k + 1)
            s(act.activation(self.yT[:, k, :], self.yT[:, k, :], ACT.Gelu_apprx_tanh))
            act.sem_inc(self.s("gelu_kept"), 1)
        act.dma_start(self.sel, io["sel"].rearrange("p (a b) -> p a b", a=8)).then_inc(self.s("sel_loaded"), 16)
        act.wait_ge(self.s("f_ready"), 1)
        s(act.activation(self.ft[2], self.ft[1], ACT.Exp))
        s(act.activation(self.ft[2], self.ft[2], ACT.Ln, bias=net.ones[0:8, 0:1]))
        act.sem_inc(self.s("log_ready"), 1)
        self.scalar_heads(act)
        for c in range(2):
            t = T.take(act, ("fox_glu", c))
            for m in range(2):
                s(act.activation(self.sig[c][:, m * SEQ:(m + 1) * SEQ], t[:, m * SEQ:(m + 1) * SEQ], ACT.Sigmoid,
                                 bias=net.col("b_glu", 2 * c + m)))
            T.free(act, ("fox_glu", c))
            act.sem_inc(self.s("glu_sig"), 1)

    def vector(self, dve):
        net, T, s = self.net, self.net.T, self.net.dv
        w = self.w
        are, aim = net.col("a_re", 0, 16), net.col("a_im", 0, 16)
        tt = lambda o, a, b, op: s(dve.tensor_tensor(o, a, b, op))
        ts = lambda o, a, c1, c2, op1, op2: s(dve.tensor_scalar(o, a, c1, c2, op1, op2))
        W = lambda n: w[:, n, :]
        exp_columns(net, dve, W(0), net.col("log_dt", 0, 16), W(13), W(14), W(15))
        tt(W(1), aim, W(0), ALU.mult)
        tt(W(2), are, W(0), ALU.mult)
        exp_columns(net, dve, W(3), W(2), W(13), W(14), W(15))
        ts(W(4), W(1), 1.0 / (2 * math.pi), ROUND, ALU.mult, ALU.add)
        ts(W(4), W(4), ROUND, None, ALU.subtract, ALU.bypass)
        for part in (TWO_PI_HI, TWO_PI_MID, TWO_PI_LO):
            s(dve.scalar_tensor_tensor(W(1), W(4), -part, W(1), ALU.mult, ALU.add))
        ts(W(4), W(1), 3.1415927, -3.1415927, ALU.min, ALU.max)
        sin, cos = W(6), W(7)
        sin_cos_columns(net, dve, sin, cos, W(4), W(13), W(14), W(15))
        tt(W(8), W(3), cos, ALU.mult)
        tt(W(9), W(3), sin, ALU.mult)
        ts(W(8), W(8), -1.0, None, ALU.add, ALU.bypass)
        tt(W(10), are, are, ALU.mult)
        tt(W(11), aim, aim, ALU.mult)
        tt(W(10), W(10), W(11), ALU.add)
        s(dve.reciprocal(W(10), W(10)))
        tt(W(11), W(8), are, ALU.mult)
        tt(W(12), W(9), aim, ALU.mult)
        tt(W(11), W(11), W(12), ALU.add)
        tt(W(11), W(11), W(10), ALU.mult)
        tt(W(12), W(9), are, ALU.mult)
        tt(W(13), W(8), aim, ALU.mult)
        tt(W(12), W(12), W(13), ALU.subtract)
        tt(W(12), W(12), W(10), ALU.mult)
        dve.wait_ge(self.s("params_loaded"), 16 * 4)
        zr = W(11).unsqueeze(2).to_broadcast([P, 16, 32])
        zi = W(12).unsqueeze(2).to_broadcast([P, 16, 32])
        tmp = self.t.rearrange("p (a b) -> p a b", a=16)
        tt(self.Cz[0], self.C[0], zr, ALU.mult)
        tt(tmp, self.C[1], zi, ALU.mult)
        tt(self.Cz[0], self.Cz[0], tmp, ALU.subtract)
        tt(self.Cz[1], self.C[0], zi, ALU.mult)
        tt(tmp, self.C[1], zr, ALU.mult)
        s(dve.scalar_tensor_tensor(self.Cz[1].rearrange("p a b -> p (a b)"), self.Cz[1].rearrange("p a b -> p (a b)"),
                                   -1.0, self.t, ALU.mult, ALU.subtract))
        pr, pi = self.ph
        s(dve.memset(pr[:, :, 0:1], 1.0))
        s(dve.memset(pi[:, :, 0:1], 0.0))
        wr, wi = W(14), W(15)
        s(dve.tensor_copy(wr, cos))
        s(dve.tensor_copy(wi, sin))
        n = 1
        while n < SEQ:
            for a in range(0, n, 32):
                m = min(32, n - a)
                tm = self.t[:, 0:16 * m].rearrange("p (a b) -> p a b", a=16)
                cr, ci = wr.unsqueeze(2).to_broadcast([P, 16, m]), wi.unsqueeze(2).to_broadcast([P, 16, m])
                tt(pr[:, :, n + a:n + a + m], pr[:, :, a:a + m], cr, ALU.mult)
                tt(tm, pi[:, :, a:a + m], ci, ALU.mult)
                tt(pr[:, :, n + a:n + a + m], pr[:, :, n + a:n + a + m], tm, ALU.subtract)
                tt(pi[:, :, n + a:n + a + m], pr[:, :, a:a + m], ci, ALU.mult)
                tt(tm, pi[:, :, a:a + m], cr, ALU.mult)
                tt(pi[:, :, n + a:n + a + m], pi[:, :, n + a:n + a + m], tm, ALU.add)
            tt(W(16), wr, wr, ALU.mult)
            tt(W(17), wi, wi, ALU.mult)
            tt(W(18), wr, wi, ALU.mult)
            tt(wr, W(16), W(17), ALU.subtract)
            ts(wi, W(18), 2.0, None, ALU.mult, ALU.bypass)
            n *= 2

        def y_keep(k):
            t = T.take(dve, ("y", k))
            s(dve.scalar_tensor_tensor(self.yT[:, k, :], self.uT[:, k, :], net.col("s5_d", k), t[:, 0:SEQ], ALU.mult,
                                       ALU.add))
            T.free(dve, ("y", k))
            dve.sem_inc(self.s("y_kept"), 1)

        def parts(v):
            return v.rearrange("p (a t) -> p a t", a=2)

        for j in range(16):
            cr = pr[:, j:j + 1, :].to_broadcast([P, 2, SEQ])
            ci = pi[:, j:j + 1, :].to_broadcast([P, 2, SEQ])
            g, u, t, h = self.g[0], self.g[1], self.t, self.h[j % 2]
            b = T.take(dve, ("bu", j))
            tt(parts(u), parts(b[:, :]), cr, ALU.mult)
            tt(parts(t), parts(b[:, :]), ci, ALU.mult)
            T.free(dve, ("bu", j))
            tt(g[:, 0:SEQ], u[:, 0:SEQ], t[:, SEQ:], ALU.add)
            tt(g[:, SEQ:], u[:, SEQ:], t[:, 0:SEQ], ALU.subtract)
            for part in range(2):
                xs = g[:, part * SEQ:(part + 1) * SEQ]
                s(dve.tensor_tensor_scan(xs, W(3)[:, j:j + 1].to_broadcast([P, SEQ]), xs, 0.0, ALU.mult, ALU.add))
            tt(parts(u), parts(g), cr, ALU.mult)
            tt(parts(t), parts(g), ci, ALU.mult)
            if j >= 2:
                k, m = divmod(j - 2, 4)
                if m < 3:
                    dve.wait_ge(self.s("h_used"), 3 * k + m + 1)
                else:
                    T.take(dve, ("y", k))
            tt(h[:, 0:SEQ], u[:, 0:SEQ], t[:, SEQ:], ALU.subtract)
            tt(h[:, SEQ:], u[:, SEQ:], t[:, 0:SEQ], ALU.add)
            dve.sem_inc(self.s("h_ready"), 1)
            if j % 4 == 3 and j > 3:
                y_keep(j // 4 - 1)
        y_keep(3)
        ft = self.ft
        t = T.take(dve, "fox_f")
        ts(ft[0], t[0:8, 0:SEQ], net.col("fox_f_bias", rows=8), None, ALU.add, ALU.bypass)
        T.free(dve, "fox_f")
        log_sigmoid_front(net, dve, ft[0], ft[1])
        dve.sem_inc(self.s("f_ready"), 1)
        dve.wait_ge(self.s("log_ready"), 1)
        s(dve.scalar_tensor_tensor(ft[3], ft[0], 0.0, ft[2], ALU.min, ALU.subtract))
        s(dve.tensor_tensor_scan(ft[4], net.ones[0:8, 0:SEQ], ft[3], 0.0, ALU.mult, ALU.add))
        ts(ft[5], ft[4], -1.0, None, ALU.mult, ALU.bypass)
        dve.sem_inc(self.s("c_ready"), 1)
        self.vector_heads(dve)
        T.take(dve, ("fox_glu", 1))
        for c in range(2):
            dve.wait_ge(self.s("glu_sig"), c + 1)
            y = self.yT[:, 2 * c:2 * c + 2, :].rearrange("p a b -> p (a b)")
            tt(y, y, self.sig[c], ALU.mult)
            dve.sem_inc(self.s("glu_done"), 1)
        self.vector_out(dve)

    def gpsimd(self, pool):
        pass


class Mlstm(Residual, Heads):
    tag = "mlstm"
    shared = {"head": HEAD_COUNTS}
    mlstm = True

    def __init__(self, net):
        self.net = net
        a = Arena(net.scratch)
        self.catT = a.take(8 * SEQ, 8, SEQ)
        self.qkT = a.take(16 * SEQ, 16, SEQ)
        self.vv = a.take(NT * D, NT, D)
        self.oT = a.take(8 * SEQ, 8, SEQ)
        self.pad = [a.take(2 * (SEQ + 3), 2, SEQ + 3) for _ in range(2)]
        self.conv = [a.take(SEQ) for _ in range(4)]
        self.silu = [a.take(SEQ) for _ in range(2)]
        self.alloc_heads(a)
        self.sel = a.take(8 * P, 8, P, rows=8)
        self.ft = [a.take(SEQ, rows=8) for _ in range(6)]
        self.F_rows = a.take(16, NT, 8)
        self.mask = net.causal[:, :]

    def q(self, h):
        return self.qkT[:, h, :]

    def k(self, h):
        return self.qkT[:, 8 + h, :]

    def v(self, h, i):
        return self.vv[:, i, h * P:(h + 1) * P]

    def out_rows(self, h):
        return 0, P

    def keep_out(self, act, h, out):
        self.net.ac(act.activation(self.catT[:, h, :], out, ACT.Copy))

    def head_bias(self, pe, h, i, out, n, first, last):
        F, iF = self.ft[4], self.ft[5]
        pe.matmul(out, self.sel[0:8, h, :], iF[0:8, 0:n], start=first, stop=False)
        return pe.matmul(out, F[0:8, i * P:(i + 1) * P], self.sel[0:8, h, 0:1].to_broadcast([8, n]), start=False,
                         stop=last)

    def tensor(self, pe):
        net, T = self.net, self.net.T
        net.small_T(pe, "mlstm_f", "mlstm_f", net.xT)
        net.small_T(pe, "mlstm_i", "mlstm_i", net.xT)
        for b in range(4):
            net.product_T(pe, ("mlstm_qk", b), net.xT)
        for b in range(2):
            net.product(pe, ("mlstm_v", b), net.xT)
        for b in range(2):
            net.product_T(pe, ("mlstm_o", b), net.xT)
        pe.wait_ge(self.s("F_ready"), 1)
        t = T.open(pe, "mlstm_FT")
        for i in range(NT):
            mm = pe.transpose(t[:, 8 * i:8 * i + 8], self.ft[4][0:8, i * P:(i + 1) * P], net.ident[0:8, 0:8])
        T.close("mlstm_FT", mm)
        pe.wait_ge(self.s("qk_ready"), 16)
        pe.wait_ge(self.s("v_kept"), 4)
        pe.wait_ge(self.s("sel_loaded"), 16)
        self.tensor_heads(pe)
        pe.wait_ge(self.s("gated"), 1)
        self.tensor_out(pe, self.catT)

    def scalar(self, act):
        net, T, s, io = self.net, self.net.T, self.net.ac, self.net.io
        act.dma_start(self.sel, io["sel"].rearrange("p (a b) -> p a b", a=8)).then_inc(self.s("sel_loaded"), 16)
        act.wait_ge(self.s("f_ready"), 1)
        s(act.activation(self.ft[2], self.ft[1], ACT.Exp))
        s(act.activation(self.ft[2], self.ft[2], ACT.Ln, bias=net.ones[0:8, 0:1]))
        act.sem_inc(self.s("log_ready"), 1)
        for j in range(16):
            act.wait_ge(self.s("conv_ready"), j + 1)
            if j < 8:
                s(act.activation(self.qkT[:, j, :], self.conv[j % 4], ACT.Silu))
            else:
                s(act.activation(self.qkT[:, j, :], self.conv[j % 4], ACT.Silu))
                s(act.activation(self.qkT[:, j, :], self.qkT[:, j, :], ACT.Copy, scale=P ** -0.5))
            act.sem_inc(self.s("qk_ready"), 1)
        for b in range(2):
            for i in range(NT):
                key = (("mlstm_v", b), i)
                t = T.take(act, key)
                s(act.activation(self.vv[:, i, b * 512:(b + 1) * 512], t[:, :], ACT.Copy))
                T.free(act, key)
                act.sem_inc(self.s("v_kept"), 1)
        for b in range(2):
            for c in range(2):
                key = (("mlstm_o", b), c)
                t = T.take(act, key)
                s(act.activation(self.oT[:, 4 * b + 2 * c:4 * b + 2 * c + 2, :],
                                 t[:, :].rearrange("p (m t) -> p m t", m=2), ACT.Sigmoid))
                T.free(act, key)
        act.sem_inc(self.s("o_kept"), 1)
        self.scalar_heads(act)

    def vector(self, dve):
        net, T, s = self.net, self.net.T, self.net.dv
        ft = self.ft
        t = T.take(dve, "mlstm_f")
        s(dve.tensor_scalar(ft[0], t[0:8, 0:SEQ], net.col("mlstm_f_bias", rows=8), None, ALU.add))
        T.free(dve, "mlstm_f")
        log_sigmoid_front(net, dve, ft[0], ft[1])
        dve.sem_inc(self.s("f_ready"), 1)
        for pad in self.pad:
            s(dve.memset(pad[:, :, 0:3], 0.0))
        dve.wait_ge(self.s("log_ready"), 1)
        s(dve.scalar_tensor_tensor(ft[3], ft[0], 0.0, ft[2], ALU.min, ALU.subtract))
        s(dve.tensor_tensor_scan(ft[4], net.ones[0:8, 0:SEQ], ft[3], 0.0, ALU.mult, ALU.add))
        t = T.take(dve, "mlstm_i")
        s(dve.scalar_tensor_tensor(ft[5], t[0:8, 0:SEQ], net.col("mlstm_i_bias", rows=8), ft[4], ALU.add, ALU.subtract))
        T.free(dve, "mlstm_i")
        dve.sem_inc(self.s("F_ready"), 1)
        for b in range(4):
            for c in range(2):
                key, pad = (("mlstm_qk", b), c), self.pad[c]
                t = T.take(dve, key)
                s(dve.tensor_copy(pad[:, :, 3:], t[:, :].rearrange("p (m t) -> p m t", m=2)))
                T.free(dve, key)
                for m in range(2):
                    j = 4 * b + 2 * c + m
                    y = self.conv[j % 4]
                    if j >= 4:
                        dve.wait_ge(self.s("qk_ready"), j - 3)
                    s(dve.tensor_scalar(y, pad[:, m, 0:SEQ], net.col("conv_w", j), net.col("conv_b", j), ALU.mult,
                                        ALU.add))
                    for tap in range(1, 4):
                        s(dve.scalar_tensor_tensor(y, pad[:, m, tap:tap + SEQ], net.col("conv_w", 16 * tap + j), y,
                                                   ALU.mult, ALU.add))
                    dve.sem_inc(self.s("conv_ready"), 1)
        t = T.take(dve, "mlstm_FT")
        s(dve.tensor_copy(self.F_rows, t[:, 0:16].rearrange("p (i h) -> p i h", i=NT)))
        T.free(dve, "mlstm_FT")
        self.vector_heads(dve)
        dve.wait_ge(self.s("o_kept"), 1)
        dve.wait_ge(self.s("out_kept"), self.base("out_kept") + HEADS)
        s(dve.tensor_tensor(self.catT, self.catT, self.oT, ALU.mult))
        dve.sem_inc(self.s("gated"), 1)
        self.vector_out(dve)

    def gpsimd(self, pool):
        pass


def gate_rows(net, pe, key):
    for c in range(2):
        us = [net.use_unit(pe) for _ in range(2)]
        t = net.T.open(pe, (key, c))
        for k in range(KT):
            w = us[k // 4][1].rearrange("p (k n) -> p k n", k=4)
            mm = pe.matmul(t[:, :], net.mod[:, 32 + k:33 + k].to_broadcast([P, P]), w[:, k % 4, :], start=k == 0,
                           stop=k == KT - 1)
        net.T.close((key, c), mm)
        net.release([u for u, _ in us], (key, c))


def keep_gate_rows(net, dve, key, out):
    for c in range(2):
        t = net.T.take(dve, (key, c))
        net.dv(dve.tensor_tensor(out[:, c * 512:(c + 1) * 512], t[:, :], net.rows[:, 0, c * 512:(c + 1) * 512], ALU.add))
        net.T.free(dve, (key, c))


class Modulation(Phase):
    tag = "ada"

    def __init__(self, net):
        self.net = net

    def tensor(self, pe):
        net, T = self.net, self.net.T
        pe.wait_ge(self.s("silu_ready"), 1)
        for b in range(8):
            us = [net.use_unit(pe) for _ in range(2)]
            t = T.open(pe, ("ada", b))
            for m in range(4):
                for k in range(KT):
                    w = us[k // 4][1].rearrange("p (k n) -> p k n", k=4)
                    mm = pe.matmul(t[:, m:m + 1], w[:, k % 4, m * P:(m + 1) * P], net.mod[:, 32 + k:33 + k],
                                   start=k == 0, stop=k == KT - 1)
            T.close(("ada", b), mm)
            net.release([u for u, _ in us], ("ada", b))

    def scalar(self, act):
        self.net.ac(act.activation(self.net.mod[:, 32:40], self.net.col("c", 0, 8), ACT.Silu))
        act.sem_inc(self.s("silu_ready"), 1)

    def vector(self, dve):
        net, s, mod = self.net, self.net.dv, self.net.mod
        for b in range(8):
            t = net.T.take(dve, ("ada", b))
            s(dve.tensor_tensor(mod[:, 4 * b:4 * b + 4], t[:, 0:4], net.col("ada_b", 4 * b, 4), ALU.add))
            net.T.free(dve, ("ada", b))
        for n in range(2):
            sc = mod[:, 16 * n + 8:16 * n + 16]
            s(dve.tensor_scalar(sc, sc, 1.0, None, ALU.add))
            s(dve.tensor_tensor(sc, sc, net.col(f"norm{n + 1}_g", 0, 8), ALU.mult))


class RmsNorm(Phase):
    shared = {"rms": {"squares": NT, "mean": NT, "rstd": NT, "normed": NT}}

    def __init__(self, net, n):
        self.net, self.n, self.tag = net, n, f"rms{n}"
        a = Arena(net.scratch)
        self.xn = a.take(NT * D, NT, D)
        self.junk = a.take(D)

    def rows(self):
        return ("final_g",) if self.n == 2 else ()

    def scalar(self, act):
        net, s, st = self.net, self.net.ac, self.net.stat
        for i in range(NT):
            s(act.activation(self.junk, net.x[:, i, :], ACT.Square, accum_out=st[:, i:i + 1]))
            act.sem_inc(self.s("squares"), 1)
        if self.n == 2:
            return
        for i in range(NT):
            for c in range(2):
                t = net.T.take(act, (self.tag, i, c))
                for k in range(4):
                    j = 4 * c + k
                    s(act.activation(net.xT[:, j, i * P:(i + 1) * P], t[:, k * P:(k + 1) * P], ACT.Identity,
                                     scale=net.mod[:, 16 * self.n + 8 + j:16 * self.n + 9 + j],
                                     bias=net.mod[:, 16 * self.n + j:16 * self.n + j + 1]))
                net.T.free(act, (self.tag, i, c))

    def tensor(self, pe):
        net = self.net
        if self.n == 2:
            return
        for i in range(NT):
            pe.wait_ge(self.s("normed"), self.base("normed") + i + 1)
            for c in range(2):
                t = net.T.open(pe, (self.tag, i, c))
                for k in range(4):
                    n0 = (4 * c + k) * P
                    mm = pe.transpose(t[:, k * P:(k + 1) * P], self.xn[:, i, n0:n0 + P], net.ident[:, :])
                net.T.close((self.tag, i, c), mm)

    def vector(self, dve):
        net, s, st = self.net, self.net.dv, self.net.stat
        for i in range(NT):
            dve.wait_ge(self.s("squares"), self.base("squares") + i + 1)
            s(dve.tensor_scalar(st[:, 2 + i:3 + i], st[:, i:i + 1], 1.0 / D, RMS_EPS, ALU.mult, ALU.add))
            dve.sem_inc(self.s("mean"), 1)
        for i in range(NT):
            dve.wait_ge(self.s("rstd"), self.base("rstd") + i + 1)
            out = net.x if self.n == 2 else self.xn
            s(dve.tensor_scalar(out[:, i, :], net.x[:, i, :], st[:, 4 + i:5 + i], None, ALU.mult))
            if self.n == 2:
                self.rows_here(dve)
                s(dve.tensor_tensor(out[:, i, :], out[:, i, :], net.rows[:, 0, :], ALU.mult))
            dve.sem_inc(self.s("normed"), 1)

    def gpsimd(self, pool):
        net, st = self.net, self.net.stat
        net.po(pool.memset(st[:, 60:61], -0.5))
        for i in range(NT):
            pool.wait_ge(self.s("mean"), self.base("mean") + i + 1)
            net.po(pool.tensor_tensor(st[:, 4 + i:5 + i], st[:, 2 + i:3 + i], st[:, 60:61], ALU.pow))
            pool.sem_inc(self.s("rstd"), 1)


class Branch(Phase):

    def tensor_branch(self, pe, catT, kt=KT):
        for c in range(2):
            self.net.product(pe, (self.tag, "gate", c), self.net.xT)
            self.net.product(pe, (self.tag, "out", c), catT, kt=kt)

    def scalar_branch(self, act):
        net = self.net
        for c in range(2):
            for i in range(NT):
                key = ((self.tag, "gate", c), i)
                t = net.T.take(act, key)
                if c:
                    act.wait_ge(self.s("gate_used"), self.base("gate_used") + i + 1)
                net.ac(act.activation(self.gate[i], t[:, :], ACT.Sigmoid))
                net.T.free(act, key)
                act.sem_inc(self.s("gate_ready"), 1)

    def vector_branch(self, dve, first):
        net, s = self.net, self.net.dv
        for c in range(2):
            for i in range(NT):
                key = ((self.tag, "out", c), i)
                dve.wait_ge(self.s("gate_ready"), self.base("gate_ready") + 2 * c + i + 1)
                t = net.T.take(dve, key)
                m = self.merged[:, i, c * 512:(c + 1) * 512]
                if first:
                    s(dve.tensor_tensor(m, self.gate[i], t[:, :], ALU.mult))
                else:
                    s(dve.tensor_tensor(self.gate[i], self.gate[i], t[:, :], ALU.mult))
                    s(dve.tensor_tensor(m, m, self.gate[i], ALU.add))
                net.T.free(dve, key)
                dve.sem_inc(self.s("gate_used"), 1)

    def take_merged(self):
        return Arena(self.net.scratch, SCRATCH - NT * D).take(NT * D, NT, D)


class Indexed(Branch, Heads):
    tag = "dsa"
    shared = {"head": HEAD_COUNTS, "branch": GATE_COUNTS}

    def __init__(self, net):
        self.net = net
        a = Arena(net.scratch)
        self.merged = self.take_merged()
        self.catT = a.take(8 * SEQ, 8, SEQ)
        self.qT = a.take(8 * SEQ, 8, SEQ)
        self.kT = a.take(8 * SEQ, 8, SEQ)
        self.vv = a.take(NT * D, NT, D)
        self.iqT = a.take(4 * SEQ, 4, SEQ)
        self.ikT = a.take(SEQ)
        self.iw = a.take(16, NT, 8)
        self.X = a.take(8 * SEQ, 8, SEQ)
        self.J = a.take(P)
        self.alloc_heads(a)
        self.score, self.work, self.term, self.sel_mask = (a.take(TRI) for _ in range(4))
        self.top = a.take(8)
        self.gate = [a.take(512) for _ in range(2)]
        self.buckets = a.take(TRI, rows=32)
        self.rel = a.take(8, rows=32)
        self.U = a.take(TRI, rows=8)
        assert a.at <= SCRATCH - NT * D
        self.mask = self.sel_mask

    def q(self, h):
        return self.qT[:, h, :]

    def k(self, h):
        return self.kT[:, h, :]

    def v(self, h, i):
        return self.vv[:, i, h * P:(h + 1) * P]

    def out_rows(self, h):
        return 0, P

    def keep_out(self, act, h, out):
        self.net.ac(act.activation(self.catT[:, h, :], out, ACT.Copy))

    def head_bias(self, pe, h, i, out, n, first, last):
        at = P if i == 0 else 0
        return pe.matmul(out, self.J, self.X[:, h, at:at + n], start=first, stop=last)

    def tensor(self, pe):
        net, T = self.net, self.net.T
        net.small_rows(pe, "dsa_iw", "idx_w", net.xT)
        u, w = net.use_unit(pe)
        t = T.open(pe, "dsa_ik")
        for k in range(KT):
            mm = pe.matmul(t[:, 0:SEQ], w[:, k * P:(k + 1) * P], net.xT[:, k, :], start=k == 0, stop=k == KT - 1)
        T.close("dsa_ik", mm)
        net.release([u], "dsa_ik")
        net.product_T(pe, "dsa_iq", net.xT)
        pe.wait_ge(self.s("tables_loaded"), 48)
        t = T.open(pe, "dsa_U")
        T.close("dsa_U", pe.matmul(t[0:8, 0:TRI], self.rel[0:32, 0:8], self.buckets[0:32, :], start=True, stop=True))
        pe.wait_ge(self.s("index_kept"), 3)
        for h in range(HEADS):
            t = T.open(pe, ("dsa_index", h))
            r = 64 * (h % 2)
            for i in range(NT):
                mm = pe.matmul(t[:, i * P:i * P + (i + 1) * P], self.iqT[r:r + 64, h // 2, i * P:(i + 1) * P],
                               self.ikT[r:r + 64, 0:(i + 1) * P], start=True, stop=True)
            T.close(("dsa_index", h), mm)
            if h == 3:
                for b in range(2):
                    net.product_T(pe, ("dsa_q", b), net.xT)
        for b in range(2):
            net.product_T(pe, ("dsa_k", b), net.xT)
        for b in range(2):
            net.product(pe, ("dsa_v", b), net.xT)
        pe.wait_ge(self.s("qkv_kept"), 12)
        pe.wait_ge(self.s("X_loaded"), 16)
        self.tensor_heads(pe)
        pe.wait_ge(self.s("out_kept"), self.base("out_kept") + HEADS)
        self.tensor_branch(pe, self.catT)

    def scalar(self, act):
        net, T, s, io = self.net, self.net.T, self.net.ac, self.net.io
        for dst, src in ((self.rel, io["rel_bias"]), (self.buckets, io["buckets"]), (self.J, io["flip"])):
            act.dma_start(dst, src).then_inc(self.s("tables_loaded"), 16)
        t = T.take(act, "dsa_ik")
        s(act.activation(self.ikT, t[:, 0:SEQ], ACT.Copy))
        T.free(act, "dsa_ik")
        act.sem_inc(self.s("index_kept"), 1)
        for c in range(2):
            t = T.take(act, ("dsa_iq", c))
            s(act.activation(self.iqT[:, 2 * c:2 * c + 2, :], t[:, :].rearrange("p (m t) -> p m t", m=2), ACT.Copy))
            T.free(act, ("dsa_iq", c))
            act.sem_inc(self.s("index_kept"), 1)
        t = T.take(act, "dsa_U")
        s(act.activation(self.U, t[0:8, 0:TRI], ACT.Copy))
        T.free(act, "dsa_U")
        act.dma_start(io["bias_by_distance"], self.U).then_inc(self.s("U_stored"), 16)
        act.wait_ge(self.s("U_stored"), 16)
        u = io["bias_by_distance"]
        act.dma_start(self.X, bass.AP(u.tensor, u.offset, [[1, P], [TRI, 8], [1, SEQ]])).then_inc(self.s("X_loaded"), 16)
        for key, dst, scale in (("dsa_q", self.qT, P ** -0.5), ("dsa_k", self.kT, 1.0)):
            for b in range(2):
                for c in range(2):
                    t = T.take(act, ((key, b), c))
                    j = 4 * b + 2 * c
                    s(act.activation(dst[:, j:j + 2, :], t[:, :].rearrange("p (m t) -> p m t", m=2), ACT.Copy,
                                     scale=scale))
                    T.free(act, ((key, b), c))
                    act.sem_inc(self.s("qkv_kept"), 1)
        for b in range(2):
            for i in range(NT):
                t = T.take(act, (("dsa_v", b), i))
                s(act.activation(self.vv[:, i, b * 512:(b + 1) * 512], t[:, :], ACT.Copy))
                T.free(act, (("dsa_v", b), i))
                act.sem_inc(self.s("qkv_kept"), 1)
        self.scalar_heads(act)
        self.scalar_branch(act)

    def vector(self, dve):
        net, T, s = self.net, self.net.T, self.net.dv
        t = T.take(dve, "dsa_iw")
        s(dve.tensor_scalar(self.iw, t[:, 0:16].rearrange("p (i h) -> p i h", i=NT), 512 ** -0.5, None, ALU.mult))
        T.free(dve, "dsa_iw")
        for h in range(HEADS):
            t = T.take(dve, ("dsa_index", h))
            dst = self.score if h == 0 else self.term
            for i in range(NT):
                a, n = i * P, (i + 1) * P
                s(dve.tensor_scalar(dst[:, a:a + n], t[:, a:a + n], 0.0, self.iw[:, i, h:h + 1], ALU.max, ALU.mult))
            T.free(dve, ("dsa_index", h))
            if h:
                s(dve.tensor_tensor(self.score, self.score, self.term, ALU.add))
        s(dve.tensor_tensor(self.score, self.score, net.causal[:, :], ALU.add))
        for i in range(NT):
            a, n = i * P, (i + 1) * P
            x, y = self.score[:, a:a + n], self.work[:, a:a + n]
            for _ in range(TOPK // 8):
                s(dve.max(self.top, x))
                s(dve.match_replace(y, self.top, x, TAKEN))
                x, y = y, x
            s(dve.tensor_scalar(self.sel_mask[:, a:a + n], x, TAKEN / 2, MASKED, ALU.is_gt, ALU.mult))
        s(dve.tensor_tensor(self.sel_mask, self.sel_mask, net.causal[:, :], ALU.add))
        self.vector_heads(dve)
        self.vector_branch(dve, True)


class Hgrn(Branch):
    tag = "hgrn"
    shared = {"branch": GATE_COUNTS}

    def __init__(self, net):
        self.net = net
        a = Arena(net.scratch)
        self.merged = self.take_merged()
        self.qT = a.take(8 * SEQ, 8, SEQ)
        self.kT = a.take(8 * SEQ, 8, SEQ)
        self.b = a.take(8 * SEQ, 8, SEQ)
        self.M = [a.take(8 * SEQ, 8, SEQ) for _ in range(2)]
        self.vv = a.take(NT * D, NT, D)
        self.AT = a.take(16 * P, 16, P)
        self.AT01 = a.take(8 * P, 8, P)
        self.level_masks = a.take(8 * P, 8, P)
        self.small = a.take(80)
        self.gate = [self.b.rearrange("p a b -> p (a b)")[:, c * 512:(c + 1) * 512] for c in range(2)]
        self.o = self.M[1].rearrange("p a b -> p (a b)").rearrange("p (i d) -> p i d", i=NT)
        self.g = self.M[0].rearrange("p a b -> p (a b)").rearrange("p (i d) -> p i d", i=NT)
        self.sq = self.kT.rearrange("p a b -> p (a b)").rearrange("p (i d) -> p i d", i=NT)
        self.catT = self.qT
        assert a.at <= SCRATCH - NT * D

    def rows(self):
        return ("hgrn_g",)

    def tensor(self, pe):
        net, T = self.net, self.net.T
        for b in range(2):
            net.product_T(pe, ("hgrn_f", b), net.xT)
        for b in range(2):
            net.product_T(pe, ("hgrn_q", b), net.xT)
        for b in range(2):
            net.product(pe, ("hgrn_v", b), net.xT)
        pe.wait_ge(self.s("k_ready"), 1)
        pe.wait_ge(self.s("q_kept"), 4)
        for n in range(4):
            t = T.open(pe, ("hgrn_level", -1, n))
            for m in range(4):
                h, i = divmod(4 * n + m, 2)
                mm = pe.matmul(t[:, m * P:(m + 1) * P], self.kT[:, h, i * P:(i + 1) * P],
                               self.qT[:, h, i * P:(i + 1) * P], start=True, stop=True)
            T.close(("hgrn_level", -1, n), mm)
        pe.wait_ge(self.s("m_ready"), 1)
        for n in range(2):
            t = T.open(pe, ("hgrn_cross", n))
            for m in range(4):
                h = 4 * n + m
                mm = pe.matmul(t[:, m * P:(m + 1) * P], self.M[0][:, h, 0:P], self.M[0][:, h, P:SEQ], start=True,
                               stop=True)
            T.close(("hgrn_cross", n), mm)
        for lv in range(len(LEVELS)):
            pe.wait_ge(self.s("m_ready"), lv + 2)
            M = self.M[(lv + 1) % 2]
            for n in range(4):
                t = T.open(pe, ("hgrn_level", lv, n))
                for m in range(4):
                    h, i = divmod(4 * n + m, 2)
                    tok = M[:, h, i * P:(i + 1) * P]
                    mm = pe.matmul(t[:, m * P:(m + 1) * P], tok, tok, start=True, stop=True)
                T.close(("hgrn_level", lv, n), mm)
        for b in range(2):
            net.product(pe, ("hgrn_g", b), net.xT)
        pe.wait_ge(self.s("v_kept"), 4)
        pe.wait_ge(self.s("at_ready"), 1)
        pe.wait_ge(self.s("cross_kept"), 2)
        for i in range(NT):
            for n in range(2):
                t = T.open(pe, ("hgrn_o", i, n))
                for m in range(4):
                    h = 4 * n + m
                    out, vs = t[:, m * P:(m + 1) * P], slice(h * P, (h + 1) * P)
                    if i:
                        pe.matmul(out, self.AT01[:, h, :], self.vv[:, 0, vs], start=True, stop=False)
                    mm = pe.matmul(out, self.AT[:, 2 * h + i, :], self.vv[:, i, vs], start=i == 0, stop=True)
                T.close(("hgrn_o", i, n), mm)
        for i in range(NT):
            for n in range(2):
                pe.wait_ge(self.s("o_gated"), 2 * i + n + 1)
                t = T.open(pe, ("hgrn_oT", i, n))
                for m in range(4):
                    h = 4 * n + m
                    mm = pe.transpose(t[:, m * P:(m + 1) * P], self.o[:, i, h * P:(h + 1) * P], net.ident[:, :])
                T.close(("hgrn_oT", i, n), mm)
        pe.wait_ge(self.s("oT_kept"), 4)
        self.tensor_branch(pe, self.catT)

    def scalar(self, act):
        net, T, s, io = self.net, self.net.T, self.net.ac, self.net.io
        act.dma_start(self.level_masks.bitcast(I32), io["level_masks"].rearrange("p (a b) -> p a b", a=8))\
           .then_inc(self.s("masks_loaded"), 16)
        act.wait_ge(self.s("lb_diff"), 1)
        s(act.activation(self.small[:, 8:16], self.small[:, 0:8], ACT.Exp))
        act.sem_inc(self.s("lb_exp"), 1)
        for b in range(2):
            for c in range(2):
                t = T.take(act, (("hgrn_f", b), c))
                j = 4 * b + 2 * c
                s(act.activation(self.kT[:, j:j + 2, :], t[:, :].rearrange("p (m t) -> p m t", m=2), ACT.Sigmoid))
                T.free(act, (("hgrn_f", b), c))
                act.sem_inc(self.s("sig_ready"), 1)
        act.wait_ge(self.s("f_ready"), 1)
        s(act.activation(self.b, self.kT, ACT.Ln))
        act.sem_inc(self.s("log_ready"), 1)
        for b in range(2):
            for c in range(2):
                t = T.take(act, (("hgrn_q", b), c))
                j = 4 * b + 2 * c
                s(act.activation(self.qT[:, j:j + 2, :], t[:, :].rearrange("p (m t) -> p m t", m=2), ACT.Copy))
                T.free(act, (("hgrn_q", b), c))
                act.sem_inc(self.s("q_kept"), 1)
        for b in range(2):
            for i in range(NT):
                t = T.take(act, (("hgrn_v", b), i))
                s(act.activation(self.vv[:, i, b * 512:(b + 1) * 512], t[:, :], ACT.Copy))
                T.free(act, (("hgrn_v", b), i))
                act.sem_inc(self.s("v_kept"), 1)
        for lv in range(-1, len(LEVELS)):
            M = self.M[(lv + 1) % 2]
            act.wait_ge(self.s("e_ready"), lv + 2)
            s(act.activation(M, M, ACT.Exp))
            act.sem_inc(self.s("exp_ready"), 1)
            if lv < 0:
                for n in range(2):
                    t = T.take(act, ("hgrn_cross", n))
                    s(act.activation(self.AT01[:, 4 * n:4 * n + 4, :], t[:, :].rearrange("p (m t) -> p m t", m=4),
                                     ACT.Copy))
                    T.free(act, ("hgrn_cross", n))
                    act.sem_inc(self.s("cross_kept"), 1)
        act.wait_ge(self.s("at_ready"), 1)
        for b in range(2):
            for i in range(NT):
                t = T.take(act, (("hgrn_g", b), i))
                s(act.activation(self.g[:, i, b * 512:(b + 1) * 512], t[:, :], ACT.Silu))
                T.free(act, (("hgrn_g", b), i))
                act.sem_inc(self.s("g_kept"), 1)
        for i in range(NT):
            for n in range(2):
                t = T.take(act, ("hgrn_o", i, n))
                s(act.activation(self.o[:, i, n * 512:(n + 1) * 512], t[:, :], ACT.Copy))
                T.free(act, ("hgrn_o", i, n))
                act.sem_inc(self.s("o_kept"), 1)
        for i in range(NT):
            for n in range(2):
                t = T.take(act, ("hgrn_oT", i, n))
                s(act.activation(self.catT[:, 4 * n:4 * n + 4, i * P:(i + 1) * P],
                                 t[:, :].rearrange("p (m t) -> p m t", m=4), ACT.Copy))
                T.free(act, ("hgrn_oT", i, n))
                act.sem_inc(self.s("oT_kept"), 1)
        self.scalar_branch(act)

    def vector(self, dve):
        net, T, s = self.net, self.net.T, self.net.dv
        sm = self.small
        s(dve.tensor_tensor(sm[:, 0:8], net.col("lb_raw", 0, 8), net.col("lb_raw", 0, 8), ALU.subtract))
        dve.sem_inc(self.s("lb_diff"), 1)
        dve.wait_ge(self.s("lb_exp"), 1)
        s(dve.reciprocal(sm[:, 16:24], sm[:, 8:16]))
        s(dve.tensor_tensor(sm[:, 16:24], sm[:, 16:24], sm[:, 8:16], ALU.mult))
        s(dve.tensor_tensor(sm[:, 24:32], sm[:, 16:24], sm[:, 16:24], ALU.subtract))
        s(dve.tensor_scalar(sm[:, 32:40], sm[:, 24:32], -1.0, 1.0, ALU.mult, ALU.add))
        for j in range(8):
            if j % 2 == 0:
                dve.wait_ge(self.s("sig_ready"), j // 2 + 1)
            s(dve.tensor_scalar(self.kT[:, j, :], self.kT[:, j, :], sm[:, 32 + j:33 + j], sm[:, 24 + j:25 + j],
                                ALU.mult, ALU.add))
        dve.sem_inc(self.s("f_ready"), 1)
        s(dve.memset(self.AT, 0.0))
        dve.wait_ge(self.s("log_ready"), 1)
        s(dve.tensor_scalar(self.kT, self.kT, -1.0, 1.0, ALU.mult, ALU.add))
        dve.sem_inc(self.s("k_ready"), 1)
        for h in range(HEADS):
            for i in range(NT):
                b = self.b[:, h, i * P:(i + 1) * P]
                s(dve.tensor_tensor_scan(b, net.ones[:, 0:P], b, 0.0, ALU.mult, ALU.add))
        dve.wait_ge(self.s("q_kept"), 4)
        dve.wait_ge(self.s("masks_loaded"), 16)

        def blocks_of(x, B):
            return x.rearrange("p h t -> p (h t)").rearrange("p (n s b) -> p n s b", s=2, b=B)

        def exponent(lv):
            M, B = self.M[(lv + 1) % 2], P if lv < 0 else LEVELS[lv]
            if lv >= 1:
                T.take(dve, ("hgrn_level", lv - 2, 3)) if lv >= 2 else T.take(dve, ("hgrn_cross", 1))
            m, b = blocks_of(M, B), blocks_of(self.b, B)
            n = 8 * SEQ // (2 * B)
            mid = b[:, :, 0, B - 1:B].to_broadcast([P, n, B])
            s(dve.tensor_tensor(m[:, :, 0, :], mid, b[:, :, 0, :], ALU.subtract))
            if lv < 0:
                s(dve.tensor_copy(m[:, :, 1, :], b[:, :, 1, :]))
            else:
                s(dve.tensor_tensor(m[:, :, 1, :], b[:, :, 1, :], mid, ALU.subtract))
            dve.sem_inc(self.s("e_ready"), 1)

        def keep_level(lv):
            mask = self.level_masks[:, lv if lv >= 0 else 7, :].bitcast(I32)
            for n in range(4):
                t = T.take(dve, ("hgrn_level", lv, n))
                s(dve.copy_predicated(self.AT[:, 4 * n:4 * n + 4, :], mask.unsqueeze(1).to_broadcast([P, 4, P]),
                                      t[:, :].rearrange("p (m t) -> p m t", m=4)))
                T.free(dve, ("hgrn_level", lv, n))

        exponent(-1)
        for lv in range(-1, len(LEVELS)):
            M, B = self.M[(lv + 1) % 2], P if lv < 0 else LEVELS[lv]
            if lv + 1 < len(LEVELS):
                exponent(lv + 1)
            dve.wait_ge(self.s("exp_ready"), lv + 2)
            m, k, q = blocks_of(M, B), blocks_of(self.kT, B), blocks_of(self.qT, B)
            s(dve.tensor_tensor(m[:, :, 0, :], m[:, :, 0, :], k[:, :, 0, :], ALU.mult))
            s(dve.tensor_tensor(m[:, :, 1, :], m[:, :, 1, :], q[:, :, 1, :], ALU.mult))
            dve.sem_inc(self.s("m_ready"), 1)
            if lv == -1:
                keep_level(-1)
            elif lv >= 1:
                keep_level(lv - 1)
        keep_level(len(LEVELS) - 1)
        dve.sem_inc(self.s("at_ready"), 1)
        self.rows_here(dve)
        for i in range(NT):
            for n in range(2):
                j = 2 * i + n
                dve.wait_ge(self.s("o_kept"), j + 1)
                o4 = self.o[:, i, n * 512:(n + 1) * 512].rearrange("p (h v) -> p h v", h=4)
                q4 = self.sq[:, i, n * 512:(n + 1) * 512].rearrange("p (h v) -> p h v", h=4)
                s(dve.tensor_tensor(q4, o4, o4, ALU.mult))
                s(dve.tensor_reduce(sm[:, 40 + 4 * j:44 + 4 * j], q4, AX, ALU.add))
                s(dve.tensor_scalar(sm[:, 40 + 4 * j:44 + 4 * j], sm[:, 40 + 4 * j:44 + 4 * j], 1.0 / P, RMS_EPS,
                                    ALU.mult, ALU.add))
                dve.sem_inc(self.s("mean"), 1)
        dve.wait_ge(self.s("g_kept"), 4)
        for i in range(NT):
            for n in range(2):
                j = 2 * i + n
                dve.wait_ge(self.s("rstd"), j + 1)
                o4 = self.o[:, i, n * 512:(n + 1) * 512].rearrange("p (h v) -> p h v", h=4)
                o1 = self.o[:, i, n * 512:(n + 1) * 512]
                s(dve.tensor_tensor(o4, o4, sm[:, 56 + 4 * j:60 + 4 * j].unsqueeze(2).to_broadcast([P, 4, P]), ALU.mult))
                s(dve.tensor_tensor(o1, o1, net.rows[:, 0, n * 512:(n + 1) * 512], ALU.mult))
                s(dve.tensor_tensor(o1, o1, self.g[:, i, n * 512:(n + 1) * 512], ALU.mult))
                dve.sem_inc(self.s("o_gated"), 1)
        self.vector_branch(dve, False)

    def gpsimd(self, pool):
        net, sm = self.net, self.small
        net.po(pool.memset(sm[:, 72:76], -0.5))
        for j in range(4):
            pool.wait_ge(self.s("mean"), j + 1)
            net.po(pool.tensor_tensor(sm[:, 56 + 4 * j:60 + 4 * j], sm[:, 40 + 4 * j:44 + 4 * j], sm[:, 72:76], ALU.pow))
            pool.sem_inc(self.s("rstd"), 1)


class Retention(Branch):
    tag = "ret"
    shared = {"branch": GATE_COUNTS}

    def __init__(self, net):
        self.net = net
        a = Arena(net.scratch)
        self.merged = self.take_merged()
        self.qT = a.take(8 * SEQ, 8, SEQ)
        self.kT = a.take(8 * SEQ, 8, SEQ)
        self.catT = Arena(net.scratch).take(16 * SEQ, 16, SEQ)
        self.vv = a.take(NT * 2048, NT, 2048)
        self.g = a.take(NT * 2048, NT, 2048)
        self.decay = a.take(4 * TRI, 4, TRI)
        self.AT = [a.take(TRI) for _ in range(2)]
        self.cos = a.take(SEQ)
        self.sin = a.take(SEQ)
        self.ta, self.tb = a.take(512), a.take(512)
        self.small = a.take(32)
        self.gate = [self.ta, self.tb]
        assert a.at <= SCRATCH - NT * D, a.at

    def tensor(self, pe):
        net, T = self.net, self.net.T
        for key in ("ret_q", "ret_k"):
            for b in range(2):
                net.product_T(pe, (key, b), net.xT)
        for b in range(4):
            net.product(pe, ("ret_v", b), net.xT)
        for b in range(4):
            net.product(pe, ("ret_g", b), net.xT)
        pe.wait_ge(self.s("rotated"), 8)
        for h in range(5):
            if h < 4:
                t = T.open(pe, ("ret_S", h))
                for i in range(NT):
                    for m in range(2):
                        out = t[:, 0:SEQ] if i == 0 else t[:, SEQ:TRI]
                        mm = pe.matmul(out, self.kT[:, 2 * h + m, i * P:(i + 1) * P], self.qT[:, 2 * h + m, i * P:SEQ],
                                       start=m == 0, stop=m == 1)
                T.close(("ret_S", h), mm)
            if h >= 1:
                g = h - 1
                pe.wait_ge(self.s("at_ready"), g + 1)
                pe.wait_ge(self.s("v_kept"), 8)
                A = self.AT[g % 2]
                for i in range(NT):
                    t = T.open(pe, ("ret_o", g, i))
                    vs = slice(512 * g, 512 * g + 512)
                    mm = pe.matmul(t[:, :], A[:, i * P:(i + 1) * P], self.vv[:, 0, vs], start=True, stop=i == 0)
                    if i:
                        mm = pe.matmul(t[:, :], A[:, SEQ:TRI], self.vv[:, 1, vs], start=False, stop=True)
                    T.close(("ret_o", g, i), mm)
        for i in range(NT):
            for n in range(4):
                pe.wait_ge(self.s("gated"), 8)
                t = T.open(pe, ("ret_oT", i, n))
                for m in range(4):
                    j = 4 * n + m
                    mm = pe.transpose(t[:, m * P:(m + 1) * P], self.g[:, i, j * P:(j + 1) * P], net.ident[:, :])
                T.close(("ret_oT", i, n), mm)
        pe.wait_ge(self.s("oT_kept"), 8)
        self.tensor_branch(pe, self.catT, kt=16)

    def scalar(self, act):
        net, T, s, io = self.net, self.net.T, self.net.ac, self.net.io
        act.dma_start(self.decay, io["decay"].rearrange("p (a b) -> p a b", a=4)).then_inc(self.s("tables_loaded"), 16)
        act.dma_start(self.cos, io["rotary"][0]).then_inc(self.s("tables_loaded"), 16)
        act.dma_start(self.sin, io["rotary"][1]).then_inc(self.s("tables_loaded"), 16)
        for b in range(4):
            for i in range(NT):
                t = T.take(act, (("ret_v", b), i))
                s(act.activation(self.vv[:, i, b * 512:(b + 1) * 512], t[:, :], ACT.Copy))
                T.free(act, (("ret_v", b), i))
                act.sem_inc(self.s("v_kept"), 1)
        for b in range(4):
            for i in range(NT):
                t = T.take(act, (("ret_g", b), i))
                s(act.activation(self.g[:, i, b * 512:(b + 1) * 512], t[:, :], ACT.Silu))
                T.free(act, (("ret_g", b), i))
        act.sem_inc(self.s("g_kept"), 1)
        for h in range(4):
            for i in range(NT):
                t = T.take(act, ("ret_o", h, i))
                j = 2 * h + i
                s(act.activation(self.ta, t[:, :], ACT.Square, accum_out=self.small[:, j:j + 1]))
                act.sem_inc(self.s("squares"), 1)
        for i in range(NT):
            for n in range(4):
                t = T.take(act, ("ret_oT", i, n))
                s(act.activation(self.catT[:, 4 * n:4 * n + 4, i * P:(i + 1) * P],
                                 t[:, :].rearrange("p (m t) -> p m t", m=4), ACT.Copy))
                T.free(act, ("ret_oT", i, n))
                act.sem_inc(self.s("oT_kept"), 1)
        self.scalar_branch(act)

    def vector(self, dve):
        net, T, s = self.net, self.net.T, self.net.dv
        dve.wait_ge(self.s("tables_loaded"), 48)
        cos = self.cos.unsqueeze(1).to_broadcast([P, 2, SEQ])
        sin = self.sin.unsqueeze(1).to_broadcast([P, 2, SEQ])
        for key, dst in (("ret_q", self.qT), ("ret_k", self.kT)):
            for h in range(4):
                key2 = ((key, h // 2), h % 2)
                t = T.take(dve, key2)
                pair = t[:, :].rearrange("p (m t) -> p m t", m=2)
                s(dve.tensor_tensor(self.ta.rearrange("p (m t) -> p m t", m=2), pair, cos, ALU.mult))
                s(dve.tensor_tensor(self.tb.rearrange("p (m t) -> p m t", m=2), pair, sin, ALU.mult))
                T.free(dve, key2)
                s(dve.tensor_tensor(dst[:, 2 * h, :], self.ta[:, 0:SEQ], self.tb[:, SEQ:], ALU.subtract))
                s(dve.tensor_tensor(dst[:, 2 * h + 1, :], self.ta[:, SEQ:], self.tb[:, 0:SEQ], ALU.add))
                dve.sem_inc(self.s("rotated"), 1)
        for h in range(5):
            if h < 4:
                t = T.take(dve, ("ret_S", h))
                if h >= 2:
                    T.take(dve, ("ret_o", h - 2, 1))
                s(dve.tensor_tensor(self.AT[h % 2], t[:, 0:TRI], self.decay[:, h, :], ALU.mult))
                T.free(dve, ("ret_S", h))
                dve.sem_inc(self.s("at_ready"), 1)
            if h >= 1:
                g = h - 1
                for i in range(NT):
                    j = 2 * g + i
                    dve.wait_ge(self.s("squares"), j + 1)
                    s(dve.tensor_scalar(self.small[:, 8 + j:9 + j], self.small[:, j:j + 1], 1.0 / 512, RMS_EPS,
                                        ALU.mult, ALU.add))
                    dve.sem_inc(self.s("mean"), 1)
                    if j == 0:
                        dve.wait_ge(self.s("g_kept"), 1)
                    dve.wait_ge(self.s("rstd"), j + 1)
                    t = T.take(dve, ("ret_o", g, i))
                    gs = self.g[:, i, 512 * g:512 * g + 512]
                    s(dve.scalar_tensor_tensor(gs, t[:, :], self.small[:, 16 + j:17 + j], gs, ALU.mult, ALU.mult))
                    T.free(dve, ("ret_o", g, i))
                    dve.sem_inc(self.s("gated"), 1)
        self.vector_branch(dve, False)

    def gpsimd(self, pool):
        net, sm = self.net, self.small
        net.po(pool.memset(sm[:, 24:25], -0.5))
        for j in range(8):
            pool.wait_ge(self.s("mean"), j + 1)
            net.po(pool.tensor_tensor(sm[:, 16 + j:17 + j], sm[:, 8 + j:9 + j], sm[:, 24:25], ALU.pow))
            pool.sem_inc(self.s("rstd"), 1)


class Merge(Phase):
    tag = "merge"

    def __init__(self, net):
        self.net = net
        a = Arena(net.scratch)
        self.merged = Branch.take_merged(self)
        self.mT = a.take(8 * SEQ, 8, SEQ)
        self.gt = a.take(D)
        self.tmp = a.take(512)

    def rows(self):
        return ("ada_gt1",)

    def tensor(self, pe):
        net, T = self.net, self.net.T
        for i in range(NT):
            for c in range(2):
                t = T.open(pe, ("merge_T", i, c))
                for k in range(4):
                    n0 = (4 * c + k) * P
                    mm = pe.transpose(t[:, k * P:(k + 1) * P], self.merged[:, i, n0:n0 + P], net.ident[:, :])
                T.close(("merge_T", i, c), mm)
        gate_rows(net, pe, "gt1")
        pe.wait_ge(self.s("mT_kept"), 4)
        for c in range(2):
            net.product(pe, ("merge_out", c), self.mT)

    def scalar(self, act):
        net, T = self.net, self.net.T
        for i in range(NT):
            for c in range(2):
                t = T.take(act, ("merge_T", i, c))
                net.ac(act.activation(self.mT[:, 4 * c:4 * c + 4, i * P:(i + 1) * P],
                                      t[:, :].rearrange("p (k t) -> p k t", k=4), ACT.Copy))
                T.free(act, ("merge_T", i, c))
                act.sem_inc(self.s("mT_kept"), 1)

    def vector(self, dve):
        net, T, s = self.net, self.net.T, self.net.dv
        self.rows_here(dve)
        keep_gate_rows(net, dve, "gt1", self.gt)
        for c in range(2):
            for i in range(NT):
                key = (("merge_out", c), i)
                t = T.take(dve, key)
                xs = net.x[:, i, c * 512:(c + 1) * 512]
                s(dve.tensor_tensor(self.tmp, t[:, :], self.gt[:, c * 512:(c + 1) * 512], ALU.mult))
                s(dve.tensor_tensor(xs, xs, self.tmp, ALU.add))
                T.free(dve, key)


def exp_columns(net, dve, out, x, n, r, bits):
    s = net.dv
    s(dve.tensor_scalar(n, x, 1.0 / math.log(2.0), ROUND, ALU.mult, ALU.add))
    s(dve.tensor_scalar(n, n, ROUND, 127.0, ALU.subtract, ALU.min))
    s(dve.tensor_scalar(n, n, -127.0, None, ALU.max))
    s(dve.scalar_tensor_tensor(r, n, -0.693359375, x, ALU.mult, ALU.add))
    s(dve.scalar_tensor_tensor(r, n, 2.12194440e-4, r, ALU.mult, ALU.add))
    s(dve.tensor_scalar(r, r, 0.5, -0.5, ALU.min, ALU.max))
    s(dve.tensor_scalar(bits.bitcast(I32), n, 8388608.0, 1065353216.0, ALU.mult, ALU.add))
    s(dve.tensor_scalar(n, r, 1.0 / 5040, None, ALU.mult))
    for c in (1.0 / 720, 1.0 / 120, 1.0 / 24, 1.0 / 6, 0.5, 1.0):
        s(dve.scalar_tensor_tensor(n, n, c, r, ALU.add, ALU.mult))
    s(dve.scalar_tensor_tensor(out, n, 1.0, bits, ALU.add, ALU.mult))


def sin_cos_columns(net, dve, sin, cos, x, p, y2, v):
    s = net.dv
    s(dve.tensor_scalar(x, x, 0.125, None, ALU.mult))
    s(dve.tensor_tensor(y2, x, x, ALU.mult))
    s(dve.tensor_scalar(p, y2, 1.0 / 362880, None, ALU.mult))
    for c in (-1.0 / 5040, 1.0 / 120, -1.0 / 6):
        s(dve.scalar_tensor_tensor(p, p, c, y2, ALU.add, ALU.mult))
    s(dve.scalar_tensor_tensor(sin, p, 1.0, x, ALU.add, ALU.mult))
    s(dve.tensor_scalar(v, y2, 1.0 / 3628800, None, ALU.mult))
    for c in (-1.0 / 40320, 1.0 / 720, -1.0 / 24, 0.5):
        s(dve.scalar_tensor_tensor(v, v, c, y2, ALU.add, ALU.mult))
    for _ in range(3):
        s(dve.tensor_scalar(cos, v, -1.0, 1.0, ALU.mult, ALU.add))
        s(dve.scalar_tensor_tensor(v, sin, 2.0, sin, ALU.mult, ALU.mult))
        s(dve.scalar_tensor_tensor(sin, sin, 2.0, cos, ALU.mult, ALU.mult))
    s(dve.tensor_scalar(cos, v, -1.0, 1.0, ALU.mult, ALU.add))


class Loop:

    def __init__(self, first, turns, release):
        self.first, self.turns, self.release = first, turns, release


class Mixture(Phase):

    def __init__(self, net, n):
        self.net, self.n, self.tag = net, n, f"moe{n}"
        self.G, self.E = ROUTES[n]
        self.experts = self.G * self.E
        self.F = MOE2_F if n == 2 else MOE1_F
        self.ft = self.F // P
        self.per_gate = KT * self.F // UNIT
        self.body = SLOTS // (3 * self.per_gate)
        self.turns = self.experts // self.body
        self.shared = {"moe": {"group_max": NT, "second_max": NT, "route_exps": NT, "comb_ready": 1,
                               "cb_kept": self.experts // 2, "down_done": 2 + self.experts,
                               "hid_ready": self.experts * self.ft, "silu_ready": self.experts * self.ft}}
        a = Arena(net.scratch)
        self.cb = a.take(self.experts * SEQ, self.experts, SEQ)
        self.hid = [a.take(self.ft * SEQ, self.ft, SEQ) for _ in range(2)]
        self.silu = [a.take(SEQ) for _ in range(2)]
        self.up = [a.take(SEQ) for _ in range(2)]
        n_l = self.G + self.experts
        self.L = a.take(NT * n_l, NT, n_l)
        self.comb = a.take(NT * self.experts, NT, self.experts)
        self.r = a.take(NT * 80, NT, 80)
        self.tmp = a.take(D) if n == 2 else None
        self.gt = a.take(D) if n == 2 else None

    def tensor(self, pe):
        net, T = self.net, self.net.T
        net.small_rows(pe, (self.tag, "route"), f"route{self.n}", net.xT)
        if self.n == 2:
            gate_rows(net, pe, "gt2")
        pe.wait_ge(self.s("comb_ready"), self.base("comb_ready") + 1)
        for e in range(0, self.experts, 2):
            t = T.open(pe, (self.tag, "cb", e))
            for m in range(2):
                for i in range(NT):
                    at = m * SEQ + i * P
                    mm = pe.matmul(t[:, at:at + P], self.comb[:, i, e + m:e + m + 1].to_broadcast([P, P]),
                                   net.ident[:, :], start=True, stop=True)
            T.close((self.tag, "cb", e), mm)
        self.acc = []
        for b in range(4):
            t = T.open(pe, (self.tag, "acc", b), (b,))
            self.acc.append(t)
            mm = pe.matmul(t[:, :], net.zeros[:, 0:P], net.zeros[:, :], start=True, stop=False, skip_group_check=True)
            if b >= 2:
                mm.then_inc(self.s("down_done"), 1)
        f_jobs = self.body * self.ft
        first = net.unit
        base = [T.uses[4], T.uses[5]]
        assert min(base) > 0
        self.bank_base = base
        loaded = [(net.sem(f"slot{(first + j) % SLOTS}_loaded"), (first + j) // SLOTS + 1) for j in range(SLOTS)]
        pg = self.per_gate
        with pe.Fori(0, self.turns) as turn:
            for e in range(self.body):
                u = [net.slot(first + e * 3 * pg + j) for j in range(3 * pg)]
                kper = KT // pg
                for j in range(2 * pg):
                    sem, v = loaded[e * 3 * pg + j]
                    pe.wait_ge(sem, (turn + v) * 16)
                for f in range(self.ft):
                    job = e * self.ft + f
                    b = job % 2
                    pe.wait_ge(T.freed[4 + b], turn * (f_jobs // 2) + (base[b] + job // 2))
                    t = T.bank[4 + b]
                    for m in range(2):
                        for k in range(KT):
                            w = u[m * pg + k // kper].rearrange("p (k n) -> p k n", k=kper)
                            mm = pe.matmul(t[:, m * SEQ:(m + 1) * SEQ], w[:, k % kper, f * P:(f + 1) * P],
                                           net.xT[:, k, :], start=k == 0, stop=k == KT - 1)
                    mm.then_inc(T.ready[4 + b], 1)
                for j in range(2 * pg, 3 * pg):
                    sem, v = loaded[e * 3 * pg + j]
                    pe.wait_ge(sem, (turn + v) * 16)
                for f in range(self.ft):
                    pe.wait_ge(self.s("hid_ready"), turn * f_jobs + (self.base("hid_ready") + e * self.ft + f + 1))
                    w = u[2 * pg + f // 2].rearrange("p (k n) -> p k n", k=2)
                    for i in range(NT):
                        for c in range(2):
                            mm = pe.matmul(self.acc[2 * i + c][:, :], self.hid[e % 2][:, f, i * P:(i + 1) * P],
                                           w[:, f % 2, c * 512:(c + 1) * 512], start=False, stop=False,
                                           skip_group_check=True)
                mm.then_inc(self.s("down_done"), 1)
        for b in range(2):
            T.uses[4 + b] += self.turns * f_jobs // 2
        for b in range(4):
            mm = pe.matmul(self.acc[b][:, :], net.zeros[:, 0:P], net.zeros[:, :], start=False, stop=True,
                           skip_group_check=True)
            T.close((self.tag, "acc", b), mm)
        release = []
        for e in range(self.body):
            job = (e + 1) * self.ft - 1
            release += [(T.ready[4 + job % 2], base[job % 2] + job // 2 + 1, f_jobs // 2)] * (2 * pg)
            release += [(self.s("down_done"), self.base("down_done") + 2 + e + 1, self.body)] * pg
        net.loops.append(Loop(first, self.turns, release))
        net.unit += SLOTS * self.turns
        for j, (sem, v, per) in enumerate(release):
            net.released[first + SLOTS * (self.turns - 1) + j] = (sem, v + per * (self.turns - 1))

    def rows(self):
        return ("ada_gt2",) if self.n == 2 else ()

    def first_of(self, out, vals, idx, tmp):
        dve, s = self.net.dv.eng, self.net.dv
        s(dve.tensor_scalar(out, vals, tmp[:, 0:1], None, ALU.is_equal))
        s(dve.tensor_tensor(out, out, idx, ALU.mult))
        s(dve.tensor_reduce(tmp[:, 1:2], out, AX, ALU.min))
        s(dve.tensor_scalar(out, out, tmp[:, 1:2], None, ALU.is_equal))

    def vector(self, dve):
        net, T, s = self.net, self.net.T, self.net.dv
        G, E, n = self.G, self.E, self.G + self.experts
        t = T.take(dve, (self.tag, "route"))
        if self.n == 2:
            self.rows_here(dve)
        at = ROUTE_BIAS[self.n]
        for i in range(NT):
            L, r = self.L[:, i, :], self.r[:, i, :]
            s(dve.tensor_tensor(L, t[:, i * n:(i + 1) * n], net.bias_row[:, at:at + n], ALU.add))
            s(dve.tensor_reduce(r[:, 0:1], L[:, 0:G], AX, ALU.max))
            s(dve.tensor_scalar(r[:, 2:3], r[:, 0:1], -1.0, None, ALU.mult))
            dve.sem_inc(self.s("group_max"), 1)
            oh_g = r[:, 16:16 + G]
            self.first_of(oh_g, L[:, 0:G], net.bias_row[:, 76:76 + G], r[:, 0:2])
            prod = self.comb[:, i, :].rearrange("p (g e) -> p g e", g=G)
            s(dve.tensor_tensor(prod, L[:, G:].rearrange("p (g e) -> p g e", g=G),
                                oh_g.unsqueeze(2).to_broadcast([P, G, E]), ALU.mult))
            es = r[:, 24:24 + E]
            s(dve.tensor_reduce(es, prod.rearrange("p g e -> p e g"), AX, ALU.add))
            s(dve.tensor_reduce(r[:, 4:5], es, AX, ALU.max))
            s(dve.tensor_scalar(r[:, 6:7], r[:, 4:5], -1.0, None, ALU.mult))
            self.first_of(r[:, 32:32 + E], es, net.bias_row[:, 76:76 + E], r[:, 4:6])
            s(dve.scalar_tensor_tensor(es, r[:, 32:32 + E], MASKED, es, ALU.mult, ALU.add))
            s(dve.tensor_reduce(r[:, 8:9], es, AX, ALU.max))
            dve.sem_inc(self.s("second_max"), 1)
            self.first_of(r[:, 40:40 + E], es, net.bias_row[:, 76:76 + E], r[:, 8:10])
        T.free(dve, (self.tag, "route"))
        for i in range(NT):
            r = self.r[:, i, :]
            dve.wait_ge(self.s("route_exps"), self.base("route_exps") + i + 1)
            s(dve.reciprocal(r[:, 12:13], r[:, 11:12]))
            s(dve.tensor_scalar(r[:, 13:14], r[:, 10:11], 1.0, None, ALU.add))
            s(dve.reciprocal(r[:, 13:14], r[:, 13:14]))
            s(dve.tensor_tensor(r[:, 12:13], r[:, 12:13], r[:, 13:14], ALU.mult))
            s(dve.scalar_tensor_tensor(r[:, 48:48 + E], r[:, 40:40 + E], r[:, 10:11], r[:, 32:32 + E], ALU.mult, ALU.add))
            s(dve.tensor_scalar(r[:, 48:48 + E], r[:, 48:48 + E], r[:, 12:13], None, ALU.mult))
            s(dve.tensor_tensor(self.comb[:, i, :].rearrange("p (g e) -> p g e", g=G),
                                r[:, 16:16 + G].unsqueeze(2).to_broadcast([P, G, E]),
                                r[:, 48:48 + E].unsqueeze(1).to_broadcast([P, G, E]), ALU.mult))
        dve.sem_inc(self.s("comb_ready"), 1)
        if self.n == 2:
            keep_gate_rows(net, dve, "gt2", self.gt)
        f_jobs = self.body * self.ft
        dve.wait_ge(self.s("cb_kept"), self.base("cb_kept") + self.experts // 2)
        with dve.Fori(0, self.turns) as turn:
            for e in range(self.body):
                dve.wait_ge(self.s("down_done"), turn * self.body + (self.base("down_done") + e + 1))
                for f in range(self.ft):
                    job = e * self.ft + f
                    b, k = job % 2, job // 2
                    dve.wait_ge(self.s("silu_ready"), turn * f_jobs + (self.base("silu_ready") + job + 1))
                    dve.tensor_tensor(self.up[b], self.silu[b], T.bank[4 + b][:, SEQ:2 * SEQ], ALU.mult)\
                       .then_inc(T.freed[4 + b], 1)
                    dve.wait_ge(T.freed[4 + b], turn * (f_jobs // 2) + (self.bank_base[b] + k + 1))
                    dve.tensor_tensor(self.hid[e % 2][:, f, :], self.up[b],
                                      self.cb[:, bass.ds(turn * self.body + e, 1), :].rearrange("p o t -> p (o t)"),
                                      ALU.mult).then_inc(self.s("hid_ready"), 1)
        for i in range(NT):
            for c in range(2):
                t = T.take(dve, (self.tag, "acc", 2 * i + c))
                xs = net.x[:, i, c * 512:(c + 1) * 512]
                if self.n == 2:
                    tmp = self.tmp[:, 0:512]
                    s(dve.tensor_tensor(tmp, t[:, :], self.gt[:, c * 512:(c + 1) * 512], ALU.mult))
                    s(dve.tensor_tensor(xs, xs, tmp, ALU.add))
                else:
                    s(dve.scalar_tensor_tensor(xs, xs, ALPHA, t[:, :], ALU.mult, ALU.add))
                T.free(dve, (self.tag, "acc", 2 * i + c))

    def scalar(self, act):
        net, T, s = self.net, self.net.T, self.net.ac
        for i in range(NT):
            L, r = self.L[:, i, :], self.r[:, i, :]
            act.wait_ge(self.s("group_max"), self.base("group_max") + i + 1)
            s(act.activation(r[:, 56:56 + self.G], L[:, 0:self.G], ACT.Exp, bias=r[:, 2:3], accum_out=r[:, 11:12]))
            act.wait_ge(self.s("second_max"), self.base("second_max") + i + 1)
            s(act.activation(r[:, 10:11], r[:, 8:9], ACT.Exp, bias=r[:, 6:7]))
            act.sem_inc(self.s("route_exps"), 1)
        for e in range(0, self.experts, 2):
            t = T.take(act, (self.tag, "cb", e))
            s(act.activation(self.cb[:, e:e + 2, :], t[:, :].rearrange("p (e t) -> p e t", e=2), ACT.Copy))
            T.free(act, (self.tag, "cb", e))
            act.sem_inc(self.s("cb_kept"), 1)
        f_jobs = self.body * self.ft
        with act.Fori(0, self.turns) as turn:
            for job in range(f_jobs):
                b = job % 2
                act.wait_ge(T.ready[4 + b], turn * (f_jobs // 2) + (self.bank_base[b] + job // 2 + 1))
                act.activation(self.silu[b], T.bank[4 + b][:, 0:SEQ], ACT.Silu).then_inc(self.s("silu_ready"), 1)

    def gpsimd(self, pool):
        pass


def log_sigmoid_front(net, dve, x, out):
    net.dv(dve.scalar_tensor_tensor(out, x, -1.0, x, ALU.mult, ALU.min))


PHASES = [(Start, ()), (Fox, ()), (LayerNorm, (0,)), (Mixture, (0,)), (LayerNorm, (1,)), (Mlstm, ()),
          (LayerNorm, (2,)), (Mixture, (1,)), (LayerNorm, (3,)), (Modulation, ()), (RmsNorm, (0,)), (Indexed, ()),
          (Hgrn, ()), (Retention, ()), (Merge, ()), (RmsNorm, (1,)), (Mixture, (2,)), (RmsNorm, (2,))]


def stream_weights(net, sp, stream, total):
    u = 0
    loops = list(net.loops)

    def load(v):
        if v >= SLOTS:
            sp.wait_ge(*net.released[v - SLOTS])
        sp.dma_start(net.slot(v), stream[v]).then_inc(net.sem(f"slot{v % SLOTS}_loaded"), 16)

    while u < total:
        if loops and u == loops[0].first + SLOTS:
            loop = loops.pop(0)
            with sp.Fori(1, loop.turns) as turn:
                for j in range(SLOTS):
                    sem, base, per = loop.release[j]
                    sp.wait_ge(sem, base + (turn - 1) * per)
                    at = net.slot(loop.first + j)
                    sp.dma_start(at, stream[bass.ds(turn * SLOTS + (loop.first + j), 1)].rearrange("o p n -> p (o n)"))\
                      .then_inc(net.sem(f"slot{(loop.first + j) % SLOTS}_loaded"), 16)
            u = loop.first + SLOTS * loop.turns
        else:
            load(u)
            u += 1


def program(nc, io, phase_list, total_units):
    with ExitStack() as ctx:
        net = Net(nc, ctx, io, phase_list)
        phases = net.phase_objects = [cls(net, *args) for cls, args in phase_list]
        net.rows_at, n = {}, 0
        for ph in phases:
            n += 16 * len(ph.rows())
            net.rows_at[ph.tag] = n
        net.dv = net.ac = net.po = None
        block = ctx.enter_context(nc.Block())

        @block.tensor
        def _(pe):
            for ph in phases:
                ph.tensor(pe)
                net.join(pe, "tensor")

        @block.vector
        def _(dve):
            net.dv = Steps(dve, net.sem("vector_steps"))
            for ph in phases:
                ph.vector(dve)
                net.join(dve, "vector")

        @block.scalar
        def _(act):
            net.ac = Steps(act, net.sem("scalar_steps"))
            for ph in phases:
                for r, name in enumerate(ph.rows()):
                    act.dma_start(net.rows[:, r, :], io["rows"][ROWS.index(name)].partition_broadcast(P))\
                       .then_inc(net.sem("row_loaded"), 16)
                ph.scalar(act)
                net.join(act, "scalar")
            act.dma_start(io["out"].rearrange("(i p) d -> p i d", p=P), net.x).then_inc(net.sem("out_stored"), 16)
            act.wait_ge(net.sem("out_stored"), 16)

        @block.gpsimd
        def _(pool):
            net.po = Steps(pool, net.sem("gpsimd_steps"))
            for ph in phases:
                ph.gpsimd(pool)
                net.join(pool, "gpsimd")

        @block.sync
        def _(sp):
            stream_weights(net, sp, io["stream"], total_units)
        print("semaphores", len(net.sems) + 16, "units", net.unit) if DEBUG else None


DEBUG = False


def tiles(w, rows, n0, n1):
    part = w[rows[0]:rows[1], n0:n1]
    return part.reshape(-1, P, n1 - n0).transpose(1, 0, 2).reshape(P, -1)


def blocks(w, n0, n1):
    return [tiles(w, (r, r + 512), c, c + 512) for c in range(n0, n1, 512) for r in range(0, w.shape[0], 512)]


def column(v, n):
    return v.reshape(n, P).T


def place(v):
    out = np.zeros((P, 1), v.dtype)
    out[:v.shape[0], 0] = v
    return out


def constants():
    q, k = np.arange(P)[:, None], np.arange(P)[None, :]
    diag = np.where(k <= q, 0.0, MASKED).astype(np.float32)
    out = {"ident": np.eye(P, dtype=np.float32),
           "causal": np.concatenate([diag, np.zeros((P, P), np.float32), diag], 1)}
    sel = np.zeros((8, 8, P), np.float32)
    for h in range(8):
        sel[h, h] = 1.0
    out["sel"] = sel.reshape(8, 8 * P)
    out["flip"] = np.ascontiguousarray(np.eye(P, dtype=np.float32)[::-1])
    rel = np.maximum(SEQ - 1 - np.arange(TRI), 0)
    relf = np.maximum(rel, 1).astype(np.float32)
    large = 16 + (np.log(relf / np.float32(16)) / np.float32(math.log(8)) * np.float32(16)).astype(np.int32)
    bucket = np.where(rel < 16, rel, np.minimum(large, 31))
    out["buckets"] = (np.arange(32)[:, None] == bucket[None, :]).astype(np.float32)
    s, t = np.arange(P)[:, None], np.arange(P)[None, :]
    masks = [(s // (2 * b) == t // (2 * b)) & (s // b % 2 == 0) & (t // b % 2 == 1) for b in LEVELS] + [s == t]
    out["level_masks"] = np.concatenate([m.astype(np.int32) for m in masks], 1)
    decay = []
    for h in range(4):
        g = math.log(1.0 - 2.0 ** (-5.0 - h))
        d0 = np.where(t >= s, np.exp((t - s) * g), 0.0) / 16
        d1 = np.exp((t - s + P) * g) / 16
        decay += [d0, d1, d0]
    out["decay"] = np.concatenate(decay, 1).astype(np.float32)
    theta = (1.0 / (np.float32(10000.0) ** np.linspace(0.0, 1.0, P, dtype=np.float32))).astype(np.float32)
    angle = (theta[:, None] * np.arange(SEQ, dtype=np.float32)[None, :]).astype(np.float32)
    out["rotary"] = np.stack([np.cos(angle.astype(np.float64)), np.sin(angle.astype(np.float64))]).astype(np.float32)
    return out


def streams(i):
    s = []
    w = i["even_w_in"][0]
    u = w[:, 1544:2056]
    s += blocks(u, 0, 512) + blocks(w, 0, 1536) + blocks(i["s5_w_glu"][0], 0, 512) + blocks(i["even_w_out"][0], 0, 1024)
    s += experts(i["moe_w_gate"][0], i["moe_w_up"][0], i["moe_w_down"][0])
    w = i["odd_w_in"][0]
    s += blocks(w, 0, 4096) + blocks(i["odd_w_out"][0], 0, 1024)
    s += experts(i["moe_w_gate"][1], i["moe_w_up"][1], i["moe_w_down"][1])
    return s + streams2(i)


def streams2(i):
    ada, w = i["ada_w_2"][0], i["w_in_2"][0]
    at, parts = 0, {}
    for name, n in (("aq", 1024), ("ak", 1024), ("av", 1024), ("iq", 512), ("ik", 64), ("iw", 8), ("bq", 1024),
                    ("bf", 1024), ("bi", 1024), ("bg", 1024), ("cq", 1024), ("ck", 1024), ("cv", 2048), ("cg", 2048),
                    ("ga", 1024), ("gb", 1024), ("gc", 1024)):
        parts[name] = w[:, at:at + n]
        at += n
    whole = lambda m: blocks(m, 0, m.shape[1])
    s = blocks(ada, 0, 2048) + blocks(ada, 3072, 5120)
    ik = np.concatenate([parts["ik"], parts["ik"]], 1)
    s += [np.concatenate([tiles(ik, (0, D), 0, P), np.zeros((P, UNIT - D), np.float32)], 1)]
    s += whole(parts["iq"]) + whole(parts["aq"]) + whole(parts["ak"]) + whole(parts["av"])
    s += branch(parts["ga"], i["w_branch_a_2"][0])
    s += whole(parts["bf"]) + whole(parts["bq"]) + whole(parts["bi"]) + whole(parts["bg"])
    s += branch(parts["gb"], i["w_branch_b_2"][0])
    for n in ("cq", "ck"):
        m = parts[n].reshape(D, 4, P, 2).transpose(0, 1, 3, 2).reshape(D, D)
        s += whole(m)
    s += whole(parts["cv"]) + whole(parts["cg"]) + branch(parts["gc"], i["w_branch_c_2"][0])
    s += blocks(ada, 2048, 3072) + whole(i["w_out_2"][0])
    s += blocks(ada, 5120, 6144) + experts(i["expert_w_gate_2"][0], i["expert_w_up_2"][0], i["expert_w_down_2"][0])
    return s


def branch(gate, out):
    return [u for c in (0, 512) for w in (gate, out) for u in blocks(w, c, c + 512)]


def experts(gate, up, down):
    s = []
    for e in range(gate.shape[0]):
        rows = UNIT // gate.shape[2] * P
        for w in (gate[e], up[e]):
            s += [tiles(w, (r, r + rows), 0, w.shape[1]) for r in range(0, D, rows)]
        s += [tiles(down[e], (r, r + 256), 0, D) for r in range(0, down.shape[1], 256)]
    return s


def layout(i):
    c = constants()
    ew, ow = i["even_w_in"][0], i["odd_w_in"][0]
    w2 = i["w_in_2"][0]
    small = {"fox_f": ew[:, 1536:1544], "mlstm_i": ow[:, 4096:4104], "mlstm_f": ow[:, 4104:4112],
             "idx_w": w2[:, 3648:3656],
             "route2": np.concatenate([i["router_group_w_2"][0], i["router_expert_w_2"][0]], 1)}
    for n in range(2):
        e = i["moe_w_expert"][n].transpose(1, 0, 2).reshape(D, 16)
        small[f"route{n}"] = np.concatenate([i["moe_w_group"][n], e], 1)
    cols = {"b_glu": column(i["s5_b_glu"][0], 4), "s5_d": column(i["s5_d"][0].reshape(-1), 4),
            "a_re": column(i["s5_a_re"][0].reshape(-1), 16), "a_im": column(i["s5_a_im"][0].reshape(-1), 16),
            "log_dt": column(np.repeat(i["s5_log_dt"][0], 64), 16),
            "fox_f_bias": place(i["fox_f_bias"][0]), "mlstm_i_bias": place(i["mlstm_i_bias"][0]),
            "mlstm_f_bias": place(i["mlstm_f_bias"][0]), "conv_b": column(i["mlstm_conv_b"][0], 16),
            "conv_w": np.concatenate([column(i["mlstm_conv_w"][0][t], 16) for t in range(4)], 1),
            "ada_b": column(np.concatenate([i["ada_b_2"][0][0:2048], i["ada_b_2"][0][3072:5120]]), 32),
            "norm1_g": column(i["norm1_g_2"][0], 8), "norm2_g": column(i["norm2_g_2"][0], 8),
            "c": column(i["c_2"][0], 8), "lb_raw": column(i["hgrn_lb_raw_2"][0], 8)}
    b = [np.zeros((P, 4, P), np.float32) for _ in range(2)]
    cc = [np.zeros((P, 16, 32), np.float32) for _ in range(2)]
    for part, (bn, cn) in enumerate((("s5_b_re", "s5_c_re"), ("s5_b_im", "s5_c_im"))):
        for g in range(32):
            j, odd = g // 2, g % 2
            r = 32 * (j % 4) + 16 * odd
            b[part][r:r + 16, j // 4, 64 * odd:64 * odd + 64] = i[bn][0, g].T
            cc[part][64 * odd:64 * odd + 64, j, 16 * odd:16 * odd + 16] = i[cn][0, g].T
    rows = [v for n in range(4) for v in (i["ln_g"][n // 2, n % 2], i["ln_b"][n // 2, n % 2])]
    rows += [i["final_norm_g_2"], i["ada_b_2"][0][2048:3072], i["ada_b_2"][0][5120:6144], np.concatenate([i["hgrn_norm_g_2"][0]] * 8)]
    bias = np.concatenate([i["moe_b_group"][0], i["moe_b_expert"][0].reshape(-1), i["moe_b_group"][1],
                           i["moe_b_expert"][1].reshape(-1), i["router_group_b_2"][0], i["router_expert_b_2"][0],
                           np.arange(-100, -92, dtype=np.float32)])
    x = i["x"][0]
    c.update(x=x, xT=x.T, small=np.concatenate([small[n] for n in SMALL], 1),
             cols=np.concatenate([cols[n] for n in COLS], 1),
             bias_row=bias, s5_b=np.stack(b).reshape(2, P, 512), s5_c=np.stack(cc).reshape(2, P, 512),
             rows=np.stack(rows), rel_bias=i["rel_bias_2"], stream=np.stack(streams(i)))
    return {n: np.ascontiguousarray(a) for n, a in c.items()}


def kernel(**inputs):
    import concourse.bacc as bacc
    from concourse.bass_utils import run_bass_kernel_spmd

    nc = bacc.Bacc("TRN2", target_bir_lowering=False, num_devices=1)
    arrays = layout({n: np.asarray(a) for n, a in inputs.items()})
    io = {n: nc.dram_tensor(n, a.shape, mybir.dt.from_np(a.dtype), kind="ExternalInput").ap() for n, a in arrays.items()}
    io["bias_by_distance"] = nc.dram_tensor("bias_by_distance", (8, TRI), F32, kind="Internal").ap()
    io["out"] = nc.dram_tensor("out", (SEQ, D), F32, kind="ExternalOutput").ap()
    program(nc, io, PHASES, arrays["stream"].shape[0])
    got = run_bass_kernel_spmd(nc, [arrays], core_ids=[0])
    return got.results[0]["out"].reshape(1, SEQ, D)
```

```python
import math
from contextlib import ExitStack

import numpy as np

import concourse.bass as bass
from concourse import mybir
from concourse.alu_op_type import AluOpType as ALU

ACT = mybir.ActivationFunctionType
F32 = mybir.dt.float32
I32 = mybir.dt.int32
AX = mybir.AxisListType.X

P = 128
SEQ = 256
D = 1024
KT = D // P
NT = SEQ // P
HEADS = 8
UNIT = 2048
SLOTS = 12
BANKS = 8
SCRATCH = 19900
ALPHA = 4 ** 0.25
LN_EPS = 1e-5
RMS_EPS = 1e-6
MASKED = -1e30
TAKEN = -3e38
PAIRS = 2 * SEQ
TILE = 64
MAX_TILES = SEQ // TILE
WIDE = PAIRS + SEQ
ROUND = 12582912.0
TWO_PI_HI, TWO_PI_MID, TWO_PI_LO = 6.28125, 0.0019350051879882812, 3.0198e-07
MOE1_E, MOE1_F = 16, 256
MOE2_E, MOE2_F = 32, 512
TOPK = 64
TRI = 3 * P
LEVELS = (64, 32, 16, 8, 4, 2, 1)

SMALL = {}
for _name, _n in (("fox_f", 8), ("route0", 20), ("mlstm_i", 8), ("mlstm_f", 8), ("route1", 20), ("idx_w", 8),
                  ("route2", 36)):
    SMALL[_name] = (sum(n for _, n in SMALL.values()), _n)
N_SMALL = sum(n for _, n in SMALL.values())
COLS = {}
for _name, _n in (("b_glu", 4), ("s5_d", 4), ("a_re", 16), ("a_im", 16), ("log_dt", 16), ("fox_f_bias", 1),
                  ("mlstm_i_bias", 1), ("mlstm_f_bias", 1), ("conv_b", 16), ("conv_w", 64), ("ada_b", 32),
                  ("norm1_g", 8), ("norm2_g", 8), ("c", 8), ("lb_raw", 8)):
    COLS[_name] = (sum(n for _, n in COLS.values()), _n)
N_COLS = sum(n for _, n in COLS.values())
ROUTES = ((4, 4), (4, 4), (4, 8))
ROUTE_BIAS = (0, 20, 40)
ROWS = ("ln_g0", "ln_b0", "ln_g1", "ln_b1", "ln_g2", "ln_b2", "ln_g3", "ln_b3", "final_g", "ada_gt1", "ada_gt2",
        "hgrn_g", "iota")


class Steps:

    def __init__(self, eng, sem):
        self.eng, self.sem, self.n = eng, sem, 0

    def __call__(self, ins):
        ins.then_inc(self.sem, 1)
        self.n += 1
        self.eng.wait_ge(self.sem, self.n)


class PsumTiles:

    def __init__(self, ctx, nc):
        self.bank = [ctx.enter_context(nc.psum_tensor(f"bank{b}", [P, 512], F32)) for b in range(BANKS)]
        self.ready = [ctx.enter_context(nc.semaphore(f"bank{b}_ready")) for b in range(BANKS)]
        self.freed = [ctx.enter_context(nc.semaphore(f"bank{b}_freed")) for b in range(BANKS)]
        self.uses = [0] * BANKS
        self.jobs = {}
        self.turn = 0

    def open(self, pe, key, banks=range(BANKS)):
        b = banks[self.turn % len(banks)]
        self.turn += 1
        if self.uses[b]:
            pe.wait_ge(self.freed[b], self.uses[b])
        self.jobs[key] = (b, self.uses[b])
        self.uses[b] += 1
        return self.bank[b]

    def close(self, key, ins):
        ins.then_inc(self.ready[self.jobs[key][0]], 1)

    def take(self, eng, key):
        b, k = self.jobs[key]
        eng.wait_ge(self.ready[b], k + 1)
        return self.bank[b]

    def free(self, eng, key):
        eng.sem_inc(self.freed[self.jobs[key][0]], 1)


class Arena:

    def __init__(self, mem, at=0):
        self.mem, self.at = mem, at

    def take(self, n, *shape, rows=P):
        v = self.mem[0:rows, self.at:self.at + n]
        self.at += n
        assert self.at <= self.mem.shape[1], self.at
        if len(shape) == 2:
            v = v.rearrange("p (a b) -> p a b", a=shape[0], b=shape[1])
        elif len(shape) == 3:
            v = v.rearrange("p (a b c) -> p a b c", a=shape[0], b=shape[1], c=shape[2])
        return v


class Net:
    def __init__(self, nc, ctx, io, phases):
        self.nc, self.io = nc, io
        self.ctx = ctx
        self.sems = {}
        self.T = PsumTiles(ctx, nc)
        sb = lambda name, n, rows=P, dt=F32: ctx.enter_context(nc.sbuf_tensor(name + "_sb", [rows, n], dt))
        self.ring = sb("ring", SLOTS * UNIT)
        self.x = sb("x", NT * D)[:, :].rearrange("p (i d) -> p i d", i=NT)
        self.xT = sb("xT", KT * SEQ)[:, :].rearrange("p (k t) -> p k t", k=KT)
        self.small = sb("small", KT * N_SMALL)[:, :].rearrange("p (k n) -> p k n", k=KT)
        self.cols = sb("cols", N_COLS)
        self.ident = sb("ident", P)
        self.causal = sb("causal", TRI)
        self.bias_row = sb("bias_row", 84)
        self.rows = sb("rows", 2 * D)[:, :].rearrange("p (r d) -> p r d", r=2)
        self.stat = sb("stat", 64)
        self.ones = sb("ones", 256)
        self.mod = sb("mod", 40)
        self.zeros = sb("zeros", 512)
        self.scratch = sb("scratch", SCRATCH)
        self.unit = 0
        self.released = {}
        self.loops = []
        self.n_ended = {}
        self.n_rows = 0

    def sem(self, name):
        if name not in self.sems:
            self.sems[name] = self.ctx.enter_context(self.nc.semaphore(name))
        return self.sems[name]

    def col(self, name, j=0, n=1, rows=P):
        at, width = COLS[name]
        return self.cols[0:rows, at + j:at + j + n]

    def join(self, eng, name):
        sems = [self.sem(f"{e}_ended") for e in ("tensor", "vector", "scalar", "gpsimd")]
        self.n_ended[name] = self.n_ended.get(name, 0) + 1
        eng.drain().then_inc(self.sem(f"{name}_ended"), 1)
        for s in sems:
            eng.wait_ge(s, self.n_ended[name])

    def slot(self, u):
        s = u % SLOTS
        return self.ring[:, s * UNIT:(s + 1) * UNIT]

    def use_unit(self, pe):
        u = self.unit
        self.unit += 1
        pe.wait_ge(self.sem(f"slot{u % SLOTS}_loaded"), 16 * (u // SLOTS + 1))
        return u, self.slot(u)

    def release(self, units, key):
        b, k = self.T.jobs[key]
        for u in units:
            self.released[u] = (self.T.ready[b], k + 1)

    def product(self, pe, key, actT, kt=KT, banks=range(BANKS)):
        us = [self.use_unit(pe) for _ in range(kt // 4)]
        for i in range(NT):
            t = self.T.open(pe, (key, i), banks)
            for k in range(kt):
                w = us[k // 4][1].rearrange("p (k n) -> p k n", k=4)
                mm = pe.matmul(t[:, :], actT[:, k, i * P:(i + 1) * P], w[:, k % 4, :], start=k == 0, stop=k == kt - 1)
            self.T.close((key, i), mm)
        self.release([u for u, _ in us], (key, NT - 1))

    def product_T(self, pe, key, actT, kt=KT, banks=range(BANKS)):
        us = [self.use_unit(pe) for _ in range(kt // 4)]
        for c in range(2):
            t = self.T.open(pe, (key, c), banks)
            for m in range(2):
                for k in range(kt):
                    w = us[k // 4][1].rearrange("p (k n) -> p k n", k=4)
                    n0 = (2 * c + m) * P
                    mm = pe.matmul(t[:, m * SEQ:(m + 1) * SEQ], w[:, k % 4, n0:n0 + P], actT[:, k, :],
                                   start=k == 0, stop=k == kt - 1)
            self.T.close((key, c), mm)
        self.release([u for u, _ in us], (key, 1))

    def small_T(self, pe, key, name, actT, banks=range(BANKS)):
        at, n = SMALL[name]
        t = self.T.open(pe, key, banks)
        for k in range(KT):
            mm = pe.matmul(t[0:n, 0:SEQ], self.small[:, k, at:at + n], actT[:, k, :], start=k == 0, stop=k == KT - 1)
        self.T.close(key, mm)

    def small_rows(self, pe, key, name, actT, banks=range(BANKS)):
        at, n = SMALL[name]
        t = self.T.open(pe, key, banks)
        for i in range(NT):
            for k in range(KT):
                mm = pe.matmul(t[:, i * n:(i + 1) * n], actT[:, k, i * P:(i + 1) * P], self.small[:, k, at:at + n],
                               start=k == 0, stop=k == KT - 1)
        self.T.close(key, mm)


class Phase:

    joins = True
    shared = {}

    def s(self, what):
        for family, counts in self.shared.items():
            if what in counts:
                return self.net.sem(f"{family}_{what}")
        return self.net.sem(f"{self.tag}_{what}")

    def base(self, what):
        n = 0
        for ph in self.net.phase_objects:
            if ph is self:
                return n
            for family, counts in self.shared.items():
                if what in counts and family in ph.shared:
                    n += ph.shared[family][what]

    def rows(self):
        return ()

    def rows_here(self, eng):
        eng.wait_ge(self.net.sem("row_loaded"), self.net.rows_at[self.tag])

    def gpsimd(self, pool):
        pass


class Start(Phase):
    tag = "start"
    joins = False

    def __init__(self, net):
        self.net = net

    def tensor(self, pe):
        pe.wait_ge(self.net.sem("inputs_loaded"), 16 * 3)

    def vector(self, dve):
        net = self.net
        dve.wait_ge(net.sem("cols_loaded"), 16)
        net.dv(dve.memset(net.ones[:, :], 1.0))
        net.dv(dve.memset(net.zeros[:, :], 0.0))

    def scalar(self, act):
        net, io = self.net, self.net.io
        act.dma_start(net.cols[:, :], io["cols"]).then_inc(net.sem("cols_loaded"), 16)
        for dst, src in ((net.xT, io["xT"].rearrange("(k p) t -> p k t", p=P)),
                         (net.small, io["small"].rearrange("(k p) n -> p k n", p=P)),
                         (net.ident[:, :], io["ident"])):
            act.dma_start(dst, src).then_inc(net.sem("inputs_loaded"), 16)
        for dst, src in ((net.causal[:, :], io["causal"]),
                         (net.bias_row[:, :], io["bias_row"].partition_broadcast(P)),
                         (net.x, io["x"].rearrange("(i p) d -> p i d", p=P))):
            act.dma_start(dst, src).then_inc(net.sem("rest_loaded"), 16)
        act.wait_ge(net.sem("cols_loaded"), 16)


class LayerNorm(Phase):
    shared = {"ln": {"var": NT, "rstd": NT, "normed": NT}}

    def __init__(self, net, n):
        self.net, self.n, self.tag = net, n, f"ln{n}"

    def tensor(self, pe):
        net = self.net
        for i in range(NT):
            pe.wait_ge(self.s("normed"), self.base("normed") + i + 1)
            for c in range(2):
                t = net.T.open(pe, (self.tag, i, c))
                for k in range(4):
                    n0 = (4 * c + k) * P
                    mm = pe.transpose(t[:, k * P:(k + 1) * P], net.x[:, i, n0:n0 + P], net.ident[:, :])
                net.T.close((self.tag, i, c), mm)

    def vector(self, dve):
        net, s, st = self.net, self.net.dv, self.net.stat
        for i in range(NT):
            raw = st[:, 16 * i:16 * i + 12]
            for c in range(2):
                s(dve.bn_stats(raw[:, 6 * c:6 * c + 6], net.x[:, i, 512 * c:512 * c + 512]))
            s(dve.bn_aggr(st[:, 32 + 4 * i:34 + 4 * i], raw))
            s(dve.tensor_scalar(st[:, 34 + 4 * i:35 + 4 * i], st[:, 33 + 4 * i:34 + 4 * i], LN_EPS, None, ALU.add))
            dve.sem_inc(self.s("var"), 1)
        self.rows_here(dve)
        for i in range(NT):
            dve.wait_ge(self.s("rstd"), self.base("rstd") + i + 1)
            s(dve.tensor_scalar(net.x[:, i, :], net.x[:, i, :], st[:, 32 + 4 * i:33 + 4 * i],
                                st[:, 35 + 4 * i:36 + 4 * i], ALU.subtract, ALU.mult))
            s(dve.tensor_tensor(net.x[:, i, :], net.x[:, i, :], net.rows[:, 0, :], ALU.mult))
            s(dve.tensor_tensor(net.x[:, i, :], net.x[:, i, :], net.rows[:, 1, :], ALU.add))
            dve.sem_inc(self.s("normed"), 1)

    def gpsimd(self, pool):
        net, st = self.net, self.net.stat
        net.po(pool.memset(st[:, 60:61], -0.5))
        for i in range(NT):
            pool.wait_ge(self.s("var"), self.base("var") + i + 1)
            net.po(pool.tensor_tensor(st[:, 35 + 4 * i:36 + 4 * i], st[:, 34 + 4 * i:35 + 4 * i], st[:, 60:61], ALU.pow))
            pool.sem_inc(self.s("rstd"), 1)

    def scalar(self, act):
        net = self.net
        for i in range(NT):
            for c in range(2):
                t = net.T.take(act, (self.tag, i, c))
                net.ac(act.activation(net.xT[:, 4 * c:4 * c + 4, i * P:(i + 1) * P],
                                      t[:, :].rearrange("p (k t) -> p k t", k=4), ACT.Copy))
                net.T.free(act, (self.tag, i, c))

    def rows(self):
        return f"ln_g{self.n}", f"ln_b{self.n}"


class Residual(Phase):

    def tensor_out(self, pe, catT):
        for c in range(2):
            self.net.product(pe, (self.tag, "mix", c), catT)

    def vector_out(self, dve):
        net = self.net
        for c in range(2):
            for i in range(NT):
                t = net.T.take(dve, ((self.tag, "mix", c), i))
                xs = net.x[:, i, c * 512:(c + 1) * 512]
                net.dv(dve.scalar_tensor_tensor(xs, xs, ALPHA, t[:, :], ALU.mult, ALU.add))
                net.T.free(dve, ((self.tag, "mix", c), i))


class Heads:
    mlstm = False

    def alloc_heads(self, a):
        self.sm, self.p, self.pT = ([a.take(TRI) for _ in range(2)] for _ in range(3))
        self.hs = a.take(32).rearrange("p (b n) -> p b n", b=2)

    def tensor_heads(self, pe):
        net, T = self.net, self.net.T
        for h in range(HEADS + 1):
            if h < HEADS:
                if self.mlstm:
                    t = T.open(pe, (self.tag, "L", h))
                    for i in range(NT):
                        out, n = t[:, i * P:i * P + (i + 1) * P], (i + 1) * P
                        mm = self.head_bias(pe, h, i, out, n, True, True)
                    T.close((self.tag, "L", h), mm)
                t = T.open(pe, (self.tag, "S", h))
                for i in range(NT):
                    out, n = t[:, i * P:i * P + (i + 1) * P], (i + 1) * P
                    mm = pe.matmul(out, self.q(h)[:, i * P:(i + 1) * P], self.k(h)[:, 0:n], start=True,
                                   stop=self.mlstm)
                    if not self.mlstm:
                        mm = self.head_bias(pe, h, i, out, n, False, True)
                T.close((self.tag, "S", h), mm)
            if h >= 1:
                g = h - 1
                pe.wait_ge(self.s("p_ready"), self.base("p_ready") + g + 1)
                t = T.open(pe, (self.tag, "PT", g))
                for b in range(3):
                    mm = pe.transpose(t[:, b * P:(b + 1) * P], self.p[g % 2][:, b * P:(b + 1) * P], net.ident[:, :])
                T.close((self.tag, "PT", g), mm)
                t = T.open(pe, (self.tag, "O", g))
                pe.wait_ge(self.s("pT_ready"), self.base("pT_ready") + g + 1)
                lo, hi = self.out_rows(g)
                pe.matmul(t[lo:hi, 0:SEQ], self.v(g, 0), self.pT[g % 2][:, 0:2 * P], start=True, stop=False,
                          skip_group_check=True)
                mm = pe.matmul(t[lo:hi, P:SEQ], self.v(g, 1), self.pT[g % 2][:, 2 * P:3 * P], start=False, stop=True,
                               skip_group_check=True)
                T.close((self.tag, "O", g), mm)

    def vector_heads(self, dve):
        net, T, s = self.net, self.net.T, self.net.dv
        for h in range(HEADS + 1):
            if h < HEADS:
                sm, hs = self.sm[h % 2], self.hs[:, h % 2, :]
                key = (self.tag, "L" if self.mlstm else "S", h)
                t = T.take(dve, key)
                s(dve.tensor_tensor(sm, t[:, 0:TRI], self.mask, ALU.add))
                T.free(dve, key)
                for i in range(NT):
                    s(dve.tensor_reduce(hs[:, i:i + 1], sm[:, i * P:i * P + (i + 1) * P], AX, ALU.max))
                if self.mlstm:
                    s(dve.tensor_tensor(hs[:, 0:2], hs[:, 0:2], self.F_rows[:, :, h], ALU.max))
                s(dve.tensor_scalar(hs[:, 2:4], hs[:, 0:2], -1.0, None, ALU.mult))
                dve.sem_inc(self.s("max_ready"), 1)
            if h >= 1:
                g = h - 1
                p, hs = self.p[g % 2], self.hs[:, g % 2, :]
                dve.wait_ge(self.s("exp_ready"), self.base("exp_ready") + g + 1)
                if self.mlstm:
                    t = T.take(dve, (self.tag, "S", g))
                    for i in range(NT):
                        a, n = i * P, (i + 1) * P
                        s(dve.tensor_tensor_reduce(p[:, a:a + n], p[:, a:a + n], t[:, a:a + n], 1.0, 0.0, ALU.mult,
                                                   ALU.add, hs[:, 4 + i:5 + i]))
                    T.free(dve, (self.tag, "S", g))
                    s(dve.scalar_tensor_tensor(hs[:, 6:8], hs[:, 4:6], -1.0, hs[:, 4:6], ALU.mult, ALU.max))
                    s(dve.tensor_tensor(hs[:, 6:8], hs[:, 6:8], hs[:, 8:10], ALU.max))
                    s(dve.reciprocal(hs[:, 10:12], hs[:, 6:8]))
                else:
                    s(dve.reciprocal(hs[:, 10:12], hs[:, 4:6]))
                for i in range(NT):
                    a, n = i * P, (i + 1) * P
                    s(dve.tensor_scalar(p[:, a:a + n], p[:, a:a + n], hs[:, 10 + i:11 + i], None, ALU.mult))
                dve.sem_inc(self.s("p_ready"), 1)

    def scalar_heads(self, act):
        net, T, s = self.net, self.net.T, self.net.ac
        for h in range(HEADS + 1):
            if h < HEADS:
                act.wait_ge(self.s("max_ready"), self.base("max_ready") + h + 1)
                hs = self.hs[:, h % 2, :]
                for i in range(NT):
                    a, n = i * P, (i + 1) * P
                    kw = {} if self.mlstm else {"accum_out": hs[:, 4 + i:5 + i]}
                    s(act.activation(self.p[h % 2][:, a:a + n], self.sm[h % 2][:, a:a + n], ACT.Exp,
                                     bias=hs[:, 2 + i:3 + i], **kw))
                if self.mlstm:
                    s(act.activation(hs[:, 8:10], hs[:, 2:4], ACT.Exp))
                act.sem_inc(self.s("exp_ready"), 1)
            if h >= 1:
                g = h - 1
                t = T.take(act, (self.tag, "PT", g))
                s(act.activation(self.pT[g % 2], t[:, 0:TRI], ACT.Copy))
                T.free(act, (self.tag, "PT", g))
                act.sem_inc(self.s("pT_ready"), 1)
                t = T.take(act, (self.tag, "O", g))
                lo, hi = self.out_rows(g)
                self.keep_out(act, g, t[lo:hi, 0:SEQ])
                T.free(act, (self.tag, "O", g))
                act.sem_inc(self.s("out_kept"), 1)


HEAD_COUNTS = {w: HEADS for w in ("max_ready", "exp_ready", "p_ready", "pT_ready", "out_kept")}
GATE_COUNTS = {w: 2 * NT for w in ("gate_ready", "gate_used")}


class Fox(Residual, Heads):
    tag = "fox"
    shared = {"head": HEAD_COUNTS}

    def __init__(self, net):
        self.net = net
        a = Arena(net.scratch)
        self.catT = a.take(8 * SEQ, 8, SEQ)
        self.uT = a.take(4 * SEQ, 4, SEQ)
        self.qT = a.take(4 * SEQ, 4, SEQ)
        self.kT = a.take(4 * SEQ, 4, SEQ)
        self.vv = a.take(NT * 512, NT, 512)
        self.B = [a.take(512, 4, P) for _ in range(2)]
        self.Cz = [a.take(512, 16, 32) for _ in range(2)]
        self.g = [a.take(512) for _ in range(2)]
        self.u, self.t = a.take(512), a.take(512)
        self.turned = [self.catT[:, 2 * n:2 * n + 2, :].rearrange("p a b -> p (a b)") for n in range(2)]
        self.h = [a.take(512) for _ in range(2)]
        self.C = [h.rearrange("p (a b) -> p a b", a=16) for h in self.h]
        self.w = a.take(20 * 16, 20, 16)
        b = Arena(net.scratch, a.at)
        self.ph = [a.take(16 * SEQ, 16, SEQ) for _ in range(2)]
        self.alloc_heads(b)
        self.sel = b.take(8 * P, 8, P, rows=8)
        self.ft = [b.take(SEQ, rows=8) for _ in range(6)]
        self.yT = self.catT[:, 4:8, :]
        self.mask = net.causal[:, :]
        self.sig = [self.B[0].rearrange("p a b -> p (a b)"), self.B[1].rearrange("p a b -> p (a b)")]

    def q(self, h):
        r = 64 * (h % 2)
        return self.qT[r:r + 64, h // 2, :]

    def k(self, h):
        r = 64 * (h % 2)
        return self.kT[r:r + 64, h // 2, :]

    def v(self, h, i):
        return self.vv[:, i, h * 64:(h + 1) * 64]

    def out_rows(self, h):
        return 64 * (h % 2), 64 * (h % 2) + 64

    def keep_out(self, act, h, out):
        lo, hi = self.out_rows(h)
        self.net.ac(act.activation(self.catT[lo:hi, h // 2, :], out, ACT.Copy))

    def head_bias(self, pe, h, i, out, n, first, last):
        c, negc = self.ft[4], self.ft[5]
        pe.matmul(out, self.sel[0:8, h, :], negc[0:8, 0:n], start=first, stop=False)
        return pe.matmul(out, c[0:8, i * P:(i + 1) * P], self.sel[0:8, h, 0:1].to_broadcast([8, n]), start=False,
                         stop=last)

    def tensor(self, pe):
        net, T = self.net, self.net.T
        low, high = range(4), range(4, 8)
        net.product_T(pe, "fox_u", net.xT, banks=high)
        pe.wait_ge(self.s("params_loaded"), 16 * 4)

        def bu(j):
            k, m = divmod(j, 4)
            t = T.open(pe, ("bu", j), low)
            for part in range(2):
                mm = pe.matmul(t[:, part * SEQ:(part + 1) * SEQ], self.B[part][32 * m:32 * m + 32, k, :],
                               self.uT[32 * m:32 * m + 32, k, :], start=True, stop=True)
            T.close(("bu", j), mm)

        def y(k):
            t = T.open(pe, ("y", k), high)
            for m in range(4):
                j = 4 * k + m
                pe.wait_ge(self.s("h_ready"), j + 1)
                for part in range(2):
                    mm = pe.matmul(t[32 * m:32 * m + 32, 0:SEQ], self.Cz[part][:, j, :],
                                   self.h[j % 2][:, part * SEQ:(part + 1) * SEQ], start=part == 0, stop=part == 1)
                if m < 3:
                    mm.then_inc(self.s("h_used"), 1)
                else:
                    T.close(("y", k), mm)
                if j + 4 < 16:
                    bu(j + 4)

        pe.wait_ge(self.s("u_kept"), 2)
        for j in range(4):
            bu(j)
        net.product_T(pe, "fox_q", net.xT, banks=high)
        net.product_T(pe, "fox_k", net.xT, banks=high)
        net.product(pe, "fox_v", net.xT, banks=high)
        for k in range(4):
            y(k)
        net.small_T(pe, "fox_f", "fox_f", net.xT, banks=high)
        pe.wait_ge(self.s("qkv_kept"), 6)
        pe.wait_ge(self.s("sel_loaded"), 16)
        pe.wait_ge(self.s("c_ready"), 1)
        self.tensor_heads(pe)
        pe.wait_ge(self.s("gelu_kept"), 4)
        net.product_T(pe, "fox_glu", self.yT, kt=4)
        pe.wait_ge(self.s("out_kept"), self.base("out_kept") + HEADS)
        pe.wait_ge(self.s("glu_done"), 2)
        self.tensor_out(pe, self.catT)

    def scalar(self, act):
        net, T, s, io = self.net, self.net.T, self.net.ac, self.net.io
        for n, dst in enumerate(self.B):
            act.dma_start(dst, io["s5_b"][n].rearrange("p (k n) -> p k n", k=4)).then_inc(self.s("params_loaded"), 16)
        for n, dst in enumerate(self.C):
            act.dma_start(dst, io["s5_c"][n].rearrange("p (k n) -> p k n", k=16)).then_inc(self.s("params_loaded"), 16)
        for c in range(2):
            t = T.take(act, ("fox_u", c))
            s(act.activation(self.uT[:, 2 * c:2 * c + 2, :], t[:, :].rearrange("p (m t) -> p m t", m=2), ACT.Copy))
            T.free(act, ("fox_u", c))
            act.sem_inc(self.s("u_kept"), 1)
        for key, dst, scale in (("fox_q", self.qT, 0.125), ("fox_k", self.kT, 1.0)):
            for c in range(2):
                t = T.take(act, (key, c))
                s(act.activation(dst[:, 2 * c:2 * c + 2, :], t[:, :].rearrange("p (m t) -> p m t", m=2), ACT.Copy,
                                 scale=scale))
                T.free(act, (key, c))
                act.sem_inc(self.s("qkv_kept"), 1)
        for i in range(NT):
            t = T.take(act, ("fox_v", i))
            s(act.activation(self.vv[:, i, :], t[:, :], ACT.Copy))
            T.free(act, ("fox_v", i))
            act.sem_inc(self.s("qkv_kept"), 1)
        for k in range(4):
            act.wait_ge(self.s("y_kept"), k + 1)
            s(act.activation(self.yT[:, k, :], self.yT[:, k, :], ACT.Gelu_apprx_tanh))
            act.sem_inc(self.s("gelu_kept"), 1)
        act.dma_start(self.sel, io["sel"].rearrange("p (a b) -> p a b", a=8)).then_inc(self.s("sel_loaded"), 16)
        act.wait_ge(self.s("f_ready"), 1)
        s(act.activation(self.ft[2], self.ft[1], ACT.Exp))
        s(act.activation(self.ft[2], self.ft[2], ACT.Ln, bias=net.ones[0:8, 0:1]))
        act.sem_inc(self.s("log_ready"), 1)
        self.scalar_heads(act)
        for c in range(2):
            t = T.take(act, ("fox_glu", c))
            for m in range(2):
                s(act.activation(self.sig[c][:, m * SEQ:(m + 1) * SEQ], t[:, m * SEQ:(m + 1) * SEQ], ACT.Sigmoid,
                                 bias=net.col("b_glu", 2 * c + m)))
            T.free(act, ("fox_glu", c))
            act.sem_inc(self.s("glu_sig"), 1)

    def vector(self, dve):
        net, T, s = self.net, self.net.T, self.net.dv
        w = self.w
        are, aim = net.col("a_re", 0, 16), net.col("a_im", 0, 16)
        tt = lambda o, a, b, op: s(dve.tensor_tensor(o, a, b, op))
        ts = lambda o, a, c1, c2, op1, op2: s(dve.tensor_scalar(o, a, c1, c2, op1, op2))
        W = lambda n: w[:, n, :]
        exp_columns(net, dve, W(0), net.col("log_dt", 0, 16), W(13), W(14), W(15))
        tt(W(1), aim, W(0), ALU.mult)
        tt(W(2), are, W(0), ALU.mult)
        exp_columns(net, dve, W(3), W(2), W(13), W(14), W(15))
        ts(W(4), W(1), 1.0 / (2 * math.pi), ROUND, ALU.mult, ALU.add)
        ts(W(4), W(4), ROUND, None, ALU.subtract, ALU.bypass)
        for part in (TWO_PI_HI, TWO_PI_MID, TWO_PI_LO):
            s(dve.scalar_tensor_tensor(W(1), W(4), -part, W(1), ALU.mult, ALU.add))
        ts(W(4), W(1), 3.1415927, -3.1415927, ALU.min, ALU.max)
        sin, cos = W(6), W(7)
        sin_cos_columns(net, dve, sin, cos, W(4), W(13), W(14), W(15))
        tt(W(8), W(3), cos, ALU.mult)
        tt(W(9), W(3), sin, ALU.mult)
        ts(W(8), W(8), -1.0, None, ALU.add, ALU.bypass)
        tt(W(10), are, are, ALU.mult)
        tt(W(11), aim, aim, ALU.mult)
        tt(W(10), W(10), W(11), ALU.add)
        s(dve.reciprocal(W(10), W(10)))
        tt(W(11), W(8), are, ALU.mult)
        tt(W(12), W(9), aim, ALU.mult)
        tt(W(11), W(11), W(12), ALU.add)
        tt(W(11), W(11), W(10), ALU.mult)
        tt(W(12), W(9), are, ALU.mult)
        tt(W(13), W(8), aim, ALU.mult)
        tt(W(12), W(12), W(13), ALU.subtract)
        tt(W(12), W(12), W(10), ALU.mult)
        dve.wait_ge(self.s("params_loaded"), 16 * 4)
        zr = W(11).unsqueeze(2).to_broadcast([P, 16, 32])
        zi = W(12).unsqueeze(2).to_broadcast([P, 16, 32])
        tmp = self.t.rearrange("p (a b) -> p a b", a=16)
        tt(self.Cz[0], self.C[0], zr, ALU.mult)
        tt(tmp, self.C[1], zi, ALU.mult)
        tt(self.Cz[0], self.Cz[0], tmp, ALU.subtract)
        tt(self.Cz[1], self.C[0], zi, ALU.mult)
        tt(tmp, self.C[1], zr, ALU.mult)
        s(dve.scalar_tensor_tensor(self.Cz[1].rearrange("p a b -> p (a b)"), self.Cz[1].rearrange("p a b -> p (a b)"),
                                   -1.0, self.t, ALU.mult, ALU.subtract))
        pr, pi = self.ph
        s(dve.memset(pr[:, :, 0:1], 1.0))
        s(dve.memset(pi[:, :, 0:1], 0.0))
        wr, wi = W(14), W(15)
        s(dve.tensor_copy(wr, cos))
        s(dve.tensor_copy(wi, sin))
        n = 1
        while n < SEQ:
            for a in range(0, n, 32):
                m = min(32, n - a)
                tm = self.t[:, 0:16 * m].rearrange("p (a b) -> p a b", a=16)
                cr, ci = wr.unsqueeze(2).to_broadcast([P, 16, m]), wi.unsqueeze(2).to_broadcast([P, 16, m])
                tt(pr[:, :, n + a:n + a + m], pr[:, :, a:a + m], cr, ALU.mult)
                tt(tm, pi[:, :, a:a + m], ci, ALU.mult)
                tt(pr[:, :, n + a:n + a + m], pr[:, :, n + a:n + a + m], tm, ALU.subtract)
                tt(pi[:, :, n + a:n + a + m], pr[:, :, a:a + m], ci, ALU.mult)
                tt(tm, pi[:, :, a:a + m], cr, ALU.mult)
                tt(pi[:, :, n + a:n + a + m], pi[:, :, n + a:n + a + m], tm, ALU.add)
            tt(W(16), wr, wr, ALU.mult)
            tt(W(17), wi, wi, ALU.mult)
            tt(W(18), wr, wi, ALU.mult)
            tt(wr, W(16), W(17), ALU.subtract)
            ts(wi, W(18), 2.0, None, ALU.mult, ALU.bypass)
            n *= 2

        def y_keep(k):
            t = T.take(dve, ("y", k))
            s(dve.scalar_tensor_tensor(self.yT[:, k, :], self.uT[:, k, :], net.col("s5_d", k), t[:, 0:SEQ], ALU.mult,
                                       ALU.add))
            T.free(dve, ("y", k))
            dve.sem_inc(self.s("y_kept"), 1)

        def parts(v):
            return v.rearrange("p (a t) -> p a t", a=2)

        for j in range(16):
            cr = pr[:, j:j + 1, :].to_broadcast([P, 2, SEQ])
            ci = pi[:, j:j + 1, :].to_broadcast([P, 2, SEQ])
            g, u, t = self.g[j % 2], self.u, self.t
            b = T.take(dve, ("bu", j))
            tt(parts(u), parts(b[:, :]), cr, ALU.mult)
            tt(parts(t), parts(b[:, :]), ci, ALU.mult)
            T.free(dve, ("bu", j))
            if j >= 2:
                dve.wait_ge(self.s("h_ready"), j - 1)
            tt(g[:, 0:SEQ], u[:, 0:SEQ], t[:, SEQ:], ALU.add)
            tt(g[:, SEQ:], u[:, SEQ:], t[:, 0:SEQ], ALU.subtract)
            for part in range(2):
                xs = g[:, part * SEQ:(part + 1) * SEQ]
                s(dve.tensor_tensor_scan(xs, W(3)[:, j:j + 1].to_broadcast([P, SEQ]), xs, 0.0, ALU.mult, ALU.add))
            dve.sem_inc(self.s("g_ready"), 1)
            if j % 4 == 3 and j > 3:
                y_keep(j // 4 - 1)
        y_keep(3)
        dve.wait_ge(net.sem("rest_loaded"), 16 * 3)
        ft = self.ft
        t = T.take(dve, "fox_f")
        ts(ft[0], t[0:8, 0:SEQ], net.col("fox_f_bias", rows=8), None, ALU.add, ALU.bypass)
        T.free(dve, "fox_f")
        log_sigmoid_front(net, dve, ft[0], ft[1])
        dve.sem_inc(self.s("f_ready"), 1)
        dve.wait_ge(self.s("log_ready"), 1)
        s(dve.scalar_tensor_tensor(ft[3], ft[0], 0.0, ft[2], ALU.min, ALU.subtract))
        s(dve.tensor_tensor_scan(ft[4], net.ones[0:8, 0:SEQ], ft[3], 0.0, ALU.mult, ALU.add))
        ts(ft[5], ft[4], -1.0, None, ALU.mult, ALU.bypass)
        dve.sem_inc(self.s("c_ready"), 1)
        self.vector_heads(dve)
        T.take(dve, ("fox_glu", 1))
        for c in range(2):
            dve.wait_ge(self.s("glu_sig"), c + 1)
            y = self.yT[:, 2 * c:2 * c + 2, :].rearrange("p a b -> p (a b)")
            tt(y, y, self.sig[c], ALU.mult)
            dve.sem_inc(self.s("glu_done"), 1)
        self.vector_out(dve)

    def gpsimd(self, pool):
        net, T = self.net, self.net.T
        tt = lambda o, a, b, op: net.po(pool.tensor_tensor(o, a, b, op))
        parts = lambda v: v.rearrange("p (a t) -> p a t", a=2)
        for j in range(16):
            cr = self.ph[0][:, j:j + 1, :].to_broadcast([P, 2, SEQ])
            ci = self.ph[1][:, j:j + 1, :].to_broadcast([P, 2, SEQ])
            g, (u, t), h = self.g[j % 2], self.turned, self.h[j % 2]
            pool.wait_ge(self.s("g_ready"), j + 1)
            tt(parts(u), parts(g), cr, ALU.mult)
            tt(parts(t), parts(g), ci, ALU.mult)
            if j >= 2:
                k, m = divmod(j - 2, 4)
                if m < 3:
                    pool.wait_ge(self.s("h_used"), 3 * k + m + 1)
                else:
                    T.take(pool, ("y", k))
            tt(h[:, 0:SEQ], u[:, 0:SEQ], t[:, SEQ:], ALU.subtract)
            tt(h[:, SEQ:], u[:, SEQ:], t[:, 0:SEQ], ALU.add)
            pool.sem_inc(self.s("h_ready"), 1)


class Mlstm(Residual, Heads):
    tag = "mlstm"
    shared = {"head": HEAD_COUNTS}
    mlstm = True

    def __init__(self, net):
        self.net = net
        a = Arena(net.scratch)
        self.catT = a.take(8 * SEQ, 8, SEQ)
        self.qkT = a.take(16 * SEQ, 16, SEQ)
        self.vv = a.take(NT * D, NT, D)
        self.oT = a.take(8 * SEQ, 8, SEQ)
        self.pad = [a.take(2 * (SEQ + 3), 2, SEQ + 3) for _ in range(2)]
        self.conv = [a.take(SEQ) for _ in range(4)]
        self.silu = [a.take(SEQ) for _ in range(2)]
        self.alloc_heads(a)
        self.sel = a.take(8 * P, 8, P, rows=8)
        self.ft = [a.take(SEQ, rows=8) for _ in range(6)]
        self.F_rows = a.take(16, NT, 8)
        self.mod_part = [a.take(512) for _ in range(2)]
        self.mask = net.causal[:, :]

    def q(self, h):
        return self.qkT[:, h, :]

    def k(self, h):
        return self.qkT[:, 8 + h, :]

    def v(self, h, i):
        return self.vv[:, i, h * P:(h + 1) * P]

    def out_rows(self, h):
        return 0, P

    def keep_out(self, act, h, out):
        self.net.ac(act.activation(self.catT[:, h, :], out, ACT.Copy))

    def head_bias(self, pe, h, i, out, n, first, last):
        F, iF = self.ft[4], self.ft[5]
        pe.matmul(out, self.sel[0:8, h, :], iF[0:8, 0:n], start=first, stop=False)
        return pe.matmul(out, F[0:8, i * P:(i + 1) * P], self.sel[0:8, h, 0:1].to_broadcast([8, n]), start=False,
                         stop=last)

    def tensor(self, pe):
        net, T = self.net, self.net.T
        net.small_T(pe, "mlstm_f", "mlstm_f", net.xT)
        net.small_T(pe, "mlstm_i", "mlstm_i", net.xT)
        self.mod_units = []
        for b in range(8):
            if b < 4:
                net.product_T(pe, ("mlstm_qk", b), net.xT)
            elif b < 6:
                net.product(pe, ("mlstm_v", b - 4), net.xT)
            else:
                net.product_T(pe, ("mlstm_o", b - 6), net.xT)
            self.mod_units.append((net.unit, net.unit + 1))
            for n, u in enumerate(self.mod_units[-1]):
                net.released[u] = (self.s("mod_units_used"), 2 * b + n + 1)
            net.unit += 2
            if b >= 1:
                self.mod_sum(pe, b - 1)
        self.mod_sum(pe, 7)
        pe.wait_ge(self.s("F_ready"), 1)
        t = T.open(pe, "mlstm_FT")
        for i in range(NT):
            mm = pe.transpose(t[:, 8 * i:8 * i + 8], self.ft[4][0:8, i * P:(i + 1) * P], net.ident[0:8, 0:8])
        T.close("mlstm_FT", mm)
        pe.wait_ge(self.s("qk_ready"), 16)
        pe.wait_ge(self.s("v_kept"), 4)
        pe.wait_ge(self.s("sel_loaded"), 16)
        self.tensor_heads(pe)
        pe.wait_ge(self.s("gated"), 1)
        self.tensor_out(pe, self.catT)

    def mod_sum(self, pe, b):
        T = self.net.T
        pe.wait_ge(self.s("mod_summed"), b + 1)
        t = T.open(pe, ("mod", b))
        for m in range(4):
            mm = pe.matmul(t[:, m:m + 1], self.mod_part[b % 2][:, m * P:(m + 1) * P], self.net.ones[:, 0:1], start=True,
                           stop=True)
        T.close(("mod", b), mm)

    def mod_keep(self, dve, b):
        net = self.net
        t = net.T.take(dve, ("mod", b))
        net.dv(dve.tensor_tensor(net.mod[:, 4 * b:4 * b + 4], t[:, 0:4], net.col("ada_b", 4 * b, 4), ALU.add))
        net.T.free(dve, ("mod", b))

    def mod_block(self, dve, b):
        net, part = self.net, self.mod_part[b % 2]
        for n, u in enumerate(self.mod_units[b]):
            dve.wait_ge(net.sem(f"slot{u % SLOTS}_loaded"), 16 * (u // SLOTS + 1))
            w = net.slot(u).rearrange("p (k n) -> p k n", k=4)
            for k in range(4):
                c = net.mod[:, 32 + 4 * n + k:33 + 4 * n + k]
                if n == 0 and k == 0:
                    net.dv(dve.tensor_scalar(part, w[:, k, :], c, None, ALU.mult))
                else:
                    net.dv(dve.scalar_tensor_tensor(part, w[:, k, :], c, part, ALU.mult, ALU.add))
            dve.sem_inc(self.s("mod_units_used"), 1)
        dve.sem_inc(self.s("mod_summed"), 1)

    def scalar(self, act):
        net, T, s, io = self.net, self.net.T, self.net.ac, self.net.io
        s(act.activation(net.mod[:, 32:40], net.col("c", 0, 8), ACT.Silu))
        act.sem_inc(self.s("c_ready"), 1)
        act.dma_start(self.sel, io["sel"].rearrange("p (a b) -> p a b", a=8)).then_inc(self.s("sel_loaded"), 16)
        act.wait_ge(self.s("f_ready"), 1)
        s(act.activation(self.ft[2], self.ft[1], ACT.Exp))
        s(act.activation(self.ft[2], self.ft[2], ACT.Ln, bias=net.ones[0:8, 0:1]))
        act.sem_inc(self.s("log_ready"), 1)
        for j in range(16):
            act.wait_ge(self.s("conv_ready"), j + 1)
            if j < 8:
                s(act.activation(self.qkT[:, j, :], self.conv[j % 4], ACT.Silu))
            else:
                s(act.activation(self.qkT[:, j, :], self.conv[j % 4], ACT.Silu))
                s(act.activation(self.qkT[:, j, :], self.qkT[:, j, :], ACT.Copy, scale=P ** -0.5))
            act.sem_inc(self.s("qk_ready"), 1)
        for b in range(2):
            for i in range(NT):
                key = (("mlstm_v", b), i)
                t = T.take(act, key)
                s(act.activation(self.vv[:, i, b * 512:(b + 1) * 512], t[:, :], ACT.Copy))
                T.free(act, key)
                act.sem_inc(self.s("v_kept"), 1)
        for b in range(2):
            for c in range(2):
                key = (("mlstm_o", b), c)
                t = T.take(act, key)
                s(act.activation(self.oT[:, 4 * b + 2 * c:4 * b + 2 * c + 2, :],
                                 t[:, :].rearrange("p (m t) -> p m t", m=2), ACT.Sigmoid))
                T.free(act, key)
        act.sem_inc(self.s("o_kept"), 1)
        self.scalar_heads(act)

    def vector(self, dve):
        net, T, s = self.net, self.net.T, self.net.dv
        ft = self.ft
        t = T.take(dve, "mlstm_f")
        s(dve.tensor_scalar(ft[0], t[0:8, 0:SEQ], net.col("mlstm_f_bias", rows=8), None, ALU.add))
        T.free(dve, "mlstm_f")
        log_sigmoid_front(net, dve, ft[0], ft[1])
        dve.sem_inc(self.s("f_ready"), 1)
        for pad in self.pad:
            s(dve.memset(pad[:, :, 0:3], 0.0))
        dve.wait_ge(self.s("log_ready"), 1)
        s(dve.scalar_tensor_tensor(ft[3], ft[0], 0.0, ft[2], ALU.min, ALU.subtract))
        s(dve.tensor_tensor_scan(ft[4], net.ones[0:8, 0:SEQ], ft[3], 0.0, ALU.mult, ALU.add))
        t = T.take(dve, "mlstm_i")
        s(dve.scalar_tensor_tensor(ft[5], t[0:8, 0:SEQ], net.col("mlstm_i_bias", rows=8), ft[4], ALU.add, ALU.subtract))
        T.free(dve, "mlstm_i")
        dve.sem_inc(self.s("F_ready"), 1)
        for b in range(4):
            for c in range(2):
                key, pad = (("mlstm_qk", b), c), self.pad[c]
                t = T.take(dve, key)
                s(dve.tensor_copy(pad[:, :, 3:], t[:, :].rearrange("p (m t) -> p m t", m=2)))
                T.free(dve, key)
                for m in range(2):
                    j = 4 * b + 2 * c + m
                    y = self.conv[j % 4]
                    if j >= 4:
                        dve.wait_ge(self.s("qk_ready"), j - 3)
                    s(dve.tensor_scalar(y, pad[:, m, 0:SEQ], net.col("conv_w", j), net.col("conv_b", j), ALU.mult,
                                        ALU.add))
                    for tap in range(1, 4):
                        s(dve.scalar_tensor_tensor(y, pad[:, m, tap:tap + SEQ], net.col("conv_w", 16 * tap + j), y,
                                                   ALU.mult, ALU.add))
                    dve.sem_inc(self.s("conv_ready"), 1)
            if b == 0:
                dve.wait_ge(self.s("c_ready"), 1)
            self.mod_block(dve, b)
            if b >= 1:
                self.mod_keep(dve, b - 1)
        for b in range(4, 8):
            self.mod_block(dve, b)
            self.mod_keep(dve, b - 1)
        self.mod_keep(dve, 7)
        mod = net.mod
        for n in range(2):
            sc = mod[:, 16 * n + 8:16 * n + 16]
            s(dve.tensor_scalar(sc, sc, 1.0, None, ALU.add))
            s(dve.tensor_tensor(sc, sc, net.col(f"norm{n + 1}_g", 0, 8), ALU.mult))
        t = T.take(dve, "mlstm_FT")
        s(dve.tensor_copy(self.F_rows, t[:, 0:16].rearrange("p (i h) -> p i h", i=NT)))
        T.free(dve, "mlstm_FT")
        self.vector_heads(dve)
        dve.wait_ge(self.s("o_kept"), 1)
        dve.wait_ge(self.s("out_kept"), self.base("out_kept") + HEADS)
        s(dve.tensor_tensor(self.catT, self.catT, self.oT, ALU.mult))
        dve.sem_inc(self.s("gated"), 1)
        self.vector_out(dve)


def gate_rows(net, pe, key):
    for c in range(2):
        us = [net.use_unit(pe) for _ in range(2)]
        t = net.T.open(pe, (key, c))
        for k in range(KT):
            w = us[k // 4][1].rearrange("p (k n) -> p k n", k=4)
            mm = pe.matmul(t[:, :], net.mod[:, 32 + k:33 + k].to_broadcast([P, P]), w[:, k % 4, :], start=k == 0,
                           stop=k == KT - 1)
        net.T.close((key, c), mm)
        net.release([u for u, _ in us], (key, c))


def keep_gate_rows(net, dve, key, out, row=0):
    for c in range(2):
        t = net.T.take(dve, (key, c))
        net.dv(dve.tensor_tensor(out[:, c * 512:(c + 1) * 512], t[:, :], net.rows[:, row, c * 512:(c + 1) * 512], ALU.add))
        net.T.free(dve, (key, c))


class RmsNorm(Phase):
    shared = {"rms": {"squares": NT, "mean": NT, "rstd": NT, "normed": NT}}

    def __init__(self, net, n):
        self.net, self.n, self.tag = net, n, f"rms{n}"
        a = Arena(net.scratch)
        self.xn = a.take(NT * D, NT, D)
        self.junk = a.take(D)

    def rows(self):
        return ("final_g",) if self.n == 2 else ()

    def scalar(self, act):
        net, s, st = self.net, self.net.ac, self.net.stat
        for i in range(NT):
            s(act.activation(self.junk, net.x[:, i, :], ACT.Square, accum_out=st[:, i:i + 1]))
            act.sem_inc(self.s("squares"), 1)
        if self.n == 2:
            return
        for i in range(NT):
            for c in range(2):
                t = net.T.take(act, (self.tag, i, c))
                for k in range(4):
                    j = 4 * c + k
                    s(act.activation(net.xT[:, j, i * P:(i + 1) * P], t[:, k * P:(k + 1) * P], ACT.Identity,
                                     scale=net.mod[:, 16 * self.n + 8 + j:16 * self.n + 9 + j],
                                     bias=net.mod[:, 16 * self.n + j:16 * self.n + j + 1]))
                net.T.free(act, (self.tag, i, c))

    def tensor(self, pe):
        net = self.net
        if self.n == 2:
            return
        for i in range(NT):
            pe.wait_ge(self.s("normed"), self.base("normed") + i + 1)
            for c in range(2):
                t = net.T.open(pe, (self.tag, i, c))
                for k in range(4):
                    n0 = (4 * c + k) * P
                    mm = pe.transpose(t[:, k * P:(k + 1) * P], self.xn[:, i, n0:n0 + P], net.ident[:, :])
                net.T.close((self.tag, i, c), mm)

    def vector(self, dve):
        net, s, st = self.net, self.net.dv, self.net.stat
        for i in range(NT):
            dve.wait_ge(self.s("squares"), self.base("squares") + i + 1)
            s(dve.tensor_scalar(st[:, 2 + i:3 + i], st[:, i:i + 1], 1.0 / D, RMS_EPS, ALU.mult, ALU.add))
            dve.sem_inc(self.s("mean"), 1)
        for i in range(NT):
            dve.wait_ge(self.s("rstd"), self.base("rstd") + i + 1)
            out = net.x if self.n == 2 else self.xn
            s(dve.tensor_scalar(out[:, i, :], net.x[:, i, :], st[:, 4 + i:5 + i], None, ALU.mult))
            if self.n == 2:
                self.rows_here(dve)
                s(dve.tensor_tensor(out[:, i, :], out[:, i, :], net.rows[:, 0, :], ALU.mult))
            dve.sem_inc(self.s("normed"), 1)

    def gpsimd(self, pool):
        net, st = self.net, self.net.stat
        net.po(pool.memset(st[:, 60:61], -0.5))
        for i in range(NT):
            pool.wait_ge(self.s("mean"), self.base("mean") + i + 1)
            net.po(pool.tensor_tensor(st[:, 4 + i:5 + i], st[:, 2 + i:3 + i], st[:, 60:61], ALU.pow))
            pool.sem_inc(self.s("rstd"), 1)


class Branch(Phase):

    def tensor_branch(self, pe, catT, kt=KT):
        for c in range(2):
            self.net.product(pe, (self.tag, "gate", c), self.net.xT)
            self.net.product(pe, (self.tag, "out", c), catT, kt=kt)

    def scalar_branch(self, act):
        net = self.net
        for c in range(2):
            for i in range(NT):
                key = ((self.tag, "gate", c), i)
                t = net.T.take(act, key)
                if c:
                    act.wait_ge(self.s("gate_used"), self.base("gate_used") + i + 1)
                net.ac(act.activation(self.gate[i], t[:, :], ACT.Sigmoid))
                net.T.free(act, key)
                act.sem_inc(self.s("gate_ready"), 1)

    def vector_branch(self, dve, first):
        net, s = self.net, self.net.dv
        for c in range(2):
            for i in range(NT):
                key = ((self.tag, "out", c), i)
                dve.wait_ge(self.s("gate_ready"), self.base("gate_ready") + 2 * c + i + 1)
                t = net.T.take(dve, key)
                m = self.merged[:, i, c * 512:(c + 1) * 512]
                if first:
                    s(dve.tensor_tensor(m, self.gate[i], t[:, :], ALU.mult))
                else:
                    s(dve.tensor_tensor(self.gate[i], self.gate[i], t[:, :], ALU.mult))
                    s(dve.tensor_tensor(m, m, self.gate[i], ALU.add))
                net.T.free(dve, key)
                dve.sem_inc(self.s("gate_used"), 1)

    def take_merged(self):
        return Arena(self.net.scratch, SCRATCH - NT * D).take(NT * D, NT, D)


class Indexed(Branch, Heads):
    tag = "dsa"
    shared = {"head": HEAD_COUNTS, "branch": GATE_COUNTS}

    def __init__(self, net):
        self.net = net
        a = Arena(net.scratch)
        self.merged = self.take_merged()
        self.catT = a.take(8 * SEQ, 8, SEQ)
        self.qT = a.take(8 * SEQ, 8, SEQ)
        self.kT = a.take(8 * SEQ, 8, SEQ)
        self.vv = a.take(NT * D, NT, D)
        self.iqT = a.take(4 * SEQ, 4, SEQ)
        self.ikT = a.take(SEQ)
        self.iw = a.take(16, NT, 8)
        self.X = a.take(8 * SEQ, 8, SEQ)
        self.J = a.take(P)
        self.alloc_heads(a)
        self.score, self.work, self.term, self.sel_mask = (a.take(TRI) for _ in range(4))
        self.top = a.take(8)
        self.gate = [a.take(512) for _ in range(2)]
        self.buckets = a.take(TRI, rows=32)
        self.rel = a.take(8, rows=32)
        self.U = a.take(TRI, rows=8)
        assert a.at <= SCRATCH - NT * D
        self.mask = self.sel_mask

    def q(self, h):
        return self.qT[:, h, :]

    def k(self, h):
        return self.kT[:, h, :]

    def v(self, h, i):
        return self.vv[:, i, h * P:(h + 1) * P]

    def out_rows(self, h):
        return 0, P

    def keep_out(self, act, h, out):
        self.net.ac(act.activation(self.catT[:, h, :], out, ACT.Copy))

    def head_bias(self, pe, h, i, out, n, first, last):
        at = P if i == 0 else 0
        return pe.matmul(out, self.J, self.X[:, h, at:at + n], start=first, stop=last)

    def tensor(self, pe):
        net, T = self.net, self.net.T
        net.small_rows(pe, "dsa_iw", "idx_w", net.xT)
        u, w = net.use_unit(pe)
        t = T.open(pe, "dsa_ik")
        for k in range(KT):
            mm = pe.matmul(t[:, 0:SEQ], w[:, k * P:(k + 1) * P], net.xT[:, k, :], start=k == 0, stop=k == KT - 1)
        T.close("dsa_ik", mm)
        net.release([u], "dsa_ik")
        net.product_T(pe, "dsa_iq", net.xT)
        pe.wait_ge(self.s("tables_loaded"), 48)
        t = T.open(pe, "dsa_U")
        T.close("dsa_U", pe.matmul(t[0:8, 0:TRI], self.rel[0:32, 0:8], self.buckets[0:32, :], start=True, stop=True))
        pe.wait_ge(self.s("index_kept"), 3)
        for h in range(HEADS):
            t = T.open(pe, ("dsa_index", h))
            r = 64 * (h % 2)
            for i in range(NT):
                mm = pe.matmul(t[:, i * P:i * P + (i + 1) * P], self.iqT[r:r + 64, h // 2, i * P:(i + 1) * P],
                               self.ikT[r:r + 64, 0:(i + 1) * P], start=True, stop=True)
            T.close(("dsa_index", h), mm)
            if h == 3:
                for b in range(2):
                    net.product_T(pe, ("dsa_q", b), net.xT)
        for b in range(2):
            net.product_T(pe, ("dsa_k", b), net.xT)
        for b in range(2):
            net.product(pe, ("dsa_v", b), net.xT)
        pe.wait_ge(self.s("qkv_kept"), 12)
        pe.wait_ge(self.s("X_loaded"), 16)
        self.tensor_heads(pe)
        pe.wait_ge(self.s("out_kept"), self.base("out_kept") + HEADS)
        self.tensor_branch(pe, self.catT)

    def scalar(self, act):
        net, T, s, io = self.net, self.net.T, self.net.ac, self.net.io
        for dst, src in ((self.rel, io["rel_bias"]), (self.buckets, io["buckets"]), (self.J, io["flip"])):
            act.dma_start(dst, src).then_inc(self.s("tables_loaded"), 16)
        t = T.take(act, "dsa_ik")
        s(act.activation(self.ikT, t[:, 0:SEQ], ACT.Copy))
        T.free(act, "dsa_ik")
        act.sem_inc(self.s("index_kept"), 1)
        for c in range(2):
            t = T.take(act, ("dsa_iq", c))
            s(act.activation(self.iqT[:, 2 * c:2 * c + 2, :], t[:, :].rearrange("p (m t) -> p m t", m=2), ACT.Copy))
            T.free(act, ("dsa_iq", c))
            act.sem_inc(self.s("index_kept"), 1)
        t = T.take(act, "dsa_U")
        s(act.activation(self.U, t[0:8, 0:TRI], ACT.Copy))
        T.free(act, "dsa_U")
        act.dma_start(io["bias_by_distance"], self.U).then_inc(self.s("U_stored"), 16)
        act.wait_ge(self.s("U_stored"), 16)
        u = io["bias_by_distance"]
        act.dma_start(self.X, bass.AP(u.tensor, u.offset, [[1, P], [TRI, 8], [1, SEQ]])).then_inc(self.s("X_loaded"), 16)
        for key, dst, scale in (("dsa_q", self.qT, P ** -0.5), ("dsa_k", self.kT, 1.0)):
            for b in range(2):
                for c in range(2):
                    t = T.take(act, ((key, b), c))
                    j = 4 * b + 2 * c
                    s(act.activation(dst[:, j:j + 2, :], t[:, :].rearrange("p (m t) -> p m t", m=2), ACT.Copy,
                                     scale=scale))
                    T.free(act, ((key, b), c))
                    act.sem_inc(self.s("qkv_kept"), 1)
        for b in range(2):
            for i in range(NT):
                t = T.take(act, (("dsa_v", b), i))
                s(act.activation(self.vv[:, i, b * 512:(b + 1) * 512], t[:, :], ACT.Copy))
                T.free(act, (("dsa_v", b), i))
                act.sem_inc(self.s("qkv_kept"), 1)
        self.scalar_heads(act)
        self.scalar_branch(act)

    def vector(self, dve):
        net, T, s = self.net, self.net.T, self.net.dv
        t = T.take(dve, "dsa_iw")
        s(dve.tensor_scalar(self.iw, t[:, 0:16].rearrange("p (i h) -> p i h", i=NT), 512 ** -0.5, None, ALU.mult))
        T.free(dve, "dsa_iw")
        for h in range(HEADS):
            t = T.take(dve, ("dsa_index", h))
            dst = self.score if h == 0 else self.term
            for i in range(NT):
                a, n = i * P, (i + 1) * P
                s(dve.tensor_scalar(dst[:, a:a + n], t[:, a:a + n], 0.0, self.iw[:, i, h:h + 1], ALU.max, ALU.mult))
            T.free(dve, ("dsa_index", h))
            if h:
                s(dve.tensor_tensor(self.score, self.score, self.term, ALU.add))
        s(dve.tensor_tensor(self.score, self.score, net.causal[:, :], ALU.add))
        for i in range(NT):
            a, n = i * P, (i + 1) * P
            x, y = self.score[:, a:a + n], self.work[:, a:a + n]
            for _ in range(TOPK // 8):
                s(dve.max(self.top, x))
                s(dve.match_replace(y, self.top, x, TAKEN))
                x, y = y, x
            s(dve.tensor_scalar(self.sel_mask[:, a:a + n], x, TAKEN / 2, MASKED, ALU.is_gt, ALU.mult))
        s(dve.tensor_tensor(self.sel_mask, self.sel_mask, net.causal[:, :], ALU.add))
        self.vector_heads(dve)
        self.vector_branch(dve, True)


class Hgrn(Branch):
    tag = "hgrn"
    shared = {"branch": GATE_COUNTS}

    def __init__(self, net):
        self.net = net
        a = Arena(net.scratch)
        self.merged = self.take_merged()
        self.qT = a.take(8 * SEQ, 8, SEQ)
        self.kT = a.take(8 * SEQ, 8, SEQ)
        self.b = a.take(8 * SEQ, 8, SEQ)
        self.M = [a.take(8 * SEQ, 8, SEQ) for _ in range(2)]
        self.vv = a.take(NT * D, NT, D)
        self.AT = a.take(16 * P, 16, P)
        self.AT01 = a.take(8 * P, 8, P)
        self.level_masks = a.take(8 * P, 8, P)
        self.small = a.take(80)
        self.gate = [self.b.rearrange("p a b -> p (a b)")[:, c * 512:(c + 1) * 512] for c in range(2)]
        self.o = self.M[1].rearrange("p a b -> p (a b)").rearrange("p (i d) -> p i d", i=NT)
        self.g = self.M[0].rearrange("p a b -> p (a b)").rearrange("p (i d) -> p i d", i=NT)
        self.sq = self.kT.rearrange("p a b -> p (a b)").rearrange("p (i d) -> p i d", i=NT)
        self.catT = self.qT
        assert a.at <= SCRATCH - NT * D

    def rows(self):
        return ("hgrn_g",)

    def tensor(self, pe):
        net, T = self.net, self.net.T
        for b in range(2):
            net.product_T(pe, ("hgrn_f", b), net.xT)
        for b in range(2):
            net.product_T(pe, ("hgrn_q", b), net.xT)
        for b in range(2):
            net.product(pe, ("hgrn_v", b), net.xT)
        pe.wait_ge(self.s("k_ready"), 1)
        pe.wait_ge(self.s("q_kept"), 4)
        for n in range(4):
            t = T.open(pe, ("hgrn_level", -1, n))
            for m in range(4):
                h, i = divmod(4 * n + m, 2)
                mm = pe.matmul(t[:, m * P:(m + 1) * P], self.kT[:, h, i * P:(i + 1) * P],
                               self.qT[:, h, i * P:(i + 1) * P], start=True, stop=True)
            T.close(("hgrn_level", -1, n), mm)
        pe.wait_ge(self.s("m_ready"), 1)
        for n in range(2):
            t = T.open(pe, ("hgrn_cross", n))
            for m in range(4):
                h = 4 * n + m
                mm = pe.matmul(t[:, m * P:(m + 1) * P], self.M[0][:, h, 0:P], self.M[0][:, h, P:SEQ], start=True,
                               stop=True)
            T.close(("hgrn_cross", n), mm)
        for lv in range(len(LEVELS)):
            pe.wait_ge(self.s("m_ready"), lv + 2)
            M = self.M[(lv + 1) % 2]
            for n in range(4):
                t = T.open(pe, ("hgrn_level", lv, n))
                for m in range(4):
                    h, i = divmod(4 * n + m, 2)
                    tok = M[:, h, i * P:(i + 1) * P]
                    mm = pe.matmul(t[:, m * P:(m + 1) * P], tok, tok, start=True, stop=True)
                T.close(("hgrn_level", lv, n), mm)
        for b in range(2):
            net.product(pe, ("hgrn_g", b), net.xT)
        pe.wait_ge(self.s("v_kept"), 4)
        pe.wait_ge(self.s("at_ready"), 1)
        pe.wait_ge(self.s("cross_kept"), 2)
        for i in range(NT):
            for n in range(2):
                t = T.open(pe, ("hgrn_o", i, n))
                for m in range(4):
                    h = 4 * n + m
                    out, vs = t[:, m * P:(m + 1) * P], slice(h * P, (h + 1) * P)
                    if i:
                        pe.matmul(out, self.AT01[:, h, :], self.vv[:, 0, vs], start=True, stop=False)
                    mm = pe.matmul(out, self.AT[:, 2 * h + i, :], self.vv[:, i, vs], start=i == 0, stop=True)
                T.close(("hgrn_o", i, n), mm)
        for i in range(NT):
            for n in range(2):
                pe.wait_ge(self.s("o_gated"), 2 * i + n + 1)
                t = T.open(pe, ("hgrn_oT", i, n))
                for m in range(4):
                    h = 4 * n + m
                    mm = pe.transpose(t[:, m * P:(m + 1) * P], self.o[:, i, h * P:(h + 1) * P], net.ident[:, :])
                T.close(("hgrn_oT", i, n), mm)
        pe.wait_ge(self.s("oT_kept"), 4)
        self.tensor_branch(pe, self.catT)

    def scalar(self, act):
        net, T, s, io = self.net, self.net.T, self.net.ac, self.net.io
        act.dma_start(self.level_masks.bitcast(I32), io["level_masks"].rearrange("p (a b) -> p a b", a=8))\
           .then_inc(self.s("masks_loaded"), 16)
        act.wait_ge(self.s("lb_diff"), 1)
        s(act.activation(self.small[:, 8:16], self.small[:, 0:8], ACT.Exp))
        act.sem_inc(self.s("lb_exp"), 1)
        for b in range(2):
            for c in range(2):
                t = T.take(act, (("hgrn_f", b), c))
                j = 4 * b + 2 * c
                s(act.activation(self.kT[:, j:j + 2, :], t[:, :].rearrange("p (m t) -> p m t", m=2), ACT.Sigmoid))
                T.free(act, (("hgrn_f", b), c))
                act.sem_inc(self.s("sig_ready"), 1)
        act.wait_ge(self.s("f_ready"), 1)
        s(act.activation(self.b, self.kT, ACT.Ln))
        act.sem_inc(self.s("log_ready"), 1)
        for b in range(2):
            for c in range(2):
                t = T.take(act, (("hgrn_q", b), c))
                j = 4 * b + 2 * c
                s(act.activation(self.qT[:, j:j + 2, :], t[:, :].rearrange("p (m t) -> p m t", m=2), ACT.Copy))
                T.free(act, (("hgrn_q", b), c))
                act.sem_inc(self.s("q_kept"), 1)
        for b in range(2):
            for i in range(NT):
                t = T.take(act, (("hgrn_v", b), i))
                s(act.activation(self.vv[:, i, b * 512:(b + 1) * 512], t[:, :], ACT.Copy))
                T.free(act, (("hgrn_v", b), i))
                act.sem_inc(self.s("v_kept"), 1)
        for lv in range(-1, len(LEVELS)):
            M = self.M[(lv + 1) % 2]
            act.wait_ge(self.s("e_ready"), lv + 2)
            s(act.activation(M, M, ACT.Exp))
            act.sem_inc(self.s("exp_ready"), 1)
            if lv < 0:
                for n in range(2):
                    t = T.take(act, ("hgrn_cross", n))
                    s(act.activation(self.AT01[:, 4 * n:4 * n + 4, :], t[:, :].rearrange("p (m t) -> p m t", m=4),
                                     ACT.Copy))
                    T.free(act, ("hgrn_cross", n))
                    act.sem_inc(self.s("cross_kept"), 1)
        act.wait_ge(self.s("at_ready"), 1)
        for b in range(2):
            for i in range(NT):
                t = T.take(act, (("hgrn_g", b), i))
                s(act.activation(self.g[:, i, b * 512:(b + 1) * 512], t[:, :], ACT.Silu))
                T.free(act, (("hgrn_g", b), i))
                act.sem_inc(self.s("g_kept"), 1)
        for i in range(NT):
            for n in range(2):
                t = T.take(act, ("hgrn_o", i, n))
                s(act.activation(self.o[:, i, n * 512:(n + 1) * 512], t[:, :], ACT.Copy))
                T.free(act, ("hgrn_o", i, n))
                act.sem_inc(self.s("o_kept"), 1)
        for i in range(NT):
            for n in range(2):
                t = T.take(act, ("hgrn_oT", i, n))
                s(act.activation(self.catT[:, 4 * n:4 * n + 4, i * P:(i + 1) * P],
                                 t[:, :].rearrange("p (m t) -> p m t", m=4), ACT.Copy))
                T.free(act, ("hgrn_oT", i, n))
                act.sem_inc(self.s("oT_kept"), 1)
        self.scalar_branch(act)

    def vector(self, dve):
        net, T, s = self.net, self.net.T, self.net.dv
        sm = self.small
        s(dve.tensor_tensor(sm[:, 0:8], net.col("lb_raw", 0, 8), net.col("lb_raw", 0, 8), ALU.subtract))
        dve.sem_inc(self.s("lb_diff"), 1)
        dve.wait_ge(self.s("lb_exp"), 1)
        s(dve.reciprocal(sm[:, 16:24], sm[:, 8:16]))
        s(dve.tensor_tensor(sm[:, 16:24], sm[:, 16:24], sm[:, 8:16], ALU.mult))
        s(dve.tensor_tensor(sm[:, 24:32], sm[:, 16:24], sm[:, 16:24], ALU.subtract))
        s(dve.tensor_scalar(sm[:, 32:40], sm[:, 24:32], -1.0, 1.0, ALU.mult, ALU.add))
        for j in range(8):
            if j % 2 == 0:
                dve.wait_ge(self.s("sig_ready"), j // 2 + 1)
            s(dve.tensor_scalar(self.kT[:, j, :], self.kT[:, j, :], sm[:, 32 + j:33 + j], sm[:, 24 + j:25 + j],
                                ALU.mult, ALU.add))
        dve.sem_inc(self.s("f_ready"), 1)
        s(dve.memset(self.AT, 0.0))
        dve.wait_ge(self.s("log_ready"), 1)
        s(dve.tensor_scalar(self.kT, self.kT, -1.0, 1.0, ALU.mult, ALU.add))
        dve.sem_inc(self.s("k_ready"), 1)
        for h in range(HEADS):
            for i in range(NT):
                b = self.b[:, h, i * P:(i + 1) * P]
                s(dve.tensor_tensor_scan(b, net.ones[:, 0:P], b, 0.0, ALU.mult, ALU.add))
        dve.wait_ge(self.s("q_kept"), 4)
        dve.wait_ge(self.s("masks_loaded"), 16)

        def blocks_of(x, B):
            return x.rearrange("p h t -> p (h t)").rearrange("p (n s b) -> p n s b", s=2, b=B)

        def exponent(lv):
            M, B = self.M[(lv + 1) % 2], P if lv < 0 else LEVELS[lv]
            if lv >= 1:
                T.take(dve, ("hgrn_level", lv - 2, 3)) if lv >= 2 else T.take(dve, ("hgrn_cross", 1))
            m, b = blocks_of(M, B), blocks_of(self.b, B)
            n = 8 * SEQ // (2 * B)
            mid = b[:, :, 0, B - 1:B].to_broadcast([P, n, B])
            s(dve.tensor_tensor(m[:, :, 0, :], mid, b[:, :, 0, :], ALU.subtract))
            if lv < 0:
                s(dve.tensor_copy(m[:, :, 1, :], b[:, :, 1, :]))
            else:
                s(dve.tensor_tensor(m[:, :, 1, :], b[:, :, 1, :], mid, ALU.subtract))
            dve.sem_inc(self.s("e_ready"), 1)

        def keep_level(lv):
            mask = self.level_masks[:, lv if lv >= 0 else 7, :].bitcast(I32)
            for n in range(4):
                t = T.take(dve, ("hgrn_level", lv, n))
                s(dve.copy_predicated(self.AT[:, 4 * n:4 * n + 4, :], mask.unsqueeze(1).to_broadcast([P, 4, P]),
                                      t[:, :].rearrange("p (m t) -> p m t", m=4)))
                T.free(dve, ("hgrn_level", lv, n))

        exponent(-1)
        for lv in range(-1, len(LEVELS)):
            M, B = self.M[(lv + 1) % 2], P if lv < 0 else LEVELS[lv]
            if lv + 1 < len(LEVELS):
                exponent(lv + 1)
            dve.wait_ge(self.s("exp_ready"), lv + 2)
            m, k, q = blocks_of(M, B), blocks_of(self.kT, B), blocks_of(self.qT, B)
            s(dve.tensor_tensor(m[:, :, 0, :], m[:, :, 0, :], k[:, :, 0, :], ALU.mult))
            s(dve.tensor_tensor(m[:, :, 1, :], m[:, :, 1, :], q[:, :, 1, :], ALU.mult))
            dve.sem_inc(self.s("m_ready"), 1)
            if lv == -1:
                keep_level(-1)
            elif lv >= 1:
                keep_level(lv - 1)
        keep_level(len(LEVELS) - 1)
        dve.sem_inc(self.s("at_ready"), 1)
        self.rows_here(dve)
        for i in range(NT):
            for n in range(2):
                j = 2 * i + n
                dve.wait_ge(self.s("o_kept"), j + 1)
                o4 = self.o[:, i, n * 512:(n + 1) * 512].rearrange("p (h v) -> p h v", h=4)
                q4 = self.sq[:, i, n * 512:(n + 1) * 512].rearrange("p (h v) -> p h v", h=4)
                s(dve.tensor_tensor(q4, o4, o4, ALU.mult))
                s(dve.tensor_reduce(sm[:, 40 + 4 * j:44 + 4 * j], q4, AX, ALU.add))
                s(dve.tensor_scalar(sm[:, 40 + 4 * j:44 + 4 * j], sm[:, 40 + 4 * j:44 + 4 * j], 1.0 / P, RMS_EPS,
                                    ALU.mult, ALU.add))
                dve.sem_inc(self.s("mean"), 1)
        dve.wait_ge(self.s("g_kept"), 4)
        for i in range(NT):
            for n in range(2):
                j = 2 * i + n
                dve.wait_ge(self.s("rstd"), j + 1)
                o4 = self.o[:, i, n * 512:(n + 1) * 512].rearrange("p (h v) -> p h v", h=4)
                o1 = self.o[:, i, n * 512:(n + 1) * 512]
                s(dve.tensor_tensor(o4, o4, sm[:, 56 + 4 * j:60 + 4 * j].unsqueeze(2).to_broadcast([P, 4, P]), ALU.mult))
                s(dve.tensor_tensor(o1, o1, net.rows[:, 0, n * 512:(n + 1) * 512], ALU.mult))
                s(dve.tensor_tensor(o1, o1, self.g[:, i, n * 512:(n + 1) * 512], ALU.mult))
                dve.sem_inc(self.s("o_gated"), 1)
        self.vector_branch(dve, False)

    def gpsimd(self, pool):
        net, sm = self.net, self.small
        net.po(pool.memset(sm[:, 72:76], -0.5))
        for j in range(4):
            pool.wait_ge(self.s("mean"), j + 1)
            net.po(pool.tensor_tensor(sm[:, 56 + 4 * j:60 + 4 * j], sm[:, 40 + 4 * j:44 + 4 * j], sm[:, 72:76], ALU.pow))
            pool.sem_inc(self.s("rstd"), 1)


class Retention(Branch):
    tag = "ret"
    shared = {"branch": GATE_COUNTS}

    def __init__(self, net):
        self.net = net
        a = Arena(net.scratch)
        self.merged = self.take_merged()
        self.qT = a.take(8 * SEQ, 8, SEQ)
        self.kT = a.take(8 * SEQ, 8, SEQ)
        self.catT = Arena(net.scratch).take(16 * SEQ, 16, SEQ)
        self.vv = a.take(NT * 2048, NT, 2048)
        self.g = a.take(NT * 2048, NT, 2048)
        self.decay = a.take(4 * TRI, 4, TRI)
        self.AT = [a.take(TRI) for _ in range(2)]
        self.cos = a.take(SEQ)
        self.sin = a.take(SEQ)
        self.ta, self.tb = a.take(512), a.take(512)
        self.small = a.take(32)
        self.gate = [self.ta, self.tb]
        assert a.at <= SCRATCH - NT * D, a.at

    def tensor(self, pe):
        net, T = self.net, self.net.T
        for key in ("ret_q", "ret_k"):
            for b in range(2):
                net.product_T(pe, (key, b), net.xT)
        for b in range(4):
            net.product(pe, ("ret_v", b), net.xT)
        for b in range(4):
            net.product(pe, ("ret_g", b), net.xT)
        pe.wait_ge(self.s("rotated"), 8)
        for h in range(5):
            if h < 4:
                t = T.open(pe, ("ret_S", h))
                for i in range(NT):
                    for m in range(2):
                        out = t[:, 0:SEQ] if i == 0 else t[:, SEQ:TRI]
                        mm = pe.matmul(out, self.kT[:, 2 * h + m, i * P:(i + 1) * P], self.qT[:, 2 * h + m, i * P:SEQ],
                                       start=m == 0, stop=m == 1)
                T.close(("ret_S", h), mm)
            if h >= 1:
                g = h - 1
                pe.wait_ge(self.s("at_ready"), g + 1)
                pe.wait_ge(self.s("v_kept"), 8)
                A = self.AT[g % 2]
                for i in range(NT):
                    t = T.open(pe, ("ret_o", g, i))
                    vs = slice(512 * g, 512 * g + 512)
                    mm = pe.matmul(t[:, :], A[:, i * P:(i + 1) * P], self.vv[:, 0, vs], start=True, stop=i == 0)
                    if i:
                        mm = pe.matmul(t[:, :], A[:, SEQ:TRI], self.vv[:, 1, vs], start=False, stop=True)
                    T.close(("ret_o", g, i), mm)
        for i in range(NT):
            for n in range(4):
                pe.wait_ge(self.s("gated"), 8)
                t = T.open(pe, ("ret_oT", i, n))
                for m in range(4):
                    j = 4 * n + m
                    mm = pe.transpose(t[:, m * P:(m + 1) * P], self.g[:, i, j * P:(j + 1) * P], net.ident[:, :])
                T.close(("ret_oT", i, n), mm)
        pe.wait_ge(self.s("oT_kept"), 8)
        self.tensor_branch(pe, self.catT, kt=16)

    def scalar(self, act):
        net, T, s, io = self.net, self.net.T, self.net.ac, self.net.io
        act.dma_start(self.decay, io["decay"].rearrange("p (a b) -> p a b", a=4)).then_inc(self.s("tables_loaded"), 16)
        act.dma_start(self.cos, io["rotary"][0]).then_inc(self.s("tables_loaded"), 16)
        act.dma_start(self.sin, io["rotary"][1]).then_inc(self.s("tables_loaded"), 16)
        for b in range(4):
            for i in range(NT):
                t = T.take(act, (("ret_v", b), i))
                s(act.activation(self.vv[:, i, b * 512:(b + 1) * 512], t[:, :], ACT.Copy))
                T.free(act, (("ret_v", b), i))
                act.sem_inc(self.s("v_kept"), 1)
        for b in range(4):
            for i in range(NT):
                t = T.take(act, (("ret_g", b), i))
                s(act.activation(self.g[:, i, b * 512:(b + 1) * 512], t[:, :], ACT.Silu))
                T.free(act, (("ret_g", b), i))
        act.sem_inc(self.s("g_kept"), 1)
        for h in range(4):
            for i in range(NT):
                t = T.take(act, ("ret_o", h, i))
                j = 2 * h + i
                s(act.activation(self.ta, t[:, :], ACT.Square, accum_out=self.small[:, j:j + 1]))
                act.sem_inc(self.s("squares"), 1)
        for i in range(NT):
            for n in range(4):
                t = T.take(act, ("ret_oT", i, n))
                s(act.activation(self.catT[:, 4 * n:4 * n + 4, i * P:(i + 1) * P],
                                 t[:, :].rearrange("p (m t) -> p m t", m=4), ACT.Copy))
                T.free(act, ("ret_oT", i, n))
                act.sem_inc(self.s("oT_kept"), 1)
        self.scalar_branch(act)

    def vector(self, dve):
        net, T, s = self.net, self.net.T, self.net.dv
        dve.wait_ge(self.s("tables_loaded"), 48)
        cos = self.cos.unsqueeze(1).to_broadcast([P, 2, SEQ])
        sin = self.sin.unsqueeze(1).to_broadcast([P, 2, SEQ])
        for key, dst in (("ret_q", self.qT), ("ret_k", self.kT)):
            for h in range(4):
                key2 = ((key, h // 2), h % 2)
                t = T.take(dve, key2)
                pair = t[:, :].rearrange("p (m t) -> p m t", m=2)
                s(dve.tensor_tensor(self.ta.rearrange("p (m t) -> p m t", m=2), pair, cos, ALU.mult))
                s(dve.tensor_tensor(self.tb.rearrange("p (m t) -> p m t", m=2), pair, sin, ALU.mult))
                T.free(dve, key2)
                s(dve.tensor_tensor(dst[:, 2 * h, :], self.ta[:, 0:SEQ], self.tb[:, SEQ:], ALU.subtract))
                s(dve.tensor_tensor(dst[:, 2 * h + 1, :], self.ta[:, SEQ:], self.tb[:, 0:SEQ], ALU.add))
                dve.sem_inc(self.s("rotated"), 1)
        for h in range(5):
            if h < 4:
                t = T.take(dve, ("ret_S", h))
                if h >= 2:
                    T.take(dve, ("ret_o", h - 2, 1))
                s(dve.tensor_tensor(self.AT[h % 2], t[:, 0:TRI], self.decay[:, h, :], ALU.mult))
                T.free(dve, ("ret_S", h))
                dve.sem_inc(self.s("at_ready"), 1)
            if h >= 1:
                g = h - 1
                for i in range(NT):
                    j = 2 * g + i
                    dve.wait_ge(self.s("squares"), j + 1)
                    s(dve.tensor_scalar(self.small[:, 8 + j:9 + j], self.small[:, j:j + 1], 1.0 / 512, RMS_EPS,
                                        ALU.mult, ALU.add))
                    dve.sem_inc(self.s("mean"), 1)
                    if j == 0:
                        dve.wait_ge(self.s("g_kept"), 1)
                    dve.wait_ge(self.s("rstd"), j + 1)
                    t = T.take(dve, ("ret_o", g, i))
                    gs = self.g[:, i, 512 * g:512 * g + 512]
                    s(dve.scalar_tensor_tensor(gs, t[:, :], self.small[:, 16 + j:17 + j], gs, ALU.mult, ALU.mult))
                    T.free(dve, ("ret_o", g, i))
                    dve.sem_inc(self.s("gated"), 1)
        self.vector_branch(dve, False)

    def gpsimd(self, pool):
        net, sm = self.net, self.small
        net.po(pool.memset(sm[:, 24:25], -0.5))
        for j in range(8):
            pool.wait_ge(self.s("mean"), j + 1)
            net.po(pool.tensor_tensor(sm[:, 16 + j:17 + j], sm[:, 8 + j:9 + j], sm[:, 24:25], ALU.pow))
            pool.sem_inc(self.s("rstd"), 1)


class Merge(Phase):
    tag = "merge"

    def __init__(self, net):
        self.net = net
        a = Arena(net.scratch)
        self.merged = Branch.take_merged(self)
        self.mT = a.take(8 * SEQ, 8, SEQ)
        self.gt = a.take(D)
        self.tmp = a.take(512)

    def rows(self):
        return ("ada_gt1",)

    def tensor(self, pe):
        net, T = self.net, self.net.T
        for i in range(NT):
            for c in range(2):
                t = T.open(pe, ("merge_T", i, c))
                for k in range(4):
                    n0 = (4 * c + k) * P
                    mm = pe.transpose(t[:, k * P:(k + 1) * P], self.merged[:, i, n0:n0 + P], net.ident[:, :])
                T.close(("merge_T", i, c), mm)
        gate_rows(net, pe, "gt1")
        pe.wait_ge(self.s("mT_kept"), 4)
        for c in range(2):
            net.product(pe, ("merge_out", c), self.mT)

    def scalar(self, act):
        net, T = self.net, self.net.T
        for i in range(NT):
            for c in range(2):
                t = T.take(act, ("merge_T", i, c))
                net.ac(act.activation(self.mT[:, 4 * c:4 * c + 4, i * P:(i + 1) * P],
                                      t[:, :].rearrange("p (k t) -> p k t", k=4), ACT.Copy))
                T.free(act, ("merge_T", i, c))
                act.sem_inc(self.s("mT_kept"), 1)

    def vector(self, dve):
        net, T, s = self.net, self.net.T, self.net.dv
        self.rows_here(dve)
        keep_gate_rows(net, dve, "gt1", self.gt)
        for c in range(2):
            for i in range(NT):
                key = (("merge_out", c), i)
                t = T.take(dve, key)
                xs = net.x[:, i, c * 512:(c + 1) * 512]
                s(dve.tensor_tensor(self.tmp, t[:, :], self.gt[:, c * 512:(c + 1) * 512], ALU.mult))
                s(dve.tensor_tensor(xs, xs, self.tmp, ALU.add))
                T.free(dve, key)


def exp_columns(net, dve, out, x, n, r, bits):
    s = net.dv
    s(dve.tensor_scalar(n, x, 1.0 / math.log(2.0), ROUND, ALU.mult, ALU.add))
    s(dve.tensor_scalar(n, n, ROUND, 127.0, ALU.subtract, ALU.min))
    s(dve.tensor_scalar(n, n, -127.0, None, ALU.max))
    s(dve.scalar_tensor_tensor(r, n, -0.693359375, x, ALU.mult, ALU.add))
    s(dve.scalar_tensor_tensor(r, n, 2.12194440e-4, r, ALU.mult, ALU.add))
    s(dve.tensor_scalar(r, r, 0.5, -0.5, ALU.min, ALU.max))
    s(dve.tensor_scalar(bits.bitcast(I32), n, 8388608.0, 1065353216.0, ALU.mult, ALU.add))
    s(dve.tensor_scalar(n, r, 1.0 / 5040, None, ALU.mult))
    for c in (1.0 / 720, 1.0 / 120, 1.0 / 24, 1.0 / 6, 0.5, 1.0):
        s(dve.scalar_tensor_tensor(n, n, c, r, ALU.add, ALU.mult))
    s(dve.scalar_tensor_tensor(out, n, 1.0, bits, ALU.add, ALU.mult))


def sin_cos_columns(net, dve, sin, cos, x, p, y2, v):
    s = net.dv
    s(dve.tensor_scalar(x, x, 0.125, None, ALU.mult))
    s(dve.tensor_tensor(y2, x, x, ALU.mult))
    s(dve.tensor_scalar(p, y2, 1.0 / 362880, None, ALU.mult))
    for c in (-1.0 / 5040, 1.0 / 120, -1.0 / 6):
        s(dve.scalar_tensor_tensor(p, p, c, y2, ALU.add, ALU.mult))
    s(dve.scalar_tensor_tensor(sin, p, 1.0, x, ALU.add, ALU.mult))
    s(dve.tensor_scalar(v, y2, 1.0 / 3628800, None, ALU.mult))
    for c in (-1.0 / 40320, 1.0 / 720, -1.0 / 24, 0.5):
        s(dve.scalar_tensor_tensor(v, v, c, y2, ALU.add, ALU.mult))
    for _ in range(3):
        s(dve.tensor_scalar(cos, v, -1.0, 1.0, ALU.mult, ALU.add))
        s(dve.scalar_tensor_tensor(v, sin, 2.0, sin, ALU.mult, ALU.mult))
        s(dve.scalar_tensor_tensor(sin, sin, 2.0, cos, ALU.mult, ALU.mult))
    s(dve.tensor_scalar(cos, v, -1.0, 1.0, ALU.mult, ALU.add))


class Loop:

    def __init__(self, first, turns, release):
        self.first, self.turns, self.release = first, turns, release


class Mixture(Phase):

    def __init__(self, net, n):
        self.net, self.n, self.tag = net, n, f"moe{n}"
        self.G, self.E = ROUTES[n]
        self.experts = self.G * self.E
        self.F = MOE2_F if n == 2 else MOE1_F
        self.ft = self.F // P
        self.per_gate = KT * self.F // UNIT
        self.pairs = SLOTS // (6 * self.per_gate)
        self.turns = self.experts // (2 * self.pairs)
        self.wide = self.F == 512
        n_gu = 2 if self.wide else 1
        self.in_tile = {4: n_gu, 5: n_gu, 6: 4, 7: 3, "slots_copied": 2, "weigh_ready": 2 * NT, "silu_ready": 2}
        tiles = MAX_TILES * self.experts // 2
        self.shared = {"moe": {"group_max": NT, "second_max": NT, "route_exps": NT, "choice_ready": 1,
                               "slots_ready": 1, "gathered": KT, "slots_copied": 2 * tiles,
                               "weigh_ready": 2 * NT * tiles, "pair_read": self.experts, "silu_ready": 2 * tiles}}
        a = Arena(net.scratch)
        self.src = a.take(NT * D, NT, D) if n == 2 else net.x
        self.xg = a.take(KT * WIDE, KT, WIDE)
        self.xs = [a.take(KT * TILE, KT, TILE) for _ in range(2)]
        self.silu = [a.take(self.F) for _ in range(2)]
        self.hid = [a.take(self.F) for _ in range(2)]
        self.hidT = [a.take(self.ft * TILE, self.ft, TILE) for _ in range(2)]
        self.y = a.take(D)
        self.weigh = a.take(NT * P, NT, P)
        self.scatter = a.take(SEQ)
        self.pick = [a.take(PAIRS) for _ in range(NT)]
        self.pick_tmp = a.take(PAIRS)
        n_l = self.G + self.experts
        self.L = a.take(NT * n_l, NT, n_l)
        self.A = [a.take(NT * self.experts, NT, self.experts) for _ in range(3)]
        self.rank = a.take(NT * self.experts, NT, self.experts)
        self.wt = a.take(NT * self.experts, NT, self.experts)
        self.of_pair = a.take(2 * NT * 2).rearrange("p (w i e) -> p w i e", w=2, i=NT)
        self.pos = a.take(3 * self.experts, 3, self.experts)
        self.before = a.take(P)
        self.r = a.take(NT * 80, NT, 80)
        self.meta = a.take(self.experts + self.experts // 2, rows=1).bitcast(I32)
        if n == 2:
            self.tmp, self.gt = a.take(512), a.take(D)

    def rows(self):
        return ("iota", "ada_gt2") if self.n == 2 else ("iota",)

    def tensor(self, pe):
        net, T, base = self.net, self.net.T, self.base
        net.small_rows(pe, (self.tag, "route"), f"route{self.n}", net.xT)
        if self.n == 2:
            gate_rows(net, pe, "gt2")
        pe.wait_ge(self.s("before_loaded"), 16)
        pe.wait_ge(self.s("choice_ready"), base("choice_ready") + 1)
        E, A = self.experts, self.A[2]
        t = T.open(pe, (self.tag, "rank"))
        pe.matmul(t[:, 0:E], self.before, A[:, 0, :], start=True, stop=True)
        pe.matmul(t[:, E:2 * E], net.ones[:, 0:P], A[:, 0, :], start=True, stop=False)
        pe.matmul(t[:, E:2 * E], self.before, A[:, 1, :], start=False, stop=True)
        pe.matmul(t[:, 2 * E:3 * E], net.ones[:, 0:P], A[:, 0, :], start=True, stop=False)
        T.close((self.tag, "rank"), pe.matmul(t[:, 2 * E:3 * E], net.ones[:, 0:P], A[:, 1, :], start=False, stop=True))
        pe.wait_ge(self.s("slots_ready"), base("slots_ready") + 1)
        for k in range(KT):
            t = T.open(pe, (self.tag, "gather", k))
            for i in range(NT):
                mm = pe.matmul(t[:, :], self.src[:, i, k * P:(k + 1) * P], self.pick[i], start=i == 0, stop=i == 1)
            T.close((self.tag, "gather", k), mm)
        pe.wait_ge(self.s("gathered"), base("gathered") + KT)
        for n in range(4):
            t = T.open(pe, (self.tag, "out", n), (n,))
            pe.matmul(t[:, :], net.zeros[:, 0:P], net.zeros[:, :], start=True, stop=False, skip_group_check=True)
        self.bank_base = list(T.uses)
        assert min(self.bank_base[4:8]) > 0
        first = net.unit
        with pe.Fori(0, self.turns) as turn:
            for q in range(self.pairs):
                more = self.load_more(pe, turn, q)
                with pe.If(more > 0):
                    for j in range(MAX_TILES - 1):
                        self.tensor_tile(pe, first, turn, q, j)
                with pe.Else():
                    for b in (4, 5, 6, 7):
                        pe.sem_inc(T.ready[b], (MAX_TILES - 1) * self.in_tile[b])
                self.tensor_tile(pe, first, turn, q, MAX_TILES - 1)
        for b in (4, 5, 6, 7):
            T.uses[b] += self.turns * self.pairs * MAX_TILES * self.in_tile[b]
        for n in range(4):
            t = T.bank[n]
            T.close((self.tag, "out", n), pe.matmul(t[:, :], net.zeros[:, 0:P], net.zeros[:, :], start=False, stop=True,
                                                    skip_group_check=True))
        T.turn = 0
        pg, release = self.per_gate, []
        for q in range(self.pairs):
            for e in range(2):
                gate, up = ((4, e), (5, e)) if self.wide else ((4 + e, 0), (4 + e, 0))
                for b, n in [gate] * pg + [up] * pg + [((7, 1), (6, 3))[e]] * pg:
                    per = self.pairs * MAX_TILES * self.in_tile[b]
                    release.append((T.ready[b], self.use(b, 0, q, MAX_TILES - 1, n) + 1, per))
        net.loops.append(Loop(first, self.turns, release))
        net.unit += SLOTS * self.turns
        for j, (sem, v, per) in enumerate(release):
            net.released[first + SLOTS * (self.turns - 1) + j] = (sem, v + per * (self.turns - 1))

    def use(self, what, turn, q, j, n):
        per = self.in_tile[what]
        at = self.base(what) if isinstance(what, str) else self.bank_base[what]
        return turn * (self.pairs * MAX_TILES * per) + (at + (q * MAX_TILES + j) * per + n)

    def load_more(self, eng, turn, q):
        return eng.value_load(self.meta[0:1, bass.ds(turn * self.pairs + (q + self.experts), 1)], min_val=0, max_val=1)

    def tensor_tile(self, pe, first, turn, q, j):
        net, T, pg = self.net, self.net.T, self.per_gate
        kper = KT // pg
        u0 = first + q * 6 * pg

        def weights(e, part, n, k):
            u = u0 + (3 * e + part) * pg + n
            pe.wait_ge(net.sem(f"slot{u % SLOTS}_loaded"), (turn + (u // SLOTS + 1)) * 16)
            return net.slot(u).rearrange("p (k n) -> p k n", k=k)

        def open_bank(b, n):
            pe.wait_ge(T.freed[b], self.use(b, turn, q, j, n))
            return T.bank[b]

        def gate_or_up(e, part, out):
            for m in range(pg):
                w = weights(e, part, m, kper)
                for k in range(kper):
                    kk = m * kper + k
                    mm = pe.matmul(out, self.xs[e][:, kk, :], w[:, k, :], start=kk == 0, stop=kk == KT - 1)
            return mm

        def transposes(e, n):
            b = 5 if self.wide else 4 + e
            pe.wait_ge(T.freed[b], self.use(b, turn, q, j, (e if self.wide else 0)) + 1)
            t = open_bank(6, n)
            for f in range(self.ft):
                mm = pe.matmul(t[:, f * TILE:(f + 1) * TILE], self.hid[e][0:TILE, f * P:(f + 1) * P],
                               net.ident[0:TILE, 0:TILE], start=True, stop=True)
            mm.then_inc(T.ready[6], 1)

        def down(e, c, b, n):
            t = open_bank(b, n)
            for f in range(self.ft):
                w = weights(e, 2, f // 2, 2)
                mm = pe.matmul(t[e * TILE:(e + 1) * TILE, :], self.hidT[e][:, f, :], w[:, f % 2, c * 512:(c + 1) * 512],
                               start=f == 0, stop=f == self.ft - 1)
            mm.then_inc(T.ready[b], 1)

        for e in range(2):
            pe.wait_ge(self.s("slots_copied"), self.use("slots_copied", turn, q, j, e) + 1)
            if self.wide:
                gate_or_up(e, 0, open_bank(4, e)[0:TILE, :]).then_inc(T.ready[4], 1)
                if e == 1:
                    transposes(0, 0)
                gate_or_up(e, 1, open_bank(5, e)[0:TILE, :]).then_inc(T.ready[5], 1)
            else:
                t = open_bank(4 + e, 0)
                gate_or_up(e, 0, t[0:TILE, 0:256])
                gate_or_up(e, 1, t[0:TILE, 256:512]).then_inc(T.ready[4 + e], 1)
        if not self.wide:
            transposes(0, 0)
        pe.wait_ge(self.s("weigh_ready"), self.use("weigh_ready", turn, q, j, 2 * NT))
        t = open_bank(7, 0)
        for i in range(NT):
            mm = pe.transpose(t[:, i * P:(i + 1) * P], self.weigh[:, i, :], net.ident[:, :])
        mm.then_inc(T.ready[7], 1)
        down(0, 1, 6, 1)
        down(0, 0, 7, 1)
        transposes(1, 2)
        pe.wait_ge(T.freed[6], self.use(6, turn, q, j, 3))
        down(1, 0, 7, 2)
        down(1, 1, 6, 3)
        for c in range(2):
            pe.wait_ge(T.freed[7 - c], self.use(7 - c, turn, q, j, self.in_tile[7 - c]))
            for i in range(NT):
                pe.matmul(T.bank[2 * i + c][:, :], self.scatter[:, i * P:(i + 1) * P],
                          self.y[:, c * 512:(c + 1) * 512], start=False, stop=False, skip_group_check=True)

    def first_of(self, out, vals, idx, tmp):
        dve, s = self.net.dv.eng, self.net.dv
        s(dve.tensor_scalar(out, vals, tmp[:, 0:1], None, ALU.is_equal))
        s(dve.tensor_tensor(out, out, idx, ALU.mult))
        s(dve.tensor_reduce(tmp[:, 1:2], out, AX, ALU.min))
        s(dve.tensor_scalar(out, out, tmp[:, 1:2], None, ALU.is_equal))

    def vector(self, dve):
        net, T, s, base = self.net, self.net.T, self.net.dv, self.base
        G, E, EX, n = self.G, self.E, self.experts, self.G + self.experts
        s(dve.memset(self.xg[:, :, PAIRS:WIDE], 0.0))
        t = T.take(dve, (self.tag, "route"))
        self.rows_here(dve)
        at = ROUTE_BIAS[self.n]
        for i in range(NT):
            L, r = self.L[:, i, :], self.r[:, i, :]
            s(dve.tensor_tensor(L, t[:, i * n:(i + 1) * n], net.bias_row[:, at:at + n], ALU.add))
            s(dve.tensor_reduce(r[:, 0:1], L[:, 0:G], AX, ALU.max))
            s(dve.tensor_scalar(r[:, 2:3], r[:, 0:1], -1.0, None, ALU.mult))
            dve.sem_inc(self.s("group_max"), 1)
            oh_g = r[:, 16:16 + G]
            self.first_of(oh_g, L[:, 0:G], net.bias_row[:, 76:76 + G], r[:, 0:2])
            grouped = lambda v: v.rearrange("p (g e) -> p g e", g=G)
            oh_b = oh_g.unsqueeze(2).to_broadcast([P, G, E])
            prod = grouped(self.A[2][:, i, :])
            s(dve.tensor_tensor(prod, grouped(L[:, G:]), oh_b, ALU.mult))
            es = r[:, 24:24 + E]
            s(dve.tensor_reduce(es, prod.rearrange("p g e -> p e g"), AX, ALU.add))
            s(dve.tensor_reduce(r[:, 4:5], es, AX, ALU.max))
            s(dve.tensor_scalar(r[:, 6:7], r[:, 4:5], -1.0, None, ALU.mult))
            self.first_of(r[:, 32:32 + E], es, net.bias_row[:, 76:76 + E], r[:, 4:6])
            s(dve.scalar_tensor_tensor(es, r[:, 32:32 + E], MASKED, es, ALU.mult, ALU.add))
            s(dve.tensor_reduce(r[:, 8:9], es, AX, ALU.max))
            dve.sem_inc(self.s("second_max"), 1)
            self.first_of(r[:, 40:40 + E], es, net.bias_row[:, 76:76 + E], r[:, 8:10])
            for c in range(2):
                s(dve.tensor_tensor(grouped(self.A[c][:, i, :]), oh_b,
                                    r[:, 32 + 8 * c:32 + 8 * c + E].unsqueeze(1).to_broadcast([P, G, E]), ALU.mult))
            s(dve.tensor_tensor(self.A[2][:, i, :], self.A[0][:, i, :], self.A[1][:, i, :], ALU.add))
        T.free(dve, (self.tag, "route"))
        dve.sem_inc(self.s("choice_ready"), 1)
        for i in range(NT):
            r = self.r[:, i, :]
            dve.wait_ge(self.s("route_exps"), base("route_exps") + i + 1)
            s(dve.tensor_scalar(r[:, 13:14], r[:, 10:11], 1.0, r[:, 11:12], ALU.add, ALU.mult))
            s(dve.reciprocal(r[:, 12:13], r[:, 13:14]))
            s(dve.tensor_tensor(r[:, 13:14], r[:, 12:13], r[:, 10:11], ALU.mult))
        if self.n == 2:
            keep_gate_rows(net, dve, "gt2", self.gt, 1)
        t = T.take(dve, (self.tag, "rank"))
        pos, iota = self.pos, net.rows[:, 0, 0:PAIRS]
        s(dve.tensor_copy(pos[:, 0, :], t[:, 2 * EX:3 * EX]))
        s(dve.tensor_copy(self.rank, t[:, 0:2 * EX].rearrange("p (i e) -> p i e", i=NT)))
        T.free(dve, (self.tag, "rank"))
        s(dve.tensor_tensor_scan(pos[:, 1, :], net.ones[:, 0:EX], pos[:, 0, :], 0.0, ALU.mult, ALU.add))
        s(dve.tensor_tensor(pos[:, 1, :], pos[:, 1, :], pos[:, 0, :], ALU.subtract))
        s(dve.tensor_copy(self.meta[0:1, 0:EX], pos[0:1, 1, :]))
        s(dve.tensor_reduce(pos[0:1, 2, 0:EX // 2], pos[0:1, 0, :].rearrange("p (q e) -> p q e", e=2), AX, ALU.max))
        s(dve.tensor_scalar(self.meta[0:1, EX:EX + EX // 2], pos[0:1, 2, 0:EX // 2], float(TILE), None, ALU.is_gt))
        for i in range(NT):
            r = self.r[:, i, :]
            s(dve.tensor_scalar(self.wt[:, i, :], self.A[1][:, i, :], r[:, 13:14], None, ALU.mult))
            s(dve.scalar_tensor_tensor(self.wt[:, i, :], self.A[0][:, i, :], r[:, 12:13], self.wt[:, i, :], ALU.mult,
                                       ALU.add))
            s(dve.tensor_tensor(pos[:, 2, :], self.rank[:, i, :], pos[:, 1, :], ALU.add))
            for c in range(2):
                s(dve.tensor_tensor_reduce(self.A[c][:, i, :], self.A[c][:, i, :], pos[:, 2, :], 1.0, 0.0, ALU.mult,
                                           ALU.add, r[:, 14 + c:15 + c]))
            s(dve.tensor_scalar(self.pick[i], iota, r[:, 14:15], None, ALU.is_equal))
            s(dve.tensor_scalar(self.pick_tmp, iota, r[:, 15:16], None, ALU.is_equal))
            s(dve.tensor_tensor(self.pick[i], self.pick[i], self.pick_tmp, ALU.add))
        dve.sem_inc(self.s("slots_ready"), 1)
        with dve.Fori(0, self.turns) as turn:
            for q in range(self.pairs):
                more = self.load_more(dve, turn, q)
                with dve.If(more > 0):
                    for j in range(MAX_TILES - 1):
                        self.vector_tile(dve, turn, q, j)
                with dve.Else():
                    for b in (5,) if self.wide else (4, 5):
                        dve.wait_ge(T.freed[b], self.use(b, turn, q, 0, 0))
                        dve.sem_inc(T.freed[b], (MAX_TILES - 1) * self.in_tile[b])
                self.vector_tile(dve, turn, q, MAX_TILES - 1)
        for i in range(NT):
            for c in range(2):
                t = T.take(dve, (self.tag, "out", 2 * i + c))
                xs = net.x[:, i, c * 512:(c + 1) * 512]
                if self.n == 2:
                    s(dve.tensor_tensor(self.tmp, t[:, :], self.gt[:, c * 512:(c + 1) * 512], ALU.mult))
                    s(dve.tensor_tensor(xs, xs, self.tmp, ALU.add))
                else:
                    s(dve.scalar_tensor_tensor(xs, xs, ALPHA, t[:, :], ALU.mult, ALU.add))
                T.free(dve, (self.tag, "out", 2 * i + c))

    def vector_tile(self, dve, turn, q, j):
        T = self.net.T
        for e in range(2):
            b, n, at = (5, e, 0) if self.wide else (4 + e, 0, 256)
            dve.wait_ge(T.ready[b], self.use(b, turn, q, j, n) + 1)
            dve.wait_ge(self.s("silu_ready"), self.use("silu_ready", turn, q, j, e) + 1)
            dve.tensor_tensor(self.hid[e][0:TILE, :], self.silu[e][0:TILE, :], T.bank[b][0:TILE, at:at + self.F],
                              ALU.mult).then_inc(T.freed[b], 1)

    def gpsimd(self, pool):
        net, T = self.net, self.net.T
        pool.wait_ge(self.s("gathered"), self.base("gathered") + KT)
        with pool.Fori(0, self.turns) as turn:
            for q in range(self.pairs):
                at = [pool.value_load(self.meta[0:1, bass.ds(turn * (2 * self.pairs) + (2 * q + e), 1)], min_val=0,
                                      max_val=PAIRS) for e in range(2)]
                more = self.load_more(pool, turn, q)
                pair = bass.ds(turn * (2 * self.pairs) + 2 * q, 2)
                pool.wait_ge(self.s("weigh_ready"), self.use("weigh_ready", turn, q, 0, 0))
                for k, values in enumerate((self.rank, self.wt)):
                    pool.tensor_copy(self.of_pair[:, k], values[:, :, pair]).then_inc(self.s("pair_read"), 1)
                with pool.If(more > 0):
                    for j in range(MAX_TILES - 1):
                        self.gpsimd_tile(pool, turn, q, j, at)
                with pool.Else():
                    for what in ("slots_copied", "weigh_ready"):
                        pool.wait_ge(self.s(what), self.use(what, turn, q, 0, 0))
                        pool.sem_inc(self.s(what), (MAX_TILES - 1) * self.in_tile[what])
                self.gpsimd_tile(pool, turn, q, MAX_TILES - 1, at)

    def gpsimd_tile(self, pool, turn, q, j, at):
        T = self.net.T
        tile = (j + 1) % MAX_TILES
        for e in range(2):
            b, n = (5, e - 1) if self.wide else (4 + e, 0)
            pool.wait_ge(T.ready[b], self.use(b, turn, q, j, n))
            if e == 1:
                pool.wait_ge(T.ready[7], self.use(7, turn, q, j, -1))
                pool.wait_ge(self.s("pair_read"), turn * (2 * self.pairs) + (self.base("pair_read") + 2 * (q + 1)))
            pool.tensor_copy(self.xs[e], self.xg[:, :, bass.ds(at[e] + tile * TILE, TILE)])\
                .then_inc(self.s("slots_copied"), 1)
        for i in range(NT):
            for e in range(2):
                pool.tensor_scalar(self.weigh[:, i, e * TILE:(e + 1) * TILE],
                                   self.net.rows[:, 0, tile * TILE:(tile + 1) * TILE],
                                   self.of_pair[:, 0, i, e:e + 1], self.of_pair[:, 1, i, e:e + 1], ALU.is_equal,
                                   ALU.mult).then_inc(self.s("weigh_ready"), 1)

    def scalar(self, act):
        net, T, s, base = self.net, self.net.T, self.net.ac, self.base
        act.dma_start(self.before, net.io["before"]).then_inc(self.s("before_loaded"), 16)
        for i in range(NT):
            L, r = self.L[:, i, :], self.r[:, i, :]
            act.wait_ge(self.s("group_max"), base("group_max") + i + 1)
            s(act.activation(r[:, 56:56 + self.G], L[:, 0:self.G], ACT.Exp, bias=r[:, 2:3], accum_out=r[:, 11:12]))
            act.wait_ge(self.s("second_max"), base("second_max") + i + 1)
            s(act.activation(r[:, 10:11], r[:, 8:9], ACT.Exp, bias=r[:, 6:7]))
            act.sem_inc(self.s("route_exps"), 1)
        for k in range(KT):
            t = T.take(act, (self.tag, "gather", k))
            kw = {"scale": net.mod[:, 24 + k:25 + k], "bias": net.mod[:, 16 + k:17 + k]} if self.n == 2 else {}
            s(act.activation(self.xg[:, k, 0:PAIRS], t[:, :], ACT.Identity, **kw))
            T.free(act, (self.tag, "gather", k))
            act.sem_inc(self.s("gathered"), 1)
        with act.Fori(0, self.turns) as turn:
            for q in range(self.pairs):
                more = self.load_more(act, turn, q)
                with act.If(more > 0):
                    for j in range(MAX_TILES - 1):
                        self.scalar_tile(act, turn, q, j)
                with act.Else():
                    for b in (4, 6, 7) if self.wide else (6, 7):
                        act.wait_ge(T.freed[b], self.use(b, turn, q, 0, 0))
                        act.sem_inc(T.freed[b], (MAX_TILES - 1) * self.in_tile[b])
                    act.wait_ge(self.s("silu_ready"), self.use("silu_ready", turn, q, 0, 0))
                    act.sem_inc(self.s("silu_ready"), (MAX_TILES - 1) * self.in_tile["silu_ready"])
                self.scalar_tile(act, turn, q, MAX_TILES - 1)

    def scalar_tile(self, act, turn, q, j):
        T = self.net.T

        def silu(e):
            b, n = (4, e) if self.wide else (4 + e, 0)
            act.wait_ge(T.ready[b], self.use(b, turn, q, j, n) + 1)
            act.activation(self.silu[e][0:TILE, :], T.bank[b][0:TILE, 0:self.F], ACT.Silu)\
                .then_inc(self.s("silu_ready"), 1)
            if self.wide:
                act.wait_ge(self.s("silu_ready"), self.use("silu_ready", turn, q, j, e) + 1)
                act.sem_inc(T.freed[4], 1)

        def keep(b, n, out, src):
            act.wait_ge(T.ready[b], self.use(b, turn, q, j, n) + 1)
            act.activation(out, src, ACT.Copy).then_inc(T.freed[b], 1)

        def keep_hidT(e, n):
            keep(6, n, self.hidT[e], T.bank[6][:, 0:self.ft * TILE].rearrange("p (f t) -> p f t", f=self.ft))

        def keep_y(e, c, b, n):
            lo, hi = e * TILE, (e + 1) * TILE
            keep(b, n, self.y[lo:hi, c * 512:(c + 1) * 512], T.bank[b][lo:hi, :])

        silu(0)
        silu(1)
        keep_hidT(0, 0)
        keep(7, 0, self.scatter, T.bank[7][:, 0:SEQ])
        keep_y(0, 1, 6, 1)
        keep_y(0, 0, 7, 1)
        keep_hidT(1, 2)
        keep_y(1, 0, 7, 2)
        keep_y(1, 1, 6, 3)


def log_sigmoid_front(net, dve, x, out):
    net.dv(dve.scalar_tensor_tensor(out, x, -1.0, x, ALU.mult, ALU.min))


PHASES = [(Start, ()), (Fox, ()), (LayerNorm, (0,)), (Mixture, (0,)), (LayerNorm, (1,)), (Mlstm, ()),
          (LayerNorm, (2,)), (Mixture, (1,)), (LayerNorm, (3,)), (RmsNorm, (0,)), (Indexed, ()),
          (Hgrn, ()), (Retention, ()), (Merge, ()), (RmsNorm, (1,)), (Mixture, (2,)), (RmsNorm, (2,))]


def stream_weights(net, sp, stream, total):
    u = 0
    loops = list(net.loops)

    def load(v):
        if v >= SLOTS:
            sp.wait_ge(*net.released[v - SLOTS])
        sp.dma_start(net.slot(v), stream[v]).then_inc(net.sem(f"slot{v % SLOTS}_loaded"), 16)

    while u < total:
        if loops and u == loops[0].first + SLOTS:
            loop = loops.pop(0)
            with sp.Fori(1, loop.turns) as turn:
                for j in range(SLOTS):
                    sem, base, per = loop.release[j]
                    sp.wait_ge(sem, base + (turn - 1) * per)
                    at = net.slot(loop.first + j)
                    sp.dma_start(at, stream[bass.ds(turn * SLOTS + (loop.first + j), 1)].rearrange("o p n -> p (o n)"))\
                      .then_inc(net.sem(f"slot{(loop.first + j) % SLOTS}_loaded"), 16)
            u = loop.first + SLOTS * loop.turns
        else:
            load(u)
            u += 1


def program(nc, io, phase_list, total_units):
    with ExitStack() as ctx:
        net = Net(nc, ctx, io, phase_list)
        phases = net.phase_objects = [cls(net, *args) for cls, args in phase_list]
        net.rows_at, n = {}, 0
        for ph in phases:
            n += 16 * len(ph.rows())
            net.rows_at[ph.tag] = n
        net.dv = net.ac = net.po = None
        block = ctx.enter_context(nc.Block())

        @block.tensor
        def _(pe):
            for ph in phases:
                ph.tensor(pe)
                if ph.joins:
                    net.join(pe, "tensor")

        @block.vector
        def _(dve):
            net.dv = Steps(dve, net.sem("vector_steps"))
            for ph in phases:
                ph.vector(dve)
                if ph.joins:
                    net.join(dve, "vector")

        @block.scalar
        def _(act):
            net.ac = Steps(act, net.sem("scalar_steps"))
            for ph in phases:
                for r, name in enumerate(ph.rows()):
                    act.dma_start(net.rows[:, r, :], io["rows"][ROWS.index(name)].partition_broadcast(P))\
                       .then_inc(net.sem("row_loaded"), 16)
                ph.scalar(act)
                if ph.joins:
                    net.join(act, "scalar")
            act.dma_start(io["out"].rearrange("(i p) d -> p i d", p=P), net.x).then_inc(net.sem("out_stored"), 16)
            act.wait_ge(net.sem("out_stored"), 16)

        @block.gpsimd
        def _(pool):
            net.po = Steps(pool, net.sem("gpsimd_steps"))
            for ph in phases:
                ph.gpsimd(pool)
                if ph.joins:
                    net.join(pool, "gpsimd")

        @block.sync
        def _(sp):
            stream_weights(net, sp, io["stream"], total_units)


def tiles(w, rows, n0, n1):
    part = w[rows[0]:rows[1], n0:n1]
    return part.reshape(-1, P, n1 - n0).transpose(1, 0, 2).reshape(P, -1)


def blocks(w, n0, n1):
    return [tiles(w, (r, r + 512), c, c + 512) for c in range(n0, n1, 512) for r in range(0, w.shape[0], 512)]


def column(v, n):
    return v.reshape(n, P).T


def place(v):
    out = np.zeros((P, 1), v.dtype)
    out[:v.shape[0], 0] = v
    return out


def constants():
    q, k = np.arange(P)[:, None], np.arange(P)[None, :]
    diag = np.where(k <= q, 0.0, MASKED).astype(np.float32)
    out = {"ident": np.eye(P, dtype=np.float32),
           "causal": np.concatenate([diag, np.zeros((P, P), np.float32), diag], 1)}
    sel = np.zeros((8, 8, P), np.float32)
    for h in range(8):
        sel[h, h] = 1.0
    out["sel"] = sel.reshape(8, 8 * P)
    out["before"] = np.triu(np.ones((P, P), np.float32), 1)
    out["flip"] = np.ascontiguousarray(np.eye(P, dtype=np.float32)[::-1])
    rel = np.maximum(SEQ - 1 - np.arange(TRI), 0)
    relf = np.maximum(rel, 1).astype(np.float32)
    large = 16 + (np.log(relf / np.float32(16)) / np.float32(math.log(8)) * np.float32(16)).astype(np.int32)
    bucket = np.where(rel < 16, rel, np.minimum(large, 31))
    out["buckets"] = (np.arange(32)[:, None] == bucket[None, :]).astype(np.float32)
    s, t = np.arange(P)[:, None], np.arange(P)[None, :]
    masks = [(s // (2 * b) == t // (2 * b)) & (s // b % 2 == 0) & (t // b % 2 == 1) for b in LEVELS] + [s == t]
    out["level_masks"] = np.concatenate([m.astype(np.int32) for m in masks], 1)
    decay = []
    for h in range(4):
        g = math.log(1.0 - 2.0 ** (-5.0 - h))
        d0 = np.where(t >= s, np.exp((t - s) * g), 0.0) / 16
        d1 = np.exp((t - s + P) * g) / 16
        decay += [d0, d1, d0]
    out["decay"] = np.concatenate(decay, 1).astype(np.float32)
    theta = (1.0 / (np.float32(10000.0) ** np.linspace(0.0, 1.0, P, dtype=np.float32))).astype(np.float32)
    angle = (theta[:, None] * np.arange(SEQ, dtype=np.float32)[None, :]).astype(np.float32)
    out["rotary"] = np.stack([np.cos(angle.astype(np.float64)), np.sin(angle.astype(np.float64))]).astype(np.float32)
    return out


def streams(i):
    s = []
    w = i["even_w_in"][0]
    u = w[:, 1544:2056]
    s += blocks(u, 0, 512) + blocks(w, 0, 1536) + blocks(i["s5_w_glu"][0], 0, 512) + blocks(i["even_w_out"][0], 0, 1024)
    s += experts(i["moe_w_gate"][0], i["moe_w_up"][0], i["moe_w_down"][0])
    w = i["odd_w_in"][0]
    ada = i["ada_w_2"][0]
    own, mod = blocks(w, 0, 4096), blocks(ada, 0, 2048) + blocks(ada, 3072, 5120)
    for b in range(0, 16, 2):
        s += own[b:b + 2] + mod[b:b + 2]
    s += blocks(i["odd_w_out"][0], 0, 1024)
    s += experts(i["moe_w_gate"][1], i["moe_w_up"][1], i["moe_w_down"][1])
    return s + streams2(i)


def streams2(i):
    ada, w = i["ada_w_2"][0], i["w_in_2"][0]
    at, parts = 0, {}
    for name, n in (("aq", 1024), ("ak", 1024), ("av", 1024), ("iq", 512), ("ik", 64), ("iw", 8), ("bq", 1024),
                    ("bf", 1024), ("bi", 1024), ("bg", 1024), ("cq", 1024), ("ck", 1024), ("cv", 2048), ("cg", 2048),
                    ("ga", 1024), ("gb", 1024), ("gc", 1024)):
        parts[name] = w[:, at:at + n]
        at += n
    whole = lambda m: blocks(m, 0, m.shape[1])
    ik = np.concatenate([parts["ik"], parts["ik"]], 1)
    s = [np.concatenate([tiles(ik, (0, D), 0, P), np.zeros((P, UNIT - D), np.float32)], 1)]
    s += whole(parts["iq"]) + whole(parts["aq"]) + whole(parts["ak"]) + whole(parts["av"])
    s += branch(parts["ga"], i["w_branch_a_2"][0])
    s += whole(parts["bf"]) + whole(parts["bq"]) + whole(parts["bi"]) + whole(parts["bg"])
    s += branch(parts["gb"], i["w_branch_b_2"][0])
    for n in ("cq", "ck"):
        m = parts[n].reshape(D, 4, P, 2).transpose(0, 1, 3, 2).reshape(D, D)
        s += whole(m)
    s += whole(parts["cv"]) + whole(parts["cg"]) + branch(parts["gc"], i["w_branch_c_2"][0])
    s += blocks(ada, 2048, 3072) + whole(i["w_out_2"][0])
    s += blocks(ada, 5120, 6144) + experts(i["expert_w_gate_2"][0], i["expert_w_up_2"][0], i["expert_w_down_2"][0])
    return s


def branch(gate, out):
    return [u for c in (0, 512) for w in (gate, out) for u in blocks(w, c, c + 512)]


def experts(gate, up, down):
    s = []
    for e in range(gate.shape[0]):
        rows = UNIT // gate.shape[2] * P
        for w in (gate[e], up[e]):
            s += [tiles(w, (r, r + rows), 0, w.shape[1]) for r in range(0, D, rows)]
        s += [tiles(down[e], (r, r + 256), 0, D) for r in range(0, down.shape[1], 256)]
    return s


def layout(i):
    c = constants()
    ew, ow = i["even_w_in"][0], i["odd_w_in"][0]
    w2 = i["w_in_2"][0]
    small = {"fox_f": ew[:, 1536:1544], "mlstm_i": ow[:, 4096:4104], "mlstm_f": ow[:, 4104:4112],
             "idx_w": w2[:, 3648:3656],
             "route2": np.concatenate([i["router_group_w_2"][0], i["router_expert_w_2"][0]], 1)}
    for n in range(2):
        e = i["moe_w_expert"][n].transpose(1, 0, 2).reshape(D, 16)
        small[f"route{n}"] = np.concatenate([i["moe_w_group"][n], e], 1)
    cols = {"b_glu": column(i["s5_b_glu"][0], 4), "s5_d": column(i["s5_d"][0].reshape(-1), 4),
            "a_re": column(i["s5_a_re"][0].reshape(-1), 16), "a_im": column(i["s5_a_im"][0].reshape(-1), 16),
            "log_dt": column(np.repeat(i["s5_log_dt"][0], 64), 16),
            "fox_f_bias": place(i["fox_f_bias"][0]), "mlstm_i_bias": place(i["mlstm_i_bias"][0]),
            "mlstm_f_bias": place(i["mlstm_f_bias"][0]), "conv_b": column(i["mlstm_conv_b"][0], 16),
            "conv_w": np.concatenate([column(i["mlstm_conv_w"][0][t], 16) for t in range(4)], 1),
            "ada_b": column(np.concatenate([i["ada_b_2"][0][0:2048], i["ada_b_2"][0][3072:5120]]), 32),
            "norm1_g": column(i["norm1_g_2"][0], 8), "norm2_g": column(i["norm2_g_2"][0], 8),
            "c": column(i["c_2"][0], 8), "lb_raw": column(i["hgrn_lb_raw_2"][0], 8)}
    b = [np.zeros((P, 4, P), np.float32) for _ in range(2)]
    cc = [np.zeros((P, 16, 32), np.float32) for _ in range(2)]
    for part, (bn, cn) in enumerate((("s5_b_re", "s5_c_re"), ("s5_b_im", "s5_c_im"))):
        for g in range(32):
            j, odd = g // 2, g % 2
            r = 32 * (j % 4) + 16 * odd
            b[part][r:r + 16, j // 4, 64 * odd:64 * odd + 64] = i[bn][0, g].T
            cc[part][64 * odd:64 * odd + 64, j, 16 * odd:16 * odd + 16] = i[cn][0, g].T
    rows = [v for n in range(4) for v in (i["ln_g"][n // 2, n % 2], i["ln_b"][n // 2, n % 2])]
    rows += [i["final_norm_g_2"], i["ada_b_2"][0][2048:3072], i["ada_b_2"][0][5120:6144],
             np.concatenate([i["hgrn_norm_g_2"][0]] * 8), np.arange(D, dtype=np.float32)]
    bias = np.concatenate([i["moe_b_group"][0], i["moe_b_expert"][0].reshape(-1), i["moe_b_group"][1],
                           i["moe_b_expert"][1].reshape(-1), i["router_group_b_2"][0], i["router_expert_b_2"][0],
                           np.arange(-100, -92, dtype=np.float32)])
    x = i["x"][0]
    c.update(x=x, xT=x.T, small=np.concatenate([small[n] for n in SMALL], 1),
             cols=np.concatenate([cols[n] for n in COLS], 1),
             bias_row=bias, s5_b=np.stack(b).reshape(2, P, 512), s5_c=np.stack(cc).reshape(2, P, 512),
             rows=np.stack(rows), rel_bias=i["rel_bias_2"], stream=np.stack(streams(i)))
    return {n: np.ascontiguousarray(a) for n, a in c.items()}


def kernel(**inputs):
    import concourse.bacc as bacc
    from concourse.bass_utils import run_bass_kernel_spmd

    nc = bacc.Bacc("TRN2", target_bir_lowering=False, num_devices=1)
    arrays = layout({n: np.asarray(a) for n, a in inputs.items()})
    io = {n: nc.dram_tensor(n, a.shape, mybir.dt.from_np(a.dtype), kind="ExternalInput").ap() for n, a in arrays.items()}
    io["bias_by_distance"] = nc.dram_tensor("bias_by_distance", (8, TRI), F32, kind="Internal").ap()
    io["out"] = nc.dram_tensor("out", (SEQ, D), F32, kind="ExternalOutput").ap()
    program(nc, io, PHASES, arrays["stream"].shape[0])
    got = run_bass_kernel_spmd(nc, [arrays], core_ids=[0])
    return got.results[0]["out"].reshape(1, SEQ, D)
```
